# Optimizing a Trainium2 kernel written in Bass

```python
import math
import jax, jax.numpy as jnp
from jax import lax
import numpy as np

D_MODEL = 1024
BATCH = 1
SEQ = 256
DEPTH = 2

N_MIXERS = 2
SSM_GROUP = 16
SSM_GROUPS = D_MODEL // SSM_GROUP
SSM_STATE = 64
ATTN_HEADS = 8
ATTN_HD = D_MODEL // ATTN_HEADS // 2
Q_BLOCK = 128
REL_BUCKETS = 32
REL_MAX_EXACT = REL_BUCKETS // 2
REL_MAX_DIST = 128
D_FF = 2816
N_EXPERTS = 8
TOP_K = 2
RMS_EPS = 1e-6
N_SSM_LAYERS = (DEPTH + 1) // 2
N_ATTN_LAYERS = DEPTH // 2
N_DENSE_LAYERS = (DEPTH + 1) // 2
N_MOE_LAYERS = DEPTH // 2

kernel_name = "hybrid_s5_diffattn_moe_trunk"

def rms_norm(x, g):
    xf = x.astype(jnp.float32)
    y = xf * lax.rsqrt(jnp.mean(xf * xf, axis=-1, keepdims=True) + RMS_EPS)
    return (y * g.astype(jnp.float32)).astype(x.dtype)

def swiglu(h, w_gate_up, w_down):
    g, u = jnp.split(h @ w_gate_up, 2, axis=-1)
    return (jax.nn.silu(g) * u) @ w_down

def s5_mixer(u, a_re, a_im, log_dt, b_re, b_im, c_re, c_im, d_skip):
    f32 = jnp.float32
    L = u.shape[1]
    dt = jnp.exp(log_dt.astype(f32))[:, None]
    ar = a_re.astype(f32); ai = a_im.astype(f32)
    mag = jnp.exp(ar * dt)
    ab_re = mag * jnp.cos(ai * dt)
    ab_im = mag * jnp.sin(ai * dt)
    den = ar * ar + ai * ai
    nr = ab_re - 1.0; ni = ab_im
    coef_re = (nr * ar + ni * ai) / den
    coef_im = (ni * ar - nr * ai) / den
    br = b_re.astype(f32); bi = b_im.astype(f32)
    bb_re = coef_re[..., None] * br - coef_im[..., None] * bi
    bb_im = coef_re[..., None] * bi + coef_im[..., None] * br
    cr = c_re.astype(f32); ci = c_im.astype(f32)

    def combine(e1, e2):
        a1r, a1i, b1r, b1i = e1
        a2r, a2i, b2r, b2i = e2
        return (a2r * a1r - a2i * a1i,
                a2r * a1i + a2i * a1r,
                a2r * b1r - a2i * b1i + b2r,
                a2r * b1i + a2i * b1r + b2i)

    def per_sequence(ub):
        ug = ub.astype(f32).reshape(L, SSM_GROUPS, SSM_GROUP)
        x_re = jnp.einsum('lgc,gpc->lgp', ug, bb_re)
        x_im = jnp.einsum('lgc,gpc->lgp', ug, bb_im)
        a_re_l = jnp.broadcast_to(ab_re, x_re.shape)
        a_im_l = jnp.broadcast_to(ab_im, x_im.shape)
        _, _, s_re, s_im = lax.associative_scan(combine, (a_re_l, a_im_l, x_re, x_im), axis=0)
        y = jnp.einsum('lgp,gcp->lgc', s_re, cr) - jnp.einsum('lgp,gcp->lgc', s_im, ci)
        return y.reshape(L, D_MODEL)

    y = lax.map(per_sequence, u)
    y = y + d_skip.astype(f32) * u.astype(f32)
    return y.astype(u.dtype)

def rel_bucket(n):
    n = jnp.maximum(n, 0)
    is_small = n < REL_MAX_EXACT
    nf = jnp.maximum(n, 1).astype(jnp.float32)
    large = REL_MAX_EXACT + (jnp.log(nf / REL_MAX_EXACT) / math.log(REL_MAX_DIST / REL_MAX_EXACT)
                             * (REL_BUCKETS - REL_MAX_EXACT)).astype(jnp.int32)
    large = jnp.minimum(large, REL_BUCKETS - 1)
    return jnp.where(is_small, n, large)

def diff_attention(h, w_qkv, lq1, lk1, lq2, lk2, subln_g, w_o, rel_bias, lambda_init):
    B_, L, _ = h.shape
    q, k, v = jnp.split(h @ w_qkv, 3, axis=-1)
    q = q.reshape(B_, L, ATTN_HEADS, 2, ATTN_HD).transpose(0, 2, 3, 1, 4)
    k = k.reshape(B_, L, ATTN_HEADS, 2, ATTN_HD).transpose(0, 2, 3, 1, 4)
    v = v.reshape(B_, L, ATTN_HEADS, 2 * ATTN_HD).transpose(0, 2, 1, 3)
    f32 = jnp.float32
    lam = (jnp.exp(jnp.sum(lq1.astype(f32) * lk1.astype(f32)))
           - jnp.exp(jnp.sum(lq2.astype(f32) * lk2.astype(f32))) + lambda_init)
    n_blocks = L // Q_BLOCK
    q_blocks = q.reshape(B_, ATTN_HEADS, 2, n_blocks, Q_BLOCK, ATTN_HD).transpose(3, 0, 1, 2, 4, 5)
    k_pos = jnp.arange(L, dtype=jnp.int32)
    scale = ATTN_HD ** -0.5
    bias_table = rel_bias.astype(f32).T

    def block(args):
        qb, start = args
        q_pos = start + jnp.arange(Q_BLOCK, dtype=jnp.int32)
        rel = q_pos[:, None] - k_pos[None, :]
        s = jnp.einsum('bhmqd,bhmkd->bhmqk', qb, k).astype(f32) * scale
        s = s + bias_table[:, rel_bucket(rel)][None, :, None]
        s = jnp.where((rel >= 0)[None, None, None], s, -jnp.inf)
        p = jax.nn.softmax(s, axis=-1)
        p = p[:, :, 0] - lam * p[:, :, 1]
        return jnp.einsum('bhqk,bhkd->bhqd', p.astype(v.dtype), v)

    starts = jnp.arange(n_blocks, dtype=jnp.int32) * Q_BLOCK
    o = lax.map(block, (q_blocks, starts))
    o = o.transpose(1, 2, 0, 3, 4).reshape(B_, ATTN_HEADS, L, 2 * ATTN_HD)
    o = rms_norm(o, subln_g) * (1.0 - lambda_init)
    o = o.transpose(0, 2, 1, 3).reshape(B_, L, D_MODEL)
    return o @ w_o

def moe_ffn(h, router, w_gate_up, w_down):
    shape = h.shape
    hf = h.reshape(-1, D_MODEL)
    logits = (hf @ router).astype(jnp.float32)
    top_vals, top_idx = lax.top_k(logits, TOP_K)
    gates = jax.nn.softmax(top_vals, axis=-1)
    combine = jnp.sum(jax.nn.one_hot(top_idx, N_EXPERTS, dtype=jnp.float32) * gates[..., None], axis=1)
    y = jnp.zeros_like(hf)
    for e in range(N_EXPERTS):
        y = y + combine[:, e:e + 1].astype(hf.dtype) * swiglu(hf, w_gate_up[e], w_down[e])
    return y.reshape(shape)

def setup_inputs(seed: int = 0) -> dict:
    key = jax.random.key(seed)
    ks = jax.random.split(key, 24)
    nrm = jax.random.normal
    D, G, P, C, F, E = D_MODEL, SSM_GROUPS, SSM_STATE, SSM_GROUP, D_FF, N_EXPERTS
    NA, NB, ND, NM = N_SSM_LAYERS, N_ATTN_LAYERS, N_DENSE_LAYERS, N_MOE_LAYERS
    a_im0 = jnp.pi * jnp.arange(P, dtype=jnp.float32)
    return {
        "x": nrm(ks[0], (BATCH, SEQ, D), jnp.float32),
        "norm_mix_g": 1.0 + 0.01 * nrm(ks[1], (DEPTH, D)),
        "norm_ffn_g": 1.0 + 0.01 * nrm(ks[2], (DEPTH, D)),
        "final_norm_g": 1.0 + 0.01 * nrm(ks[3], (D,)),
        "ssm_a_re": -0.5 + 0.01 * nrm(ks[4], (NA, G, P)),
        "ssm_a_im": a_im0 + 0.01 * nrm(ks[5], (NA, G, P)),
        "ssm_log_dt": jax.random.uniform(ks[6], (NA, G), minval=math.log(1e-3), maxval=math.log(1e-1)),
        "ssm_b_re": nrm(ks[7], (NA, G, P, C)) * (2 * C) ** -0.5,
        "ssm_b_im": nrm(ks[8], (NA, G, P, C)) * (2 * C) ** -0.5,
        "ssm_c_re": nrm(ks[9], (NA, G, C, P)) * (2 * P) ** -0.5,
        "ssm_c_im": nrm(ks[10], (NA, G, C, P)) * (2 * P) ** -0.5,
        "ssm_d": nrm(ks[11], (NA, D)),
        "ssm_w_glu": nrm(ks[12], (NA, D, 2 * D)) * D ** -0.5,
        "attn_w_qkv": nrm(ks[13], (NB, D, 3 * D)) * D ** -0.5,
        "attn_lambda_q1": 0.1 * nrm(ks[14], (NB, ATTN_HD)),
        "attn_lambda_k1": 0.1 * nrm(ks[15], (NB, ATTN_HD)),
        "attn_lambda_q2": 0.1 * nrm(ks[16], (NB, ATTN_HD)),
        "attn_lambda_k2": 0.1 * nrm(ks[17], (NB, ATTN_HD)),
        "attn_subln_g": 1.0 + 0.01 * nrm(ks[18], (NB, 2 * ATTN_HD)),
        "attn_w_o": nrm(ks[19], (NB, D, D)) * D ** -0.5,
        "rel_bias": 0.5 * nrm(ks[20], (REL_BUCKETS, ATTN_HEADS)),
        "ffn_w_gate_up": nrm(ks[21], (ND, D, 2 * F)) * D ** -0.5,
        "ffn_w_down": nrm(ks[22], (ND, F, D)) * F ** -0.5,
        "moe_router": nrm(jax.random.fold_in(ks[23], 0), (NM, D, E)) * D ** -0.5,
        "moe_w_gate_up": nrm(jax.random.fold_in(ks[23], 1), (NM, E, D, 2 * F)) * D ** -0.5,
        "moe_w_down": nrm(jax.random.fold_in(ks[23], 2), (NM, E, F, D)) * F ** -0.5,
    }

def reference(x, norm_mix_g, norm_ffn_g, final_norm_g,
              ssm_a_re, ssm_a_im, ssm_log_dt, ssm_b_re, ssm_b_im, ssm_c_re, ssm_c_im, ssm_d, ssm_w_glu,
              attn_w_qkv, attn_lambda_q1, attn_lambda_k1, attn_lambda_q2, attn_lambda_k2,
              attn_subln_g, attn_w_o, rel_bias,
              ffn_w_gate_up, ffn_w_down, moe_router, moe_w_gate_up, moe_w_down):
    for i in range(DEPTH):
        j = i // 2
        h = rms_norm(x, norm_mix_g[i])
        if i % N_MIXERS == 0:
            y = s5_mixer(h, ssm_a_re[j], ssm_a_im[j], ssm_log_dt[j], ssm_b_re[j], ssm_b_im[j],
                         ssm_c_re[j], ssm_c_im[j], ssm_d[j])
            a, g = jnp.split(jax.nn.gelu(y) @ ssm_w_glu[j], 2, axis=-1)
            x = x + a * jax.nn.sigmoid(g)
        else:
            lambda_init = 0.8 - 0.6 * math.exp(-0.3 * i)
            x = x + diff_attention(h, attn_w_qkv[j], attn_lambda_q1[j], attn_lambda_k1[j],
                                   attn_lambda_q2[j], attn_lambda_k2[j], attn_subln_g[j],
                                   attn_w_o[j], rel_bias, lambda_init)
        h = rms_norm(x, norm_ffn_g[i])
        if i % 2 == 0:
            x = x + swiglu(h, ffn_w_gate_up[j], ffn_w_down[j])
        else:
            x = x + moe_ffn(h, moe_router[j], moe_w_gate_up[j], moe_w_down[j])
    return rms_norm(x, final_norm_g)


_drawn_inputs = setup_inputs


def setup_inputs(seed=0):
    import zlib

    import numpy as np

    out = dict(_drawn_inputs(seed))
    spreads = {}
    factors = {'norm_mix_g': 5.277,
     'final_norm_g': 36.128,
     'ssm_a_re': 64.0,
     'attn_lambda_q1': 5.042,
     'attn_subln_g': 27.02,
     'norm_ffn_g': 2.949}
    for name, (base, spread) in spreads.items():
        noise = np.random.default_rng([zlib.crc32(name.encode()), seed]).standard_normal(out[name].shape)
        drawn = base * np.exp(spread * noise) if base else spread * noise
        out[name] = __import__('jax').numpy.asarray(drawn.astype(out[name].dtype))
    for name, factor in factors.items():
        out[name] = (out[name] * factor).astype(out[name].dtype)
    return out
```

```python
import math
from contextlib import ExitStack

import concourse.bass as bass
from concourse import mybir

F32 = mybir.dt.float32
I32 = mybir.dt.int32
U32 = mybir.dt.uint32
ALU = mybir.AluOpType
ACT = mybir.ActivationFunctionType
AX = mybir.AxisListType

P = 128
D = 1024
DC = D // P
SEQ = 256
TC = SEQ // P
EPS = 1e-6
BANK = 512

G = 64
C = 16
ST = 64
CH = P // C
NCH = SEQ // CH
PAIRS = G // 2
QP = 8
ROUNDS = PAIRS // QP
KP = CH + 1

H = 8
HD = 64
BUCKETS = 32
MAX_EXACT = BUCKETS // 2
MAX_DIST = 128
RELW = 2 * P + P
NEG = -1.0e30
LAMBDA_INIT = 0.8 - 0.6 * math.exp(-0.3)

F = 2816
E = 8
FH = 256
J = F // FH
HALF = D // 2

WIDE_SLOTS = 4
DOWN_SLOTS = 4
GLU_TILES = 2 * D // BANK
QKV_TILES = 3 * D // BANK
WO_TILES = D // BANK
WIDE_STATIC = GLU_TILES + J + QKV_TILES + WO_TILES
FIRST_FFN = GLU_TILES
FIRST_QKV = FIRST_FFN + J
FIRST_WO = FIRST_QKV + QKV_TILES


def bucket_edges():
    import numpy as np
    n = np.arange(SEQ)
    f = np.maximum(n, 1).astype(np.float32)
    large = MAX_EXACT + (np.log(f / np.float32(MAX_EXACT)) / np.float32(math.log(MAX_DIST / MAX_EXACT))
                         * np.float32(BUCKETS - MAX_EXACT)).astype(np.int32)
    b = np.where(n < MAX_EXACT, n, np.minimum(large, BUCKETS - 1))
    return [int(np.searchsorted(b, k)) for k in range(BUCKETS)] + [SEQ]


def reuse_distance(j):
    return j + J - max(k for k in range(J) if k % 4 == j % 4) if j < 4 else 4


def trunk(nc, x, norm_mix_g, norm_ffn_g, final_norm_g, ssm_a_re, ssm_a_im, ssm_log_dt, ssm_b_re,
          ssm_b_im, ssm_c_re, ssm_c_im, ssm_d, ssm_w_glu, attn_w_qkv, attn_lambda_q1,
          attn_lambda_k1, attn_lambda_q2, attn_lambda_k2, attn_subln_g, attn_w_o, rel_bias,
          ffn_w_gate_up, ffn_w_down, moe_router, moe_w_gate_up, moe_w_down, out):
    ctx = ExitStack()
    with ctx:
        def sem(name):
            return ctx.enter_context(nc.semaphore(name))

        def sbuf_in(stack):
            return lambda name, shape, dt=F32: stack.enter_context(nc.sbuf_tensor(name, shape, dt))

        sb = sbuf_in(ctx)
        x_res = sb("x_res", [P, TC, D])
        hT = sb("hT", [P, DC, SEQ])
        ident = sb("ident", [P, P])
        ones = sb("ones", [P, P])
        upto = sb("upto", [P, P])
        slot_no = sb("slot_no", [P, P])
        gain_rows = sb("gain_rows", [3 * DC, P])
        gain = sb("gain", [P, 3, DC])
        small = sb("small", [P, 64])
        wide = [None] * WIDE_SLOTS
        wide[0] = sb("wide0", [P, DC, BANK])
        wide[1] = sb("wide1", [P, DC, BANK])

        ssm_stack = ExitStack()
        ss = sbuf_in(ssm_stack)
        h32 = ss("h32", [NCH, G, CH, C])
        bc32 = hT[0:NCH, :, :].rearrange("p (k c) t -> p k (c t)", k=2)
        a_raw = ss("a_raw", [PAIRS, 2, 2, ST])
        log_dt = ss("log_dt", [PAIRS, 2])
        dt_ = ss("dt_", [PAIRS, 2])
        prep = ss("prep", [PAIRS, 14, P])
        coef4 = ss("coef4", [P, 4, PAIRS])
        b_raw = ss("b_raw", [P, 2, PAIRS, C])
        c_raw = ss("c_raw", [P, 2, 4, 2, ST])
        c_q = ss("c_q", [P, 2, PAIRS, C])
        bb = ss("bb", [P, 2, PAIRS, C])
        pw = ss("pw", [P, 2, KP, PAIRS])
        pr = ss("pr", [P, 2, CH, PAIRS])
        carry = ss("carry", [P, 2, 2, PAIRS])
        tmp_v = ss("tmp_v", [P, QP * KP * C])
        tmp_p = ss("tmp_p", [P, QP * KP * C])
        uT = ss("uT", [P, G, NCH])
        xin = ss("xin", [P, 2, PAIRS, NCH])
        state = ss("state", [P, 2, PAIRS, NCH])
        kern = ss("kern", [C, 2 * QP, P])
        toep = ss("toep", [P, 2, 2 * QP, P])
        x_stack = ExitStack()
        x32 = sbuf_in(x_stack)("x32", [NCH, CH, D])
        x_stack.close()
        bp = ss("bp", [P, 2, QP, CH, C])
        bt = ss("bt", [P, 2, QP, P])
        gk = ss("gk", [P, 2, 2, QP, KP, C])
        y32 = bp[0:NCH, :, :, :, :].rearrange("n r i s c -> n (r i s c)").rearrange(
            "n (t h d) -> n t h d", t=CH, h=2)
        ssm_stack.close()

        xn = sb("xn", [P, TC, D])
        final_gain = sb("final_gain", [P, D])
        wide[2] = sb("wide2", [P, DC, BANK])
        wide[3] = sb("wide3", [P, DC, BANK])
        down = [sb(f"down{s}", [P, 2, D]) for s in range(DOWN_SLOTS)]
        gate = sb("gate", [P, 2, FH])
        act = sb("act", [P, 2, FH])
        actT = sb("actT", [P, 2, 2, P])

        attn_stack = ExitStack()
        sa = sbuf_in(attn_stack)
        qT = sa("qT", [P, H, SEQ])
        kT = sa("kT", [P, H, SEQ])
        v = sa("v", [P, TC, D])
        table = sa("table", [P, BUCKETS, H])
        relrow = sa("relrow", [P, H, RELW])
        bias = sa("bias", [P, H, 3 * P])
        sc = sa("sc", [P, 2, 2, 3 * P])
        probs = sa("probs", [P, 2, 3 * P])
        pT = sa("pT", [P, 2, 3 * P])
        asm = sa("asm", [P, 2, 16])
        lam_in = sa("lam_in", [P, 4, HD])
        lam = sa("lam", [P, 8])
        sub_gain = sa("sub_gain", [P, 1])
        osq = sa("osq", [P, TC, H])
        sqscr = sa("sqscr", [P, 2, P])
        attn_stack.close()

        moe_stack = ExitStack()
        sm = sbuf_in(moe_stack)
        xeT = sm("xeT", [P, DC, P])
        pick = sm("pick", [P, TC, P])
        pick_gate = sm("pick_gate", [P, TC, P])
        pick_gateT = sm("pick_gateT", [P, TC, P])
        ye = sm("ye", [P, D])
        router = sm("router", [P, DC, E])
        rt = sm("rt", [P, TC, 12, E])
        top_i = sm("top_i", [P, TC, 8], U32)
        key = sm("key", [P, TC, 2 * E + 1])
        gates = sm("gates", [P, TC, 2 * E + 1])
        passes = sm("passes", [P, 8])
        passes_i = sm("passes_i", [P, 1], I32)
        moe_stack.close()

        ps = ctx.enter_context(nc.psum_tensor("ps", [P, 8 * BANK], F32))

        def bank(b, n=1):
            return ps[:, b * BANK:(b + n) * BANK]

        rel_scratch = nc.dram_tensor("rel_scratch", [P, H * RELW], F32, kind="Internal")

        x32_in, xres_in = sem("x32_in"), sem("xres_in")
        prep_in, bc_in, b_in, c_in = sem("prep_in"), sem("bc_in"), sem("b_in"), sem("c_in")
        gain_in, const_in = sem("gain_in"), sem("const_in")
        wide_in = [sem(f"wide_in{s}") for s in range(WIDE_SLOTS)]
        down_in = [sem(f"down_in{j}") for j in range(J)]
        moe_wide_in = [sem(f"moe_wide_in{j}") for j in range(J)]
        pool_const, pool_step = sem("pool_const"), sem("pool_step")
        dve_step, act_step = sem("dve_step"), sem("act_step")
        pe_prep, act_prep = sem("pe_prep"), sem("act_prep")
        dve_prep, coef_ready = sem("dve_prep"), sem("coef_ready")
        u_ps, u_sb = sem("u_ps"), sem("u_sb")
        h_ready, hd_ready = sem("h_ready"), sem("hd_ready")
        bp_re, bp_im, bt_ps, bt_sb = sem("bp_re"), sem("bp_im"), sem("bt_ps"), sem("bt_sb")
        xin_ps, xin_sb = sem("xin_ps"), sem("xin_sb")
        gk_re, gk_im, kern_ps, kern_sb = sem("gk_re"), sem("gk_im"), sem("kern_ps"), sem("kern_sb")
        toep_in, toep_zero = sem("toep_in"), sem("toep_zero")
        state_ready, y_ps, y_sb = sem("state_ready"), sem("y_ps"), sem("y_sb")
        yT_ps, yT_sb = sem("yT_ps"), sem("yT_sb")
        glu_ps, glu_sig, glu_add = sem("glu_ps"), sem("glu_sig"), sem("glu_add")
        ms_ready, rms_ready, o_scaled = sem("ms_ready"), sem("rms_ready"), sem("o_scaled")
        sq_done, xn_ready, hT_ps, hT_sb = sem("sq_done"), sem("xn_ready"), sem("hT_ps"), sem("hT_sb")
        gu_done, silu_done, act_ready = sem("gu_done"), sem("silu_done"), sem("act_ready")
        actT_ps, actT_sb, down_done = sem("actT_ps"), sem("actT_sb"), sem("down_done")
        ffn_add = sem("ffn_add")
        qkv_ps, qkv_sb = sem("qkv_ps"), sem("qkv_sb")
        table_in, rel_filled, rel_out, bias_in, lam_ready = (
            sem("table_in"), sem("rel_filled"), sem("rel_out"), sem("bias_in"), sem("lam_ready"))
        sc_ps, sc_sb, max_done, exp_done, probs_ready = (
            sem("sc_ps"), sem("sc_sb"), sem("max_done"), sem("exp_done"), sem("probs_ready"))
        pT_ps, pT_sb, o_ps, osq_done, o_sb = sem("pT_ps"), sem("pT_sb"), sem("o_ps"), sem("osq_done"), sem("o_sb")
        oT_ps, oT_sb, wo_ps, wo_add = sem("oT_ps"), sem("oT_sb"), sem("wo_ps"), sem("wo_add")
        router_in, logit_ps, top_diff, top_exp, sel_ready, cnt_ps, routed = (
            sem("router_in"), sem("logit_ps"), sem("top_diff"), sem("top_exp"), sem("sel_ready"),
            sem("cnt_ps"), sem("routed"))
        pick_ready, gate_pick_ready, gather_ps, xeT_ready = (
            sem("pick_ready"), sem("gate_pick_ready"), sem("gather_ps"), sem("xeT_ready"))
        e_gu, e_silu, e_act, e_actT_ps, e_actT, e_down = (
            sem("e_gu"), sem("e_silu"), sem("e_act"), sem("e_actT_ps"), sem("e_actT"), sem("e_down"))
        pgT_ps, pgT_sb, ye_sb, scat_ps, scat_add = (
            sem("pgT_ps"), sem("pgT_sb"), sem("ye_sb"), sem("scat_ps"), sem("scat_add"))
        final_ready, out_done = sem("final_ready"), sem("out_done")

        CONSTS = 5

        glu_w = ssm_w_glu[0].rearrange("(dc p) n -> p dc n", p=P)
        qkv_w = attn_w_qkv[0].rearrange("(dc p) n -> p dc n", p=P)
        wo_w = attn_w_o[0].rearrange("(dc p) n -> p dc n", p=P)
        gu_w = ffn_w_gate_up[0].rearrange("(dc p) n -> p dc n", p=P)
        dn_w = ffn_w_down[0].rearrange("(j fc p) n -> j p fc n", p=P, fc=2)
        egu_w = moe_w_gate_up[0].rearrange("e (dc p) n -> e p dc n", p=P)
        edn_w = moe_w_down[0].rearrange("e (j fc p) n -> e j p fc n", p=P, fc=2)

        def split_halves(src, width, at, n):
            return src.rearrange("p dc (two w) -> p dc two w", two=2)[:, :, :, at:at + n]

        def static_wide(n):
            if n < FIRST_FFN:
                return split_halves(glu_w, D, n * FH, FH)
            if n < FIRST_QKV:
                return split_halves(gu_w, F, (n - FIRST_FFN) * FH, FH)
            if n < FIRST_WO:
                return qkv_w[:, :, (n - FIRST_QKV) * BANK:(n - FIRST_QKV + 1) * BANK]
            return wo_w[:, :, (n - FIRST_WO) * BANK:(n - FIRST_WO + 1) * BANK]

        def wide_halves(s):
            return wide[s][:, :, :].rearrange("p dc (two w) -> p dc two w", two=2)

        block = ctx.enter_context(nc.Block())

        @block.sync
        def _(sp):
            sp.dma_start(a_raw[:, 0, :, :], ssm_a_re[0].rearrange("(h i) p -> i h p", h=2)).then_inc(prep_in, 16)
            sp.dma_start(a_raw[:, 1, :, :], ssm_a_im[0].rearrange("(h i) p -> i h p", h=2)).then_inc(prep_in, 16)
            sp.dma_start(log_dt[:, :], ssm_log_dt[0].rearrange("(h i) -> i h", h=2),
                         allow_slow_non_contiguous=True).then_inc(prep_in, 16)
            sp.dma_start(x32[:, :, :], x[0].rearrange("(n t) d -> n t d", t=CH)).then_inc(x32_in, 16)
            for r, src in enumerate((ssm_c_re, ssm_c_im)):
                for h in range(2):
                    sp.dma_start(c_raw[:, r, :, h, :], src[0][h * PAIRS:(h + 1) * PAIRS].rearrange(
                        "g c p -> (g c) p").rearrange("(k r) p -> r k p", r=P)).then_inc(c_in, 16)
            for r, src in enumerate((ssm_b_re, ssm_b_im)):
                for h in range(2):
                    sp.dma_start(b_raw[h * ST:(h + 1) * ST, r, :, :],
                                 src[0][h * PAIRS:(h + 1) * PAIRS].rearrange("i p c -> p i c")).then_inc(b_in, 16)
            for k, src in enumerate((norm_mix_g[0:1, :], ssm_d[0:1, :])):
                sp.dma_start(bc32[:, k, :], src.to_broadcast([NCH, D])).then_inc(bc_in, 16)
            for k, src in enumerate((norm_ffn_g[0], norm_mix_g[1], norm_ffn_g[1])):
                sp.dma_start(gain_rows[k * DC:(k + 1) * DC, :], src.rearrange("(c p) -> c p", p=P)).then_inc(gain_in, 16)
            sp.dma_start(x_res[:, :, :], x[0].rearrange("(c p) d -> p c d", p=P)).then_inc(xres_in, 16)

            def wait_wide_used(n):
                if n < FIRST_FFN:
                    sp.wait_ge(glu_ps, (n + 1) * TC)
                elif n < FIRST_QKV:
                    sp.wait_ge(gu_done, (n - FIRST_FFN + 1) * TC)
                elif n < FIRST_WO:
                    m = n - FIRST_QKV + 1
                    sp.wait_ge(qkv_ps, 4 * m if m <= 4 else 16 + (m - 4) * TC)
                else:
                    sp.wait_ge(wo_ps, (n - FIRST_WO + 1) * TC)

            def load_wide(n):
                if n >= WIDE_SLOTS:
                    wait_wide_used(n - WIDE_SLOTS)
                src, s = static_wide(n), n % WIDE_SLOTS
                dst = wide_halves(s) if n < FIRST_QKV else wide[s][:, :, :]
                if n < FIRST_QKV:
                    for k in range(2):
                        sp.dma_start(dst[:, :, k, :], src[:, :, k, :]).then_inc(wide_in[s], 16)
                else:
                    sp.dma_start(dst, src).then_inc(wide_in[s], 32)

            for n in range(2):
                load_wide(n)
            for q in range(ROUNDS):
                sp.wait_ge(toep_zero, 1)
                sp.wait_ge(kern_sb, 4 * (q + 1))
                if q >= 2:
                    sp.wait_ge(y_ps, 4 * (q - 1))
                for s in range(CH):
                    sp.dma_start(toep[s * C:(s + 1) * C, q % 2, :, s * C:P],
                                 kern[:, :, 0:P - s * C]).then_inc(toep_in, 16)
            sp.wait_ge(yT_ps, 4)
            sp.dma_start(final_gain[:, :], final_norm_g.unsqueeze(0).to_broadcast([P, D])).then_inc(const_in, 16)
            for n in range(2, FIRST_FFN):
                load_wide(n)
            sp.dma_start(table[:, :, :], rel_bias.rearrange("b h -> (b h)").unsqueeze(0).to_broadcast(
                [P, BUCKETS * H])).then_inc(table_in, 16)
            for k, src in enumerate((attn_lambda_q1, attn_lambda_k1, attn_lambda_q2, attn_lambda_k2)):
                sp.dma_start(lam_in[:, k, :], src.to_broadcast([P, HD])).then_inc(table_in, 16)
            sp.dma_start(sub_gain[:, :], attn_subln_g.rearrange("o d -> d o"),
                         allow_slow_non_contiguous=True).then_inc(table_in, 16)
            for j in range(J):
                load_wide(FIRST_FFN + j)
                if j >= DOWN_SLOTS:
                    sp.wait_ge(down_done, (j - DOWN_SLOTS + 1) * TC)
                sp.dma_start(down[j % DOWN_SLOTS][:, :, :], dn_w[j]).then_inc(down_in[j], 16)
                if j == 4:
                    sp.wait_ge(rel_filled, 1)
                    sp.dma_start(rel_scratch.ap(), relrow[:, :, :]).then_inc(rel_out, 16)
                if j == 6:
                    sp.wait_ge(rel_out, 16)
                    pitch = H * RELW - 1
                    sp.dma_start(bias[:, :, 0:P],
                                 bass.AP(rel_scratch, 2 * P - 1, [[pitch, P], [RELW, H], [1, P]])).then_inc(bias_in, 16)
                    sp.dma_start(bias[:, :, P:3 * P],
                                 bass.AP(rel_scratch, P - 1, [[pitch, P], [RELW, H], [1, 2 * P]])).then_inc(bias_in, 16)
            for n in range(FIRST_QKV, WIDE_STATIC):
                load_wide(n)

            def load_expert(it, e):
                for j in range(J):
                    sp.wait_ge(e_gu, it * J + (J + j - reuse_distance(j) + 1))
                    src = egu_w[bass.ds(e, 1)].rearrange("o p dc (two w) -> (o p) dc two w", two=2)
                    for k in range(2):
                        sp.dma_start(wide_halves(j % WIDE_SLOTS)[:, :, k, :],
                                     src[:, :, k, j * FH:(j + 1) * FH]).then_inc(moe_wide_in[j], 16)
                    sp.wait_ge(e_down, it * J + (J + j - reuse_distance(j) + 1))
                    sp.dma_start(down[j % DOWN_SLOTS][:, :, :],
                                 edn_w[bass.ds(e, 1), j].rearrange("o p fc n -> (o p) fc n")).then_inc(down_in[j], 16)

            sp.wait_ge(pT_sb, H)
            sp.dma_start(router[:, :, :], moe_router[0].rearrange("(dc p) e -> p dc e", p=P)).then_inc(router_in, 16)
            for n in range(WIDE_STATIC - WIDE_SLOTS, WIDE_STATIC):
                wait_wide_used(n)
            sp.wait_ge(down_done, J * TC)
            with sp.Fori(0, E) as it:
                load_expert(it, it)
            sp.wait_ge(routed, 1)
            n_pass = sp.value_load(passes_i[0:1, 0:1], min_val=1, max_val=2)
            with sp.If(n_pass > 1):
                with sp.Fori(E, 2 * E) as it:
                    load_expert(it, it - E)
            for c in range(TC):
                sp.wait_ge(final_ready, c + 1)
                sp.dma_start(out[0, c * P:(c + 1) * P, :], xn[:, c, :]).then_inc(out_done, 16)
            sp.wait_ge(out_done, 16 * TC)

        @block.gpsimd
        def _(pool):
            n_step = [0]

            def step(ins):
                n_step[0] += 1
                ins.then_inc(pool_step, 1)
                pool.wait_ge(pool_step, n_step[0])

            step(pool.memset(ident[:, :], 0.0))
            pool.affine_select(out=ident[:, :], in_=ident[:, :], compare_op=ALU.not_equal, fill=1.0,
                               base=0, pattern=[[-1, P]], channel_multiplier=1).then_inc(pool_const, 1)
            step(pool.memset(ones[:, :], 1.0))
            pool.affine_select(out=upto[:, :], in_=ones[:, :], compare_op=ALU.is_ge, fill=0.0,
                               base=0, pattern=[[1, P]], channel_multiplier=-1).then_inc(pool_const, 1)
            pool.iota(slot_no[:, :], [[1, P]], base=0, channel_multiplier=0,
                      allow_small_or_imprecise_dtypes=True).then_inc(pool_const, 3)
            pool.memset(toep[:, :, :, :], 0.0).then_inc(toep_zero, 1)

            t = tmp_p[:, 0:QP * CH * C].rearrange("p (i s c) -> p i s c", i=QP, s=CH)
            pool.wait_ge(dve_prep, 2)
            pool.wait_ge(h_ready, 1)
            for q in range(ROUNDS):
                if q >= 1:
                    pool.wait_ge(bt_ps, 4 * q)
                i = slice(q * QP, (q + 1) * QP)
                b_of = lambda r: bb[:, r, i, :].unsqueeze(2).to_broadcast([P, QP, CH, C])
                p_of = lambda r: pr[:, r, :, i].rearrange("p s i -> p i s").unsqueeze(3).to_broadcast([P, QP, CH, C])
                step(pool.tensor_tensor(bp[:, 1, :, :, :], b_of(0), p_of(1), ALU.mult))
                step(pool.tensor_tensor(t, b_of(1), p_of(0), ALU.mult))
                pool.tensor_tensor(bp[:, 1, :, :, :], bp[:, 1, :, :, :], t, ALU.add).then_inc(bp_im, 1)

            def skip():
                pool.wait_ge(u_sb, 4)
                for s in range(CH):
                    ins = pool.tensor_tensor(h32[:, :, s, :], h32[:, :, s, :],
                                             bc32[:, 1, :].rearrange("n (g c) -> n g c", g=G), ALU.mult)
                ins.then_inc(hd_ready, 1)

            t9 = tmp_p[:, :].rearrange("p (i k c) -> p i k c", i=QP, k=KP)
            for q in range(ROUNDS):
                if q >= 2:
                    pool.wait_ge(y_ps, 4 * (q - 1))
                i = slice(q * QP, (q + 1) * QP)
                c_of = lambda r: c_q[:, r, i, :].unsqueeze(2).to_broadcast([P, QP, KP, C])
                p_of = lambda r: pw[:, r, :, i].rearrange("p k i -> p i k").unsqueeze(3).to_broadcast([P, QP, KP, C])
                g = gk[:, q % 2, 1, :, :, :]
                step(pool.tensor_tensor(g, c_of(0), p_of(1), ALU.mult))
                step(pool.tensor_tensor(t9, c_of(1), p_of(0), ALU.mult))
                step(pool.tensor_tensor(g, g, t9, ALU.add))
                pool.tensor_scalar(g, g, -1.0, None, ALU.mult).then_inc(gk_im, 1)
                if q == 1:
                    skip()

            pool.wait_ge(table_in, 16 * 6)
            edges = bucket_edges()
            step(pool.memset(relrow[:, :, :], NEG))
            for b in range(BUCKETS):
                lo, hi = SEQ - edges[b + 1], SEQ - edges[b]
                ins = pool.tensor_copy(relrow[:, :, lo:hi], table[:, b, :].unsqueeze(2).to_broadcast([P, H, hi - lo]))
            ins.then_inc(rel_filled, 1)

        @block.scalar
        def _(act_e):
            n_step = [0]

            def step(ins):
                n_step[0] += 1
                ins.then_inc(act_step, 1)
                act_e.wait_ge(act_step, n_step[0])

            def activation(*a, **k):
                return nc.scalar.activation(*a, **k)

            n_root = [0]

            def root(ms):
                n_root[0] += 1
                act_e.wait_ge(ms_ready, n_root[0])
                activation(ms, ms, ACT.Sqrt).then_inc(rms_ready, 1)

            act_e.wait_ge(prep_in, 48)
            activation(dt_[:, :], log_dt[:, :], ACT.Exp).then_inc(act_prep, 1)
            act_e.wait_ge(dve_prep, 1)
            activation(prep[:, 1, :], prep[:, 0, :], ACT.Exp).then_inc(act_prep, 1)
            activation(prep[:, 3, :], prep[:, 2, :], ACT.Sin, scale=0.5).then_inc(act_prep, 1)
            activation(prep[:, 4, :], prep[:, 2, :], ACT.Sin).then_inc(act_prep, 1)
            act_e.wait_ge(x32_in, 16)
            for s in range(CH):
                ins = activation(uT[0:NCH, 0:NCH, :].rearrange("p a b -> p (a b)"), x32[:, s, :], ACT.Square,
                                 accum_out=small[0:NCH, s:s + 1])
                ins.then_inc(sq_done, 1)
                act_e.wait_ge(sq_done, s + 1)
            root(small[0:NCH, 0:CH])
            act_e.wait_ge(pe_prep, 1)
            for r in range(2):
                activation(c_q[:, r, :, :].rearrange("p i c -> p (i c)"), bank(4 + r), ACT.Copy).then_inc(act_prep, 1)
            for b in range(4):
                act_e.wait_ge(u_ps, b + 1)
                activation(uT[:, b * C:(b + 1) * C, :].rearrange("p g n -> p (g n)"), bank(b), ACT.Copy).then_inc(u_sb, 1)
            for q in range(ROUNDS):
                for b in range(4):
                    act_e.wait_ge(bt_ps, 4 * q + b + 1)
                    activation(bt[:, :, :, :].rearrange("p r i s -> p (r i s)")[:, b * BANK:(b + 1) * BANK],
                               bank(b), ACT.Copy).then_inc(bt_sb, 1)
                act_e.wait_ge(xin_ps, q + 1)
                src = bank(4, 2).rearrange("p (r i v n) -> p r i v n", r=2, i=QP, v=2)
                for h in range(2):
                    part = slice(h * ST, (h + 1) * ST)
                    for r in range(2):
                        activation(xin[part, r, q * QP:(q + 1) * QP, :], src[part, r, :, h, :],
                                   ACT.Copy).then_inc(xin_sb, 1)
            for q in range(ROUNDS):
                if q >= 1:
                    act_e.wait_ge(toep_in, 16 * CH * q)
                for b in range(4):
                    act_e.wait_ge(kern_ps, 4 * q + b + 1)
                    activation(kern[:, 4 * b:4 * b + 4, :].rearrange("p g k -> p (g k)"), bank(4 + b % 2)[0:C, :],
                               ACT.Copy).then_inc(kern_sb, 1)
            for b in range(4):
                act_e.wait_ge(yT_ps, b + 1)
                act_e.wait_ge(hd_ready, 1)
                for k in range(2):
                    activation(hT[:, b + 4 * k, :].rearrange("p (n t) -> p t n", t=CH),
                               bank(6 + b % 2)[:, k * SEQ:(k + 1) * SEQ].rearrange("p (t n) -> p t n", t=CH),
                               ACT.Gelu_apprx_tanh).then_inc(yT_sb, 1)
            for u in range(GLU_TILES * TC):
                act_e.wait_ge(glu_ps, u + 1)
                if u >= 2:
                    act_e.wait_ge(glu_add, u - 1)
                activation(gate[:, u % 2, :], bank(u % 4)[:, FH:2 * FH], ACT.Sigmoid).then_inc(glu_sig, 1)

            def squares(ready, value):
                for c in range(TC):
                    act_e.wait_ge(ready, value(c))
                    activation(xn[:, c, :], x_res[:, c, :], ACT.Square,
                               accum_out=small[:, 8 + c:9 + c]).then_inc(sq_done, 1)
                root(small[:, 8:8 + TC])

            squares(glu_add, lambda c: GLU_TILES * TC)
            for u in range(J * TC + 1):
                if u < J * TC:
                    act_e.wait_ge(gu_done, u + 1)
                    if u >= 2:
                        act_e.wait_ge(act_ready, u - 1)
                    activation(gate[:, u % 2, :], bank(u % 2)[:, 0:FH], ACT.Silu).then_inc(silu_done, 1)
                if u >= 1:
                    w = u - 1
                    act_e.wait_ge(actT_ps, w + 1)
                    if w >= 2:
                        act_e.wait_ge(down_done, w - 1)
                    activation(actT[:, w % 2, :, :].rearrange("p f s -> p (f s)"), bank(2 + w % 2)[:, 0:2 * P],
                               ACT.Copy).then_inc(actT_sb, 1)
            squares(ffn_add, lambda c: 2 * (c + 1))
            act_e.wait_ge(lam_ready, 1)
            activation(lam[:, 2:4], lam[:, 0:2], ACT.Exp).then_inc(lam_ready, 1)
            for u in range(4 * 4 + 2 * TC):
                act_e.wait_ge(qkv_ps, u + 1)
                if u < 8:
                    o, src, scale = qT[:, u, :], bank(u % 4)[:, 0:SEQ], HD ** -0.5
                elif u < 16:
                    o, src, scale = kT[:, u - 8, :], bank(u % 4)[:, 0:SEQ], 1.0
                else:
                    k, c = divmod(u - 16, TC)
                    o, src, scale = v[:, c, k * BANK:(k + 1) * BANK], bank(u % 4), 1.0
                activation(o, src, ACT.Copy, scale=scale).then_inc(qkv_sb, 1)

            def head_tail(h):
                act_e.wait_ge(pT_ps, h + 1)
                if h >= 2:
                    act_e.wait_ge(o_ps, h - 1)
                activation(pT[:, h % 2, :], bank(4 + h % 2)[:, 0:3 * P], ACT.Copy).then_inc(pT_sb, 1)
                act_e.wait_ge(o_ps, h + 1)
                for qb in range(2):
                    activation(sqscr[:, qb, :], bank(6 + h % 2)[:, qb * P:(qb + 1) * P], ACT.Square,
                               accum_out=osq[:, qb, h:h + 1]).then_inc(osq_done, 1)

            for h in range(H):
                act_e.wait_ge(max_done, h + 1)
                for m in range(2):
                    for qb in range(2):
                        cols = slice(0, P) if qb == 0 else slice(P, 3 * P)
                        k = 2 * qb + m
                        activation(sc[:, h % 2, m, cols], sc[:, h % 2, m, cols], ACT.Exp,
                                   bias=asm[:, h % 2, k:k + 1], accum_out=asm[:, h % 2, 4 + k:5 + k]
                                   ).then_inc(exp_done, 1)
                if h >= 1:
                    act_e.wait_ge(osq_done, 2 * (h - 1))
                    head_tail(h - 1)
            head_tail(H - 1)
            root(osq[:, :, :].rearrange("p c h -> p (c h)"))
            act_e.wait_ge(lam_ready, 3)
            for u in range(4):
                act_e.wait_ge(oT_ps, u + 1)
                c, k = divmod(u, 2)
                activation(hT[:, 4 * k:4 * k + 4, c * P:(c + 1) * P],
                           bank(u).rearrange("p (dc t) -> p dc t", dc=4), ACT.Copy,
                           scale=sub_gain[:, :]).then_inc(oT_sb, 1)
            squares(wo_add, lambda c: 4)
            act_e.wait_ge(top_diff, 1)
            activation(rt[:, :, 4, 0], rt[:, :, 3, 0], ACT.Exp).then_inc(top_exp, 1)

            def expert(it):
                for j in range(J + 1):
                    if j < J:
                        act_e.wait_ge(e_gu, it * J + (J + j + 1))
                        if j >= 2:
                            act_e.wait_ge(e_act, it * J + (j - 1))
                        activation(gate[:, j % 2, :], bank(j % 2)[:, 0:FH], ACT.Silu).then_inc(e_silu, 1)
                    if j >= 1:
                        w = j - 1
                        act_e.wait_ge(e_actT_ps, it * J + (w + 1))
                        if w >= 2:
                            act_e.wait_ge(e_down, it * J + (J + w - 1))
                        activation(actT[:, w % 2, :, :].rearrange("p f s -> p (f s)"),
                                   bank(2 + w % 2)[:, 0:2 * P], ACT.Copy).then_inc(e_actT, 1)
                act_e.wait_ge(pgT_ps, it + 1)
                activation(pick_gateT[:, :, :].rearrange("p c t -> p (c t)"), bank(3)[:, 0:TC * P],
                           ACT.Copy).then_inc(pgT_sb, 1)
                act_e.wait_ge(e_down, it * J + 2 * J)
                for k in range(2):
                    activation(ye[:, k * HALF:(k + 1) * HALF], bank(4 + k), ACT.Copy).then_inc(ye_sb, 1)

            with act_e.Fori(0, E) as it:
                expert(it)
            act_e.wait_ge(routed, 1)
            n_pass = act_e.value_load(passes_i[0:1, 0:1], min_val=1, max_val=2)
            with act_e.If(n_pass > 1):
                with act_e.Fori(E, 2 * E) as it:
                    expert(it)
            for c in range(TC):
                act_e.wait_ge(scat_add, n_pass * (4 * E))
                activation(xn[:, c, :], x_res[:, c, :], ACT.Square,
                           accum_out=small[:, 8 + c:9 + c]).then_inc(sq_done, 1)
            root(small[:, 8:8 + TC])

        @block.vector
        def _(dve):
            n_step = [0]

            def step(ins):
                n_step[0] += 1
                ins.then_inc(dve_step, 1)
                dve.wait_ge(dve_step, n_step[0])

            tt, ts, stt = dve.tensor_tensor, dve.tensor_scalar, dve.scalar_tensor_tensor
            mul, add, sub = ALU.mult, ALU.add, ALU.subtract
            n_rms = [0]

            def inverse_mean(ms, width):
                step(ts(ms, ms, 1.0 / width, EPS, mul, add))
                dve.reciprocal(ms, ms).then_inc(ms_ready, 1)
                n_rms[0] += 1
                dve.wait_ge(rms_ready, n_rms[0])


            dve.wait_ge(prep_in, 48)
            dve.wait_ge(act_prep, 1)
            ar = a_raw[:, 0, :, :]
            ai = a_raw[:, 1, :, :]
            arf, aif = (z.rearrange("p h s -> p (h s)") for z in (ar, ai))
            dtb = dt_[:, :].unsqueeze(2).to_broadcast([PAIRS, 2, ST])
            w = lambda k: prep[:, k, :]
            w3 = lambda k: prep[:, k, :].rearrange("p (h s) -> p h s", h=2)
            step(tt(w3(0), ar, dtb, mul))
            step(tt(w3(2), ai, dtb, mul))
            step(ts(w(5), w(2), 1.0 / (2.0 * math.pi), 12582912.0, mul, add))
            step(ts(w(5), w(5), -12582912.0, None, add))
            c1, c2 = 6.28125, 0.0019340515136718750
            c3 = 2.0 * math.pi - c1 - c2
            for part in (c1, c2, c3):
                step(stt(w(2), w(5), -part, w(2), mul, add))
            step(ts(w(2), w(2), 3.1415925, -3.1415925, ALU.min, ALU.max))
            step(tt(w(6), arf, arf, mul))
            step(tt(w(7), aif, aif, mul))
            tt(w(6), w(6), w(7), add).then_inc(dve_prep, 1)
            dve.wait_ge(dve_prep, 1)
            step(dve.reciprocal(w(6), w(6)))
            dve.wait_ge(act_prep, 4)
            step(tt(w(3), w(3), w(3), mul))
            step(ts(w(3), w(3), -2.0, 1.0, mul, add))
            step(tt(w(8), w(1), w(3), mul))
            step(tt(w(9), w(1), w(4), mul))
            step(ts(w(7), w(8), -1.0, None, add))
            step(tt(w(10), w(7), arf, mul))
            step(tt(w(12), w(9), aif, mul))
            step(tt(w(10), w(10), w(12), add))
            step(tt(w(10), w(10), w(6), mul))
            step(tt(w(11), w(9), arf, mul))
            step(tt(w(12), w(7), aif, mul))
            step(tt(w(11), w(11), w(12), sub))
            tt(w(11), w(11), w(6), mul).then_inc(coef_ready, 1)
            dve.wait_ge(pe_prep, 3)
            step(dve.tensor_copy(gain[:, :, :].rearrange("p k c -> p (k c)"), bank(7)[:, 0:3 * DC]))
            step(dve.tensor_copy(coef4[:, :, :].rearrange("p k i -> p (k i)"), bank(6)[:, 0:4 * PAIRS]))
            dve.memset(pw[:, 0, 0, :], 1.0)
            dve.memset(pw[:, 1, 0, :], 0.0)
            step(dve.tensor_copy(pw[:, :, 1, :], coef4[:, 0:2, :]))
            for n in (1, 2, 4):
                lo, hi = slice(1, n + 1), slice(n + 1, 2 * n + 1)
                t = tmp_v[:, 0:n * PAIRS].rearrange("p (k i) -> p k i", k=n)
                by = lambda r: pw[:, r, n:n + 1, :].to_broadcast([P, n, PAIRS])
                step(tt(pw[:, 0, hi, :], pw[:, 0, lo, :], by(0), mul))
                step(tt(t, pw[:, 1, lo, :], by(1), mul))
                step(tt(pw[:, 0, hi, :], pw[:, 0, hi, :], t, sub))
                step(tt(pw[:, 1, hi, :], pw[:, 0, lo, :], by(1), mul))
                step(tt(t, pw[:, 1, lo, :], by(0), mul))
                step(tt(pw[:, 1, hi, :], pw[:, 1, hi, :], t, add))
            for s in range(CH):
                dve.tensor_copy(pr[:, :, s, :], pw[:, :, CH - 1 - s, :])
            for o in range(2):
                dve.tensor_copy(carry[:, o, o, :], pw[:, 0, CH, :])
            dve.tensor_copy(carry[:, 1, 0, :], pw[:, 1, CH, :])
            step(ts(carry[:, 0, 1, :], pw[:, 1, CH, :], -1.0, None, mul))
            dve.wait_ge(b_in, 64)
            cf = lambda r: coef4[:, 2 + r, :].unsqueeze(2).to_broadcast([P, PAIRS, C])
            t = tmp_v[:, 0:PAIRS * C].rearrange("p (i c) -> p i c", i=PAIRS)
            step(tt(bb[:, 0, :, :], b_raw[:, 0, :, :], cf(0), mul))
            step(tt(t, b_raw[:, 1, :, :], cf(1), mul))
            step(tt(bb[:, 0, :, :], bb[:, 0, :, :], t, sub))
            step(tt(bb[:, 1, :, :], b_raw[:, 1, :, :], cf(0), mul))
            step(tt(t, b_raw[:, 0, :, :], cf(1), mul))
            tt(bb[:, 1, :, :], bb[:, 1, :, :], t, add).then_inc(dve_prep, 1)
            dve.wait_ge(dve_prep, 2)

            dve.wait_ge(sq_done, CH)
            dve.wait_ge(bc_in, 32)
            inverse_mean(small[0:NCH, 0:CH], D)
            for s in range(CH):
                ins = stt(h32[:, :, s, :], x32[:, s, :].rearrange("n (g c) -> n g c", g=G), small[0:NCH, s:s + 1],
                          bc32[:, 0, :].rearrange("n (g c) -> n g c", g=G), mul, mul)
            ins.then_inc(h_ready, 1)
            dve.wait_ge(h_ready, 1)

            t = tmp_v[:, 0:QP * CH * C].rearrange("p (i s c) -> p i s c", i=QP, s=CH)
            for q in range(ROUNDS):
                if q >= 1:
                    dve.wait_ge(bt_ps, 4 * q)
                i = slice(q * QP, (q + 1) * QP)
                b_of = lambda r: bb[:, r, i, :].unsqueeze(2).to_broadcast([P, QP, CH, C])
                p_of = lambda r: pr[:, r, :, i].rearrange("p s i -> p i s").unsqueeze(3).to_broadcast([P, QP, CH, C])
                step(tt(bp[:, 0, :, :, :], b_of(0), p_of(0), mul))
                step(tt(t, b_of(1), p_of(1), mul))
                tt(bp[:, 0, :, :, :], bp[:, 0, :, :, :], t, sub).then_inc(bp_re, 1)
                dve.wait_ge(bp_re, q + 1)

            dve.wait_ge(act_prep, 6)

            def out_powers(q):
                t9 = tmp_v[:, :].rearrange("p (i k c) -> p i k c", i=QP, k=KP)
                i = slice(q * QP, (q + 1) * QP)
                c_of = lambda r: c_q[:, r, i, :].unsqueeze(2).to_broadcast([P, QP, KP, C])
                p_of = lambda r: pw[:, r, :, i].rearrange("p k i -> p i k").unsqueeze(3).to_broadcast([P, QP, KP, C])
                g = gk[:, q % 2, 0, :, :, :]
                step(tt(g, c_of(0), p_of(0), mul))
                step(tt(t9, c_of(1), p_of(1), mul))
                tt(g, g, t9, sub).then_inc(gk_re, 1)
                dve.wait_ge(gk_re, q + 1)

            out_powers(0)
            out_powers(1)
            dve.memset(state[:, :, :, 0], 0.0)
            dve.wait_ge(xin_sb, 4 * ROUNDS)
            step(dve.tensor_copy(state[:, :, :, 1], xin[:, :, :, 0]))
            prod = tmp_v[:, 0:4 * PAIRS].rearrange("p (o r i) -> p o r i", o=2, r=2)
            for n in range(1, NCH - 1):
                s_n = state[:, :, :, n].unsqueeze(1).to_broadcast([P, 2, 2, PAIRS])
                step(tt(prod, carry[:, :, :, :], s_n, mul))
                step(tt(prod[:, :, 0, :], prod[:, :, 0, :], prod[:, :, 1, :], add))
                ins = tt(state[:, :, :, n + 1], prod[:, :, 0, :], xin[:, :, :, n], add)
                if n < NCH - 2:
                    step(ins)
            ins.then_inc(state_ready, 1)
            dve.wait_ge(hd_ready, 1)
            for q in range(ROUNDS):
                for b in range(4):
                    half, k = divmod(b, 2)
                    g = half * PAIRS + q * QP + 4 * k
                    dve.wait_ge(y_ps, 4 * q + b + 1)
                    if q >= 1:
                        dve.wait_ge(yT_ps, q)
                    tt(y32[:, :, half, 4 * k * C:4 * (k + 1) * C].rearrange("n t (g c) -> n g t c", g=4),
                       h32[:, g:g + 4, :, :], bank(b)[0:NCH, :].rearrange("n (g t c) -> n g t c", g=4, t=CH),
                       add).then_inc(y_sb, 1)
                if q + 2 < ROUNDS:
                    out_powers(q + 2)
            dve.wait_ge(xres_in, 16)
            for u in range(GLU_TILES * TC):
                n, c = divmod(u, TC)
                dve.wait_ge(glu_sig, u + 1)
                step(tt(gate[:, u % 2, :], gate[:, u % 2, :], bank(u % 4)[:, 0:FH], mul))
                tt(x_res[:, c, n * FH:(n + 1) * FH], x_res[:, c, n * FH:(n + 1) * FH], gate[:, u % 2, :],
                   add).then_inc(glu_add, 1)

            n_norm = [0]

            def norm():
                k = n_norm[0]
                dve.wait_ge(sq_done, CH + TC * (k + 1))
                inverse_mean(small[:, 8:8 + TC], D)
                for c in range(TC):
                    ts(xn[:, c, :], x_res[:, c, :], small[:, 8 + c:9 + c], None, mul).then_inc(xn_ready, 1)
                if k < 3:
                    dve.wait_ge(const_in, 16)
                    for c in range(TC):
                        dve.wait_ge(hT_ps, TC * k + c + 1)
                        tt(hT[:, :, c * P:(c + 1) * P], bank(4 * c, 2).rearrange("p (dc t) -> p dc t", dc=DC),
                           gain[:, k, :].unsqueeze(2).to_broadcast([P, DC, P]), mul).then_inc(hT_sb, 1)
                n_norm[0] += 1

            norm()
            for u in range(J * TC):
                dve.wait_ge(silu_done, u + 1)
                if u >= 2:
                    dve.wait_ge(actT_ps, u - 1)
                tt(act[:, u % 2, :], gate[:, u % 2, :], bank(u % 2)[:, FH:2 * FH], mul).then_inc(act_ready, 1)
                if u == 8:
                    dve.wait_ge(table_in, 96)
                    for k in range(2):
                        step(tt(sqscr[:, k, 0:HD], lam_in[:, 2 * k, :], lam_in[:, 2 * k + 1, :], mul))
                    dve.tensor_reduce(lam[:, 0:2], sqscr[:, :, 0:HD], AX.X, add).then_inc(lam_ready, 1)
            for c in range(TC):
                dve.wait_ge(down_done, J * TC)
                for k in range(2):
                    o = x_res[:, c, k * HALF:(k + 1) * HALF]
                    tt(o, o, bank(4 + 2 * c + k), add).then_inc(ffn_add, 1)
            norm()
            dve.wait_ge(lam_ready, 2)
            step(tt(lam[:, 4:5], lam[:, 3:4], lam[:, 2:3], sub))
            step(ts(lam[:, 4:5], lam[:, 4:5], -LAMBDA_INIT, None, add))
            ts(sub_gain[:, :], sub_gain[:, :], 1.0 - LAMBDA_INIT, None, mul).then_inc(lam_ready, 1)
            dve.wait_ge(bias_in, 32)

            def scores(h):
                if h >= 2:
                    dve.wait_ge(probs_ready, h - 1)
                dve.wait_ge(sc_ps, h + 1)
                s = sc[:, h % 2, :, :]
                raw = bank(2 * (h % 2), 2).rearrange("p (m k) -> p m k", m=2)[:, :, 0:3 * P]
                tt(s, raw, bias[:, h, :].unsqueeze(1).to_broadcast([P, 2, 3 * P]), add).then_inc(sc_sb, 1)
                dve.wait_ge(sc_sb, h + 1)
                if h >= 2:
                    dve.wait_ge(o_sb, h - 1)
                st = asm[:, h % 2, :]
                dve.tensor_reduce(st[:, 0:2], s[:, :, 0:P], AX.X, ALU.max)
                step(dve.tensor_reduce(st[:, 2:4], s[:, :, P:3 * P], AX.X, ALU.max))
                ts(st[:, 0:4], st[:, 0:4], -1.0, None, mul).then_inc(max_done, 1)

            def combine(h):
                st = asm[:, h % 2, :]
                dve.wait_ge(exp_done, 4 * (h + 1))
                step(dve.reciprocal(st[:, 8:12], st[:, 4:8]))
                step(ts(st[:, 9:12:2], st[:, 9:12:2], lam[:, 4:5], None, mul))
                if h >= 2:
                    dve.wait_ge(pT_ps, h - 1)
                for qb in range(2):
                    cols = slice(0, P) if qb == 0 else slice(P, 3 * P)
                    step(ts(probs[:, h % 2, cols], sc[:, h % 2, 0, cols], st[:, 8 + 2 * qb:9 + 2 * qb], None, mul))
                    ins = stt(probs[:, h % 2, cols], sc[:, h % 2, 1, cols], st[:, 9 + 2 * qb:10 + 2 * qb],
                              probs[:, h % 2, cols], mul, add)
                ins.then_inc(probs_ready, 1)

            def head_out(h):
                dve.wait_ge(osq_done, 2 * (h + 1))
                dve.tensor_copy(xn[:, :, h * P:(h + 1) * P],
                                bank(6 + h % 2)[:, 0:2 * P].rearrange("p (c d) -> p c d", c=TC)).then_inc(o_sb, 1)

            dve.wait_ge(hT_ps, 2 * TC)
            scores(0)
            for h in range(H):
                if h + 1 < H:
                    if h >= 1:
                        head_out(h - 1)
                    scores(h + 1)
                combine(h)
            head_out(H - 2)
            head_out(H - 1)
            inverse_mean(osq[:, :, :].rearrange("p c h -> p (c h)"), 2 * HD)
            dve.wait_ge(o_sb, H)
            for c in range(TC):
                o = xn[:, c, :].rearrange("p (h d) -> p h d", h=H)
                tt(o, o, osq[:, c, :].unsqueeze(2).to_broadcast([P, H, P]), mul).then_inc(o_scaled, 1)
            for u in range(WO_TILES * TC):
                n, c = divmod(u, TC)
                dve.wait_ge(wo_ps, u + 1)
                o = x_res[:, c, n * BANK:(n + 1) * BANK]
                tt(o, o, bank(4 + u), add).then_inc(wo_add, 1)
            norm()

            dve.wait_ge(logit_ps, 1)
            logit, top, first, second, sel, comb = (rt[:, :, k, :] for k in (0, 1, 5, 6, 7, 8))
            step(dve.tensor_copy(logit, bank(6)[:, 0:TC * E].rearrange("p (c e) -> p c e", c=TC)))
            for c in range(TC):
                step(dve.max(rt[:, c, 1, :], rt[:, c, 0, :]))
                step(dve.max_index(top_i[:, c, :], rt[:, c, 1, :], rt[:, c, 0, :]))
                step(dve.tensor_copy(rt[:, c, 2, :], top_i[:, c, :]))
                for k, o in enumerate((5, 6)):
                    step(ts(rt[:, c, o, :], slot_no[:, 0:E], rt[:, c, 2, k:k + 1], None, ALU.is_equal))
            tt(rt[:, :, 3, 0], rt[:, :, 1, 1], rt[:, :, 1, 0], sub).then_inc(top_diff, 1)
            tt(sel, first, second, add).then_inc(sel_ready, 1)
            dve.wait_ge(top_exp, 1)
            step(ts(rt[:, :, 4, 1], rt[:, :, 4, 0], 1.0, None, add))
            step(dve.reciprocal(rt[:, :, 4, 2], rt[:, :, 4, 1]))
            step(tt(rt[:, :, 4, 3], rt[:, :, 4, 0], rt[:, :, 4, 2], mul))
            step(tt(comb, first, rt[:, :, 4, 2:3].to_broadcast([P, TC, E]), mul))
            step(tt(second, second, rt[:, :, 4, 3:4].to_broadcast([P, TC, E]), mul))
            step(tt(comb, comb, second, add))
            dve.memset(gates[:, :, 2 * E:2 * E + 1], 0.0)
            dve.tensor_copy(gates[:, :, 0:E], comb)
            dve.tensor_copy(gates[:, :, E:2 * E], comb)
            dve.wait_ge(cnt_ps, 1)
            dve.memset(key[:, :, 2 * E:2 * E + 1], -1.0)
            step(tt(key[:, :, 0:E], bank(7)[:, 0:TC * E].rearrange("p (c e) -> p c e", c=TC), sel, mul))
            step(ts(key[:, :, 0:E], key[:, :, 0:E], -1.0, None, add))
            dve.tensor_scalar(key[:, :, E:2 * E], key[:, :, 0:E], -float(P), None, add)
            step(dve.tensor_reduce(passes[:, 0:1], bank(7)[:, TC * E:(TC + 1) * E], AX.X, ALU.max))
            step(ts(passes[:, 1:2], passes[:, 0:1], float(P), 1.0, ALU.is_gt, add))
            dve.tensor_copy(passes_i[:, :], passes[:, 1:2]).then_inc(routed, 1)

            def pick_tokens(it):
                for c in range(TC):
                    ts(pick[:, c, :], slot_no[:, :], key[:, c, bass.ds(it, 1)], None, ALU.is_equal).then_inc(pick_ready, 1)

            def gather_out(n):
                dve.wait_ge(gather_ps, n)
                tt(xeT[:, :, :], bank(6, 2).rearrange("p (dc s) -> p dc s", dc=DC),
                   gain[:, 2, :].unsqueeze(2).to_broadcast([P, DC, P]), mul).then_inc(xeT_ready, 1)

            def expert(it):
                for j in range(J):
                    dve.wait_ge(e_silu, it * J + (j + 1))
                    if j >= 2:
                        dve.wait_ge(e_actT_ps, it * J + (j - 1))
                    tt(act[:, j % 2, :], gate[:, j % 2, :], bank(j % 2)[:, FH:2 * FH], mul).then_inc(e_act, 1)
                    if j == 4:
                        for c in range(TC):
                            ts(pick_gate[:, c, :], slot_no[:, :], key[:, c, bass.ds(it, 1)],
                               gates[:, c, bass.ds(it, 1)], ALU.is_equal, mul).then_inc(gate_pick_ready, 1)
                        pick_tokens(it + 1)
                gather_out(it + 2)
                for u in range(4):
                    c, k = divmod(u, 2)
                    o = x_res[:, c, k * HALF:(k + 1) * HALF]
                    dve.wait_ge(scat_ps, it * 4 + (u + 1))
                    tt(o, o, bank(4 + u), add).then_inc(scat_add, 1)
                dve.wait_ge(scat_add, it * 4 + 4)

            pick_tokens(0)
            gather_out(1)
            with dve.Fori(0, E) as it:
                expert(it)
            n_pass = dve.value_load(passes_i[0:1, 0:1], min_val=1, max_val=2)
            with dve.If(n_pass > 1):
                with dve.Fori(E, 2 * E) as it:
                    expert(it)
            dve.wait_ge(const_in, 16)
            dve.wait_ge(sq_done, CH + TC * 4)
            inverse_mean(small[:, 8:8 + TC], D)
            for c in range(TC):
                stt(xn[:, c, :], x_res[:, c, :], small[:, 8 + c:9 + c], final_gain[:, :], mul, mul).then_inc(final_ready, 1)

        @block.tensor
        def _(pe):
            mm = pe.matmul

            def transpose(o, i, n=P):
                return pe.transpose(o, i, ident[0:n, 0:n])

            pe.wait_ge(pool_const, CONSTS)
            pe.wait_ge(c_in, 64)
            for r in range(2):
                for k in range(4):
                    ins = transpose(bank(4 + r)[:, k * P:(k + 1) * P], c_raw[:, r, k, :, :].rearrange("p h s -> p (h s)"))
            ins.then_inc(pe_prep, 1)
            pe.wait_ge(coef_ready, 1)
            for k in range(4):
                ins = transpose(bank(6)[:, k * PAIRS:(k + 1) * PAIRS], prep[:, 8 + k, :], PAIRS)
            ins.then_inc(pe_prep, 1)
            pe.wait_ge(gain_in, 48)
            transpose(bank(7)[:, 0:3 * DC], gain_rows[:, :], 3 * DC).then_inc(pe_prep, 1)
            pe.wait_ge(h_ready, 1)
            for g in range(G):
                b, k = divmod(g, C)
                ins = transpose(bank(b)[:, k * NCH:(k + 1) * NCH], h32[:, g, :, :].rearrange("n s c -> n (s c)"), NCH)
                if k == C - 1:
                    ins.then_inc(u_ps, 1)
            for q in range(ROUNDS):
                pe.wait_ge(bp_re, q + 1)
                pe.wait_ge(bp_im, q + 1)
                for b in range(4):
                    if q == 0:
                        pe.wait_ge(u_sb, b + 1)
                    else:
                        pe.wait_ge(bt_sb, 4 * (q - 1) + b + 1)
                    for k in range(4):
                        r, i = divmod(4 * b + k, QP)
                        ins = transpose(bank(b)[:, k * P:(k + 1) * P], bp[:, r, i, :, :].rearrange("p s c -> p (s c)"))
                    ins.then_inc(bt_ps, 1)
                pe.wait_ge(bt_sb, 4 * (q + 1))
                if q == 0:
                    pe.wait_ge(act_prep, 6)
                else:
                    pe.wait_ge(xin_sb, 4 * q)
                for r in range(2):
                    for i in range(QP):
                        g = q * QP + i
                        at = (r * QP + i) * 2 * NCH
                        ins = mm(bank(4, 2)[:, at:at + 2 * NCH], bt[:, r, i, :], uT[:, g::PAIRS, :],
                                 start=True, stop=True)
                ins.then_inc(xin_ps, 1)

            def groups(q):
                for b in range(4):
                    half, k = divmod(b, 2)
                    yield b, [(half, 4 * k + n) for n in range(4)]

            def impulse(q):
                pe.wait_ge(gk_re, q + 1)
                pe.wait_ge(gk_im, q + 1)
                if q == 0:
                    pe.wait_ge(xin_sb, 4 * ROUNDS)
                for b, members in groups(q):
                    if 4 * q + b >= 2:
                        pe.wait_ge(kern_sb, 4 * q + b - 1)
                    for n, (half, i) in enumerate(members):
                        part = slice(half * ST, (half + 1) * ST)
                        for r in range(2):
                            ins = mm(bank(4 + b % 2)[0:C, n * P:(n + 1) * P], bb[part, r, q * QP + i, :],
                                     gk[part, q % 2, r, i, 0:CH, :], start=(r == 0), stop=(r == 1))
                    ins.then_inc(kern_ps, 1)

            def mixer_out(q):
                pe.wait_ge(toep_in, 16 * CH * (q + 1))
                for b, members in groups(q):
                    if q >= 1:
                        pe.wait_ge(y_sb, 4 * (q - 1) + b + 1)
                    for n, (half, i) in enumerate(members):
                        part = slice(half * ST, (half + 1) * ST)
                        o = bank(b)[0:NCH, n * P:(n + 1) * P]
                        mm(o, uT[:, half * PAIRS + q * QP + i, :], toep[:, q % 2, 4 * b + n, :],
                           start=True, stop=False)
                        for r in range(2):
                            ins = mm(o, state[part, r, q * QP + i, :], gk[part, q % 2, r, i, 1:KP, :],
                                     start=False, stop=(r == 1))
                    ins.then_inc(y_ps, 1)

            def mixer_out_T(q):
                pe.wait_ge(y_sb, 4 * (q + 1))
                if q >= 2:
                    pe.wait_ge(yT_sb, 2 * (q - 1))
                for half in range(2):
                    for s in range(CH):
                        ins = transpose(bank(6 + q % 2)[:, half * SEQ + s * NCH:half * SEQ + (s + 1) * NCH],
                                        y32[:, s, half, :], NCH)
                ins.then_inc(yT_ps, 1)

            impulse(0)
            impulse(1)
            pe.wait_ge(state_ready, 1)
            mixer_out(0)
            for q in range(1, ROUNDS):
                if q + 1 < ROUNDS:
                    impulse(q + 1)
                mixer_out_T(q - 1)
                mixer_out(q)
            mixer_out_T(ROUNDS - 1)
            pe.wait_ge(yT_sb, DC)

            def wide_tile(n):
                pe.wait_ge(wide_in[n % WIDE_SLOTS], 32 * (n // WIDE_SLOTS + 1))
                return wide[n % WIDE_SLOTS]

            for n in range(GLU_TILES):
                wt = wide_tile(n)
                for c in range(TC):
                    u = n * TC + c
                    if u >= 4:
                        pe.wait_ge(glu_add, u - 3)
                    for dc in range(DC):
                        ins = mm(bank(u % 4), hT[:, dc, c * P:(c + 1) * P], wt[:, dc, :],
                                 start=(dc == 0), stop=(dc == DC - 1))
                    ins.then_inc(glu_ps, 1)

            n_norm = [0]

            def norm_transposes():
                k = n_norm[0]
                for c in range(TC):
                    pe.wait_ge(xn_ready, TC * k + c + 1)
                    for dc in range(DC):
                        ins = transpose(bank(4 * c, 2)[:, dc * P:(dc + 1) * P], xn[:, c, dc * P:(dc + 1) * P])
                    ins.then_inc(hT_ps, 1)
                pe.wait_ge(hT_sb, TC * (k + 1))
                n_norm[0] += 1

            norm_transposes()
            for u in range(J * TC + 2):
                if u < J * TC:
                    j, c = divmod(u, TC)
                    wt = wide_tile(FIRST_FFN + j)
                    if u >= 2:
                        pe.wait_ge(act_ready, u - 1)
                    for dc in range(DC):
                        ins = mm(bank(u % 2), hT[:, dc, c * P:(c + 1) * P], wt[:, dc, :],
                                 start=(dc == 0), stop=(dc == DC - 1))
                    ins.then_inc(gu_done, 1)
                if 1 <= u <= J * TC:
                    w = u - 1
                    pe.wait_ge(act_ready, w + 1)
                    if w >= 2:
                        pe.wait_ge(actT_sb, w - 1)
                    for f in range(2):
                        ins = transpose(bank(2 + w % 2)[:, f * P:(f + 1) * P], act[:, w % 2, f * P:(f + 1) * P])
                    ins.then_inc(actT_ps, 1)
                if u >= 2:
                    w = u - 2
                    j, c = divmod(w, TC)
                    pe.wait_ge(actT_sb, w + 1)
                    pe.wait_ge(down_in[j], 16)
                    for f in range(2):
                        for k in range(2):
                            ins = mm(bank(4 + 2 * c + k), actT[:, w % 2, f, :],
                                     down[j % DOWN_SLOTS][:, f, k * HALF:(k + 1) * HALF],
                                     start=(j == 0 and f == 0), stop=(j == J - 1 and f == 1))
                    ins.then_inc(down_done, 1)
            pe.wait_ge(ffn_add, 4)
            norm_transposes()
            for n in range(QKV_TILES):
                wt = wide_tile(FIRST_QKV + n)
                for m in range(4 if n < 4 else TC):
                    u = 4 * n + m if n < 4 else 16 + (n - 4) * TC + m
                    if u >= 4:
                        pe.wait_ge(qkv_sb, u - 3)
                    for dc in range(DC):
                        flags = dict(start=(dc == 0), stop=(dc == DC - 1))
                        if n < 4:
                            ins = mm(bank(u % 4)[:, 0:SEQ], wt[:, dc, m * P:(m + 1) * P], hT[:, dc, :], **flags)
                        else:
                            ins = mm(bank(u % 4), hT[:, dc, m * P:(m + 1) * P], wt[:, dc, :], **flags)
                    ins.then_inc(qkv_ps, 1)

            def score_products(h):
                if h == 0:
                    pe.wait_ge(qkv_sb, 4 * 4 + 2 * TC)
                if h >= 2:
                    pe.wait_ge(sc_sb, h - 1)
                for m in range(2):
                    part = slice(m * HD, (m + 1) * HD)
                    o = bank(2 * (h % 2) + m)
                    mm(o[:, 0:P], qT[part, h, 0:P], kT[part, h, 0:P], start=True, stop=True)
                    ins = mm(o[:, P:3 * P], qT[part, h, P:2 * P], kT[part, h, :], start=True, stop=True)
                ins.then_inc(sc_ps, 1)

            score_products(0)
            for h in range(H):
                if h + 1 < H:
                    score_products(h + 1)
                pe.wait_ge(probs_ready, h + 1)
                if h >= 2:
                    pe.wait_ge(pT_sb, h - 1)
                for k in range(3):
                    ins = transpose(bank(4 + h % 2)[:, k * P:(k + 1) * P], probs[:, h % 2, k * P:(k + 1) * P])
                ins.then_inc(pT_ps, 1)
                pe.wait_ge(pT_sb, h + 1)
                if h >= 2:
                    pe.wait_ge(o_sb, h - 1)
                o = bank(6 + h % 2)
                head = slice(h * P, (h + 1) * P)
                mm(o[:, 0:P], pT[:, h % 2, 0:P], v[:, 0, head], start=True, stop=True)
                mm(o[:, P:2 * P], pT[:, h % 2, P:2 * P], v[:, 0, head], start=True, stop=False)
                mm(o[:, P:2 * P], pT[:, h % 2, 2 * P:3 * P], v[:, 1, head], start=False, stop=True).then_inc(o_ps, 1)
            pe.wait_ge(o_scaled, TC)
            for u in range(4):
                c, k = divmod(u, 2)
                for n in range(4):
                    dc = 4 * k + n
                    ins = transpose(bank(u)[:, n * P:(n + 1) * P], xn[:, c, dc * P:(dc + 1) * P])
                ins.then_inc(oT_ps, 1)
            pe.wait_ge(oT_sb, 4)
            for n in range(WO_TILES):
                wt = wide_tile(FIRST_WO + n)
                for c in range(TC):
                    for dc in range(DC):
                        ins = mm(bank(4 + n * TC + c), hT[:, dc, c * P:(c + 1) * P], wt[:, dc, :],
                                 start=(dc == 0), stop=(dc == DC - 1))
                    ins.then_inc(wo_ps, 1)
            pe.wait_ge(wo_add, 4)
            norm_transposes()
            pe.wait_ge(router_in, 16)
            for c in range(TC):
                for dc in range(DC):
                    ins = mm(bank(6)[:, c * E:(c + 1) * E], hT[:, dc, c * P:(c + 1) * P], router[:, dc, :],
                             start=(dc == 0), stop=(dc == DC - 1))
            ins.then_inc(logit_ps, 1)
            pe.wait_ge(sel_ready, 1)
            counts = bank(7)
            mm(counts[:, 0:E], upto[:, :], rt[:, 0, 7, :], start=True, stop=True)
            mm(counts[:, E:2 * E], ones[:, :], rt[:, 0, 7, :], start=True, stop=False)
            mm(counts[:, E:2 * E], upto[:, :], rt[:, 1, 7, :], start=False, stop=True)
            mm(counts[:, 2 * E:3 * E], ones[:, :], rt[:, 0, 7, :], start=True, stop=False)
            mm(counts[:, 2 * E:3 * E], ones[:, :], rt[:, 1, 7, :], start=False, stop=True).then_inc(cnt_ps, 1)

            def gather(n_pick):
                pe.wait_ge(pick_ready, n_pick)
                for dc in range(DC):
                    for c in range(TC):
                        ins = mm(bank(6, 2)[:, dc * P:(dc + 1) * P], xn[:, c, dc * P:(dc + 1) * P], pick[:, c, :],
                                 start=(c == 0), stop=(c == TC - 1))
                ins.then_inc(gather_ps, 1)

            def expert(it):
                pe.wait_ge(xeT_ready, it + 1)
                for j in range(J + 2):
                    if j < J:
                        pe.wait_ge(moe_wide_in[j], it * 32 + 32)
                        if j >= 2:
                            pe.wait_ge(e_act, it * J + (j - 1))
                        for dc in range(DC):
                            ins = mm(bank(j % 2), xeT[:, dc, :], wide[j % WIDE_SLOTS][:, dc, :],
                                     start=(dc == 0), stop=(dc == DC - 1))
                        ins.then_inc(e_gu, 1)
                    if j == J - 1:
                        gather(it * TC + 2 * TC)
                    if 1 <= j <= J:
                        w = j - 1
                        pe.wait_ge(e_act, it * J + (w + 1))
                        if w >= 2:
                            pe.wait_ge(e_actT, it * J + (w - 1))
                        for f in range(2):
                            ins = transpose(bank(2 + w % 2)[:, f * P:(f + 1) * P], act[:, w % 2, f * P:(f + 1) * P])
                        ins.then_inc(e_actT_ps, 1)
                    if j >= 2:
                        w = j - 2
                        pe.wait_ge(e_actT, it * J + (w + 1))
                        pe.wait_ge(down_in[w], it * 16 + 32)
                        for f in range(2):
                            for k in range(2):
                                ins = mm(bank(4 + k), actT[:, w % 2, f, :],
                                         down[w % DOWN_SLOTS][:, f, k * HALF:(k + 1) * HALF],
                                         start=(w == 0 and f == 0), stop=(w == J - 1 and f == 1))
                        ins.then_inc(e_down, 1)
                pe.wait_ge(gate_pick_ready, it * TC + TC)
                for c in range(TC):
                    ins = transpose(bank(3)[:, c * P:(c + 1) * P], pick_gate[:, c, :])
                ins.then_inc(pgT_ps, 1)
                pe.wait_ge(pgT_sb, it + 1)
                pe.wait_ge(ye_sb, it * 2 + 2)
                pe.wait_ge(xeT_ready, it + 2)
                for u in range(4):
                    c, k = divmod(u, 2)
                    mm(bank(4 + u), pick_gateT[:, c, :], ye[:, k * HALF:(k + 1) * HALF],
                       start=True, stop=True).then_inc(scat_ps, 1)
                pe.wait_ge(scat_add, it * 4 + 4)

            pe.sem_inc(e_gu, J)
            pe.sem_inc(e_down, J)
            gather(TC)
            with pe.Fori(0, E) as it:
                expert(it)
            pe.wait_ge(routed, 1)
            n_pass = pe.value_load(passes_i[0:1, 0:1], min_val=1, max_val=2)
            with pe.If(n_pass > 1):
                with pe.Fori(E, 2 * E) as it:
                    expert(it)


_INS = ["x", "norm_mix_g", "norm_ffn_g", "final_norm_g", "ssm_a_re", "ssm_a_im", "ssm_log_dt", "ssm_b_re",
        "ssm_b_im", "ssm_c_re", "ssm_c_im", "ssm_d", "ssm_w_glu", "attn_w_qkv", "attn_lambda_q1",
        "attn_lambda_k1", "attn_lambda_q2", "attn_lambda_k2", "attn_subln_g", "attn_w_o", "rel_bias",
        "ffn_w_gate_up", "ffn_w_down", "moe_router", "moe_w_gate_up", "moe_w_down"]


def kernel(**inputs):
    import numpy as _np
    import concourse.bacc as _bacc
    from concourse import mybir as _mybir
    from concourse.bass_utils import run_bass_kernel_spmd as _run

    nc = _bacc.Bacc("TRN2", target_bir_lowering=False, num_devices=1)
    arrays, args = {}, []
    for name in _INS:
        a = _np.ascontiguousarray(inputs[name])
        arrays[f"in_{name}_dram"] = a
        args.append(nc.dram_tensor(f"in_{name}_dram", a.shape, _mybir.dt.from_np(a.dtype), kind="ExternalInput").ap())
    args.append(nc.dram_tensor("out_0_dram", (1, SEQ, D), F32, kind="ExternalOutput").ap())
    trunk(nc, *args)
    r = _run(nc, [arrays], core_ids=[0])
    return r.results[0]["out_0_dram"]
```

```python
import math
from contextlib import ExitStack

import concourse.bass as bass
from concourse import mybir

F32 = mybir.dt.float32
F32R = mybir.dt.float32r
I32 = mybir.dt.int32
U32 = mybir.dt.uint32
ALU = mybir.AluOpType
ACT = mybir.ActivationFunctionType
AX = mybir.AxisListType

P = 128
D = 1024
DC = D // P
SEQ = 256
TC = SEQ // P
EPS = 1e-6
BANK = 512

G = 64
C = 16
ST = 64
CH = P // C
NCH = SEQ // CH
PAIRS = G // 2
QP = 8
ROUNDS = PAIRS // QP
KP = CH + 1

H = 8
HD = 64
BUCKETS = 32
MAX_EXACT = BUCKETS // 2
MAX_DIST = 128
RELW = 2 * P + P
NEG = -1.0e30
LAMBDA_INIT = 0.8 - 0.6 * math.exp(-0.3)

F = 2816
E = 8
FH = 256
J = F // FH
HALF = D // 2

TILE = 4 * BANK
PART = TILE // 2
RAW_SLOTS = 11
PART_SLOTS = 6
GLU_BLOCKS = 2 * D // BANK
QKV_BLOCKS = 3 * D // BANK
WO_BLOCKS = D // BANK
MIX_TILES = 3 * J
MIX_PARTS = 2 * MIX_TILES
FIRST_FFN = 2 * GLU_BLOCKS
FIRST_QKV = FIRST_FFN + MIX_TILES
FIRST_WO = FIRST_QKV + 2 * QKV_BLOCKS
FIRST_MOE = FIRST_WO + 2 * WO_BLOCKS
assert MIX_TILES % RAW_SLOTS == 0 and MIX_PARTS % PART_SLOTS == 0


def w_part(j):
    return 6 * j - 2 if j else 0


def d_part(j):
    return 6 * j + 8 if j < J - 1 else MIX_PARTS - 2


def is_down(p):
    p %= MIX_PARTS
    return any(d_part(j) <= p < d_part(j) + 2 for j in range(J))


def downs_before(p):
    turns, p = divmod(p, MIX_PARTS)
    return 2 * J * turns + sum(is_down(k) for k in range(p))


def bucket_edges():
    import numpy as np
    n = np.arange(SEQ)
    f = np.maximum(n, 1).astype(np.float32)
    large = MAX_EXACT + (np.log(f / np.float32(MAX_EXACT)) / np.float32(math.log(MAX_DIST / MAX_EXACT))
                         * np.float32(BUCKETS - MAX_EXACT)).astype(np.int32)
    b = np.where(n < MAX_EXACT, n, np.minimum(large, BUCKETS - 1))
    return [int(np.searchsorted(b, k)) for k in range(BUCKETS)] + [SEQ]


def trunk(nc, x, norm_mix_g, norm_ffn_g, final_norm_g, ssm_a_re, ssm_a_im, ssm_log_dt, ssm_b_re,
          ssm_b_im, ssm_c_re, ssm_c_im, ssm_d, ssm_w_glu, attn_w_qkv, attn_lambda_q1,
          attn_lambda_k1, attn_lambda_q2, attn_lambda_k2, attn_subln_g, attn_w_o, rel_bias,
          ffn_w_gate_up, ffn_w_down, moe_router, moe_w_gate_up, moe_w_down, out):
    ctx = ExitStack()
    with ctx:
        def sem(name):
            return ctx.enter_context(nc.semaphore(name))

        def sbuf_in(stack):
            return lambda name, shape, dt=F32: stack.enter_context(nc.sbuf_tensor(name, shape, dt))

        sb = sbuf_in(ctx)
        x_res = sb("x_res", [P, TC, D])
        ident = sb("ident", [P, P])
        ones = sb("ones", [P, P])
        upto = sb("upto", [P, P])
        slot_no = sb("slot_no", [P, P])
        gain_rows = sb("gain_rows", [3 * DC, P])
        gain = sb("gain", [P, 3, DC])
        small = sb("small", [P, 64])
        beside = ExitStack()
        bc32 = sbuf_in(beside)("bc32", [NCH, 2, D])
        beside.close()
        sc = sbuf_in(beside)("sc", [P, 2, 2, 3 * P])
        probs = sbuf_in(beside)("probs", [P, 2, 3 * P])
        pT = sbuf_in(beside)("pT", [P, 2, 3 * P])
        beside.close()
        final_gain = sbuf_in(beside)("final_gain", [P, D])
        beside.close()
        hT_hi = sb("hT_hi", [P, DC, SEQ], F32R)
        hT_lo = sb("hT_lo", [P, DC, SEQ], F32R)
        raw = [None] * RAW_SLOTS
        EARLY = 2
        for r in range(EARLY):
            raw[r] = sb(f"raw{r}", [P, TILE])

        ssm_stack = ExitStack()
        ss = sbuf_in(ssm_stack)
        h32 = ss("h32", [NCH, G, CH, C])
        a_raw = ss("a_raw", [PAIRS, 2, 2, ST])
        log_dt = ss("log_dt", [PAIRS, 2])
        dt_ = ss("dt_", [PAIRS, 2])
        prep = ss("prep", [PAIRS, 14, P])
        coef4 = ss("coef4", [P, 4, PAIRS])
        b_raw = ss("b_raw", [P, 2, PAIRS, C])
        c_raw = ss("c_raw", [P, 2, 4, 2, ST])
        c_q = ss("c_q", [P, 2, PAIRS, C])
        bb = ss("bb", [P, 2, PAIRS, C])
        pw = ss("pw", [P, 2, KP, PAIRS])
        pr = ss("pr", [P, 2, CH, PAIRS])
        carry = ss("carry", [P, 2, 2, PAIRS])
        tmp_v = ss("tmp_v", [P, QP * KP * C])
        tmp_p = ss("tmp_p", [P, QP * KP * C])
        uT = ss("uT", [P, G, NCH])
        xin = ss("xin", [P, 2, PAIRS, NCH])
        state = ss("state", [P, 2, PAIRS, NCH])
        kern = ss("kern", [C, 2 * QP, P])
        toep = ss("toep", [P, 2, 2 * QP, P])
        x_stack = ExitStack()
        x32 = sbuf_in(x_stack)("x32", [NCH, CH, D])
        x_stack.close()
        bp = ss("bp", [P, 2, QP, CH, C])
        bt = ss("bt", [P, 2, QP, P])
        gk = ss("gk", [P, 2, 2, QP, KP, C])
        y32 = bp[0:NCH, :, :, :, :].rearrange("n r i s c -> n (r i s c)").rearrange(
            "n (t h d) -> n t h d", t=CH, h=2)
        ssm_stack.close()

        xn = sb("xn", [P, TC, D])
        for r in range(EARLY, RAW_SLOTS):
            raw[r] = sb(f"raw{r}", [P, TILE])
        hi = [sb(f"hi{k}", [P, PART], F32R) for k in range(PART_SLOTS)]
        lo = [sb(f"lo{k}", [P, PART], F32R) for k in range(PART_SLOTS)]
        gate = sb("gate", [P, 2, FH])
        act = sb("act", [P, 2, FH])
        actT_hi = sb("actT_hi", [P, 2, 2 * P], F32R)
        actT_lo = sb("actT_lo", [P, 2, 2 * P], F32R)

        attn_stack = ExitStack()
        sa = sbuf_in(attn_stack)
        table = sa("table", [P, BUCKETS, H])
        asm = sa("asm", [P, 2, 16])
        lam_in = sa("lam_in", [P, 4, HD])
        lam = sa("lam", [P, 8])
        sub_gain = sa("sub_gain", [P, 1])
        osq = sa("osq", [P, TC, H])
        sqscr = sa("sqscr", [P, 2, P])
        rel_stack = ExitStack()
        relrow = sbuf_in(rel_stack)("relrow", [P, H, RELW])
        rel_stack.close()
        qT = sa("qT", [P, H, SEQ])
        kT = sa("kT", [P, H, SEQ])
        v = sa("v", [P, TC, D])
        bias = xn[:, :, :].rearrange("p c d -> p (c d)").rearrange("p (h k) -> p h k", h=H)
        attn_stack.close()

        moe_stack = ExitStack()
        sm = sbuf_in(moe_stack)
        xeT_hi = sm("xeT_hi", [P, DC, P], F32R)
        xeT_lo = sm("xeT_lo", [P, DC, P], F32R)
        pick = sm("pick", [P, TC, P])
        pick_gate = sm("pick_gate", [P, TC, P])
        pick_gateT = sm("pick_gateT", [P, TC, P])
        ye = sm("ye", [P, D])
        router = sm("router", [P, DC, E])
        rt = sm("rt", [P, TC, 12, E])
        top_i = sm("top_i", [P, TC, 8], U32)
        key = sm("key", [P, TC, 2 * E + 1])
        gates = sm("gates", [P, TC, 2 * E + 1])
        passes = sm("passes", [P, 8])
        passes_i = sm("passes_i", [P, 1], I32)
        moe_stack.close()

        ps = ctx.enter_context(nc.psum_tensor("ps", [P, 8 * BANK], F32))

        def bank(b, n=1):
            return ps[:, b * BANK:(b + n) * BANK]

        SCATTER_BANKS = (4, 5, 1, 3)

        rel_scratch = nc.dram_tensor("rel_scratch", [P, H * RELW], F32, kind="Internal")

        x32_in, xres_in = sem("x32_in"), sem("xres_in")
        prep_in, bc_in, b_in, c_in = sem("prep_in"), sem("bc_in"), sem("b_in"), sem("c_in")
        gain_in, const_in = sem("gain_in"), sem("const_in")
        raw_in = [sem(f"raw_in{r}") for r in range(RAW_SLOTS)]
        hi_ready, lo_wide, lo_down, part_used = (
            sem("hi_ready"), sem("lo_wide"), sem("lo_down"), sem("part_used"))
        pool_const, pool_step = sem("pool_const"), sem("pool_step")
        dve_step, act_step = sem("dve_step"), sem("act_step")
        pe_prep, act_prep = sem("pe_prep"), sem("act_prep")
        dve_prep, coef_ready = sem("dve_prep"), sem("coef_ready")
        u_ps, u_sb = sem("u_ps"), sem("u_sb")
        h_ready, hd_ready = sem("h_ready"), sem("hd_ready")
        bp_re, bp_im, bt_ps, bt_sb = sem("bp_re"), sem("bp_im"), sem("bt_ps"), sem("bt_sb")
        xin_ps, xin_sb = sem("xin_ps"), sem("xin_sb")
        gk_re, gk_im, kern_ps, kern_sb = sem("gk_re"), sem("gk_im"), sem("kern_ps"), sem("kern_sb")
        toep_in, toep_zero = sem("toep_in"), sem("toep_zero")
        state_ready, y_ps, y_sb = sem("state_ready"), sem("y_ps"), sem("y_sb")
        yT_ps, gelu_done = sem("yT_ps"), sem("gelu_done")
        glu_sig, glu_add = sem("glu_sig"), sem("glu_add")
        ms_ready, rms_ready, o_scaled = sem("ms_ready"), sem("rms_ready"), sem("o_scaled")
        sq_done, xn_ready, hT_ps = sem("sq_done"), sem("xn_ready"), sem("hT_ps")
        hT_gained, hi_sides, lo_sides = sem("hT_gained"), sem("hi_sides"), sem("lo_sides")
        silu_done, act_ready = sem("silu_done"), sem("act_ready")
        actT_ps, actT_hi_ready, actT_lo_ready = sem("actT_ps"), sem("actT_hi_ready"), sem("actT_lo_ready")
        ffn_add = sem("ffn_add")
        qkv_sb = sem("qkv_sb")
        table_in, rel_filled, rel_out, bias_in, lam_ready = (
            sem("table_in"), sem("rel_filled"), sem("rel_out"), sem("bias_in"), sem("lam_ready"))
        sc_ps, sc_sb, max_done, exp_done, probs_ready = (
            sem("sc_ps"), sem("sc_sb"), sem("max_done"), sem("exp_done"), sem("probs_ready"))
        pT_ps, pT_sb, o_ps, osq_done, o_sb = sem("pT_ps"), sem("pT_sb"), sem("o_ps"), sem("osq_done"), sem("o_sb")
        oT_ps, oT_gained, wo_add = sem("oT_ps"), sem("oT_gained"), sem("wo_add")
        router_in, logit_ps, top_diff, top_exp, sel_ready, cnt_ps, routed = (
            sem("router_in"), sem("logit_ps"), sem("top_diff"), sem("top_exp"), sem("sel_ready"),
            sem("cnt_ps"), sem("routed"))
        pick_ready, gate_pick_ready, gather_ps, xe_gained, xeT_hi_ready, xeT_lo_ready = (
            sem("pick_ready"), sem("gate_pick_ready"), sem("gather_ps"), sem("xe_gained"),
            sem("xeT_hi_ready"), sem("xeT_lo_ready"))
        pgT_ps, pgT_sb, ye_sb, scat_ps, scat_add = (
            sem("pgT_ps"), sem("pgT_sb"), sem("ye_sb"), sem("scat_ps"), sem("scat_add"))
        final_ready, out_done = sem("final_ready"), sem("out_done")

        CONSTS = 5

        glu_w = ssm_w_glu[0].rearrange("(dc p) n -> p dc n", p=P)
        qkv_w = attn_w_qkv[0].rearrange("(dc p) n -> p dc n", p=P)
        wo_w = attn_w_o[0].rearrange("(dc p) n -> p dc n", p=P)
        gu_w = ffn_w_gate_up[0].rearrange("(dc p) n -> p dc n", p=P)
        dn_w = ffn_w_down[0].rearrange("(j fc p) n -> j p fc n", p=P, fc=2)
        egu_w = moe_w_gate_up[0].rearrange("e (dc p) n -> e p dc n", p=P)
        edn_w = moe_w_down[0].rearrange("e (j fc p) n -> e j p fc n", p=P, fc=2)

        WIDE_BEFORE = 2 * (FIRST_MOE - J)
        DOWN_BEFORE = 2 * J

        def static_counts(n):
            p = min(max(n - 2 * FIRST_FFN, 0), MIX_PARTS)
            return n - downs_before(p), downs_before(p)

        class Pass:

            def __init__(self, it=None):
                self.it, self.dense = it, it is None
                self.nb = TC if self.dense else 1

            def add(self, per_pass, n):
                return n if self.dense else self.it * per_pass + n

            def parts(self, p):
                return self.add(MIX_PARTS, 2 * (FIRST_FFN if self.dense else FIRST_MOE) + p)

            def wide(self, p):
                if self.dense:
                    return static_counts(2 * FIRST_FFN + p)[0]
                return self.add(4 * J, WIDE_BEFORE + p - downs_before(p))

            def down(self, p):
                if self.dense:
                    return static_counts(2 * FIRST_FFN + p)[1]
                return self.add(2 * J, DOWN_BEFORE + downs_before(p))

            def items(self, k):
                return self.add(J, (0 if self.dense else TC * J) + k)

            def slot(self, p):
                return (2 * (FIRST_FFN if self.dense else FIRST_MOE) + p) % PART_SLOTS

            def raw(self, p):
                n = (FIRST_FFN if self.dense else FIRST_MOE) + p // 2
                fills = self.add(MIX_TILES // RAW_SLOTS, n // RAW_SLOTS + 1)
                return n % RAW_SLOTS, fills, slice(p % 2 * PART, (p % 2 + 1) * PART)

            def is_down(self, p):
                return is_down(p) and (not self.dense or p < MIX_PARTS)

        class Before:
            parts = staticmethod(lambda n: n)
            wide = staticmethod(lambda n: static_counts(n)[0] if n < 2 * FIRST_MOE else
                                WIDE_BEFORE + (n - 2 * FIRST_MOE) - downs_before(n - 2 * FIRST_MOE))
            slot = staticmethod(lambda n: n % PART_SLOTS)
            raw = staticmethod(lambda n: (n // 2 % RAW_SLOTS, n // 2 // RAW_SLOTS + 1,
                                          slice(n % 2 * PART, (n % 2 + 1) * PART)))
            is_down = staticmethod(lambda n: 2 * FIRST_FFN <= n < 2 * FIRST_QKV and is_down(n - 2 * FIRST_FFN))

        def split_hi(act_e, at, p):
            r, fills, cols = at.raw(p)
            act_e.wait_ge(raw_in[r], fills * 32)
            if at is not Before or p >= PART_SLOTS:
                act_e.wait_ge(part_used, at.parts(p - PART_SLOTS + 1))
            nc.scalar.activation(hi[at.slot(p)][:, :], raw[r][:, cols], ACT.Copy).then_inc(hi_ready, 1)

        def split_lo(eng, at, p):
            r, _, cols = at.raw(p)
            eng.wait_ge(hi_ready, at.parts(p + 1))
            eng.tensor_tensor(lo[at.slot(p)][:, :], raw[r][:, cols], hi[at.slot(p)][:, :].bitcast(F32),
                              ALU.subtract).then_inc(lo_down if at.is_down(p) else lo_wide, 1)

        block = ctx.enter_context(nc.Block())

        @block.sync
        def _(sp):
            sp.dma_start(a_raw[:, 0, :, :], ssm_a_re[0].rearrange("(h i) p -> i h p", h=2)).then_inc(prep_in, 16)
            sp.dma_start(a_raw[:, 1, :, :], ssm_a_im[0].rearrange("(h i) p -> i h p", h=2)).then_inc(prep_in, 16)
            sp.dma_start(log_dt[:, :], ssm_log_dt[0].rearrange("(h i) -> i h", h=2),
                         allow_slow_non_contiguous=True).then_inc(prep_in, 16)
            sp.dma_start(x32[:, :, :], x[0].rearrange("(n t) d -> n t d", t=CH)).then_inc(x32_in, 16)
            for r, src in enumerate((ssm_c_re, ssm_c_im)):
                for h in range(2):
                    sp.dma_start(c_raw[:, r, :, h, :], src[0][h * PAIRS:(h + 1) * PAIRS].rearrange(
                        "g c p -> (g c) p").rearrange("(k r) p -> r k p", r=P)).then_inc(c_in, 16)
            for r, src in enumerate((ssm_b_re, ssm_b_im)):
                for h in range(2):
                    sp.dma_start(b_raw[h * ST:(h + 1) * ST, r, :, :],
                                 src[0][h * PAIRS:(h + 1) * PAIRS].rearrange("i p c -> p i c")).then_inc(b_in, 16)
            for k, src in enumerate((norm_mix_g[0:1, :], ssm_d[0:1, :])):
                sp.dma_start(bc32[:, k, :], src.to_broadcast([NCH, D])).then_inc(bc_in, 16)
            for k, src in enumerate((norm_ffn_g[0], norm_mix_g[1], norm_ffn_g[1])):
                sp.dma_start(gain_rows[k * DC:(k + 1) * DC, :], src.rearrange("(c p) -> c p", p=P)).then_inc(gain_in, 16)
            sp.dma_start(x_res[:, :, :], x[0].rearrange("(c p) d -> p c d", p=P)).then_inc(xres_in, 16)

            def tile_dst(r, down_tile, halves):
                if down_tile:
                    return raw[r][:, :].rearrange("p (fc n) -> p fc n", fc=2)
                if halves:
                    return raw[r][:, :].rearrange("p (dc two w) -> p dc two w", dc=4, two=2)
                return raw[r][:, :].rearrange("p (dc w) -> p dc w", dc=4)

            def load_tile(r, src, down_tile, halves):
                dst = tile_dst(r, down_tile, halves)
                for k in range(2):
                    if down_tile or not halves:
                        part = slice(k * dst.shape[1] // 2, (k + 1) * dst.shape[1] // 2)
                        sp.dma_start(dst[:, part, :], src[:, part, :]).then_inc(raw_in[r], 16)
                    else:
                        sp.dma_start(dst[:, :, k, :], src[:, :, k, :]).then_inc(raw_in[r], 16)

            def halves_src(src, width, block, half):
                return src.rearrange("p dc (two w) -> p dc two w", two=2)[
                    :, 4 * half:4 * half + 4, :, block * FH:(block + 1) * FH]

            def mixer_src(gate_up, down_w, t):
                for j in range(J):
                    if t == d_part(j) // 2:
                        return down_w(j), True
                    if t - w_part(j) // 2 in (0, 1):
                        return halves_src(gate_up, F, j, t - w_part(j) // 2), False

            def load_static(n):
                if n >= RAW_SLOTS:
                    wides, downs = static_counts(2 * (n - RAW_SLOTS + 1))
                    if Before.is_down(2 * (n - RAW_SLOTS)):
                        sp.wait_ge(lo_down, downs)
                    else:
                        sp.wait_ge(lo_wide, wides)
                down_tile, halves = False, n < FIRST_QKV
                if n < FIRST_FFN:
                    src = halves_src(glu_w, D, n // 2, n % 2)
                elif n < FIRST_QKV:
                    src, down_tile = mixer_src(gu_w, lambda j: dn_w[j], n - FIRST_FFN)
                else:
                    w, m = (qkv_w, n - FIRST_QKV) if n < FIRST_WO else (wo_w, n - FIRST_WO)
                    src = w[:, 4 * (m % 2):4 * (m % 2) + 4, m // 2 * BANK:(m // 2 + 1) * BANK]
                load_tile(n % RAW_SLOTS, src, down_tile, halves)

            for n in range(EARLY):
                load_static(n)
            for q in range(ROUNDS):
                sp.wait_ge(toep_zero, 1)
                sp.wait_ge(kern_sb, 4 * (q + 1))
                if q >= 2:
                    sp.wait_ge(y_ps, 4 * (q - 1))
                for s in range(CH):
                    sp.dma_start(toep[s * C:(s + 1) * C, q % 2, :, s * C:P],
                                 kern[:, :, 0:P - s * C]).then_inc(toep_in, 16)
            sp.wait_ge(yT_ps, 4)
            for n in range(EARLY, FIRST_FFN):
                load_static(n)
            sp.dma_start(table[:, :, :], rel_bias.rearrange("b h -> (b h)").unsqueeze(0).to_broadcast(
                [P, BUCKETS * H])).then_inc(table_in, 16)
            for k, src in enumerate((attn_lambda_q1, attn_lambda_k1, attn_lambda_q2, attn_lambda_k2)):
                sp.dma_start(lam_in[:, k, :], src.to_broadcast([P, HD])).then_inc(table_in, 16)
            sp.dma_start(sub_gain[:, :], attn_subln_g.rearrange("o d -> d o"),
                         allow_slow_non_contiguous=True).then_inc(table_in, 16)
            for n in range(FIRST_FFN, FIRST_QKV):
                load_static(n)
                if n == FIRST_FFN + RAW_SLOTS:
                    sp.wait_ge(rel_filled, 1)
                    sp.dma_start(rel_scratch.ap(), relrow[:, :, :]).then_inc(rel_out, 16)
            for n in range(FIRST_QKV, FIRST_WO):
                load_static(n)
                if n == FIRST_QKV + RAW_SLOTS - 3:
                    sp.wait_ge(rel_out, 16)
                    sp.wait_ge(hT_ps, 2 * TC)
                    sp.dma_start(bias[:, :, :], bass.AP(rel_scratch, P - 1, [[H * RELW - 1, P], [RELW, H], [1, 2 * P]])
                                 ).then_inc(bias_in, 16)
            for n in range(FIRST_WO, FIRST_MOE):
                load_static(n)

            def load_expert_tile(at, e, t):
                last = 2 * (t - RAW_SLOTS)
                if last < 0:
                    sp.wait_ge(part_used, at.parts(last + 2))
                elif is_down(last):
                    sp.wait_ge(lo_down, at.down(last + 2))
                else:
                    sp.wait_ge(lo_wide, at.wide(last + 2))
                src, down_tile = mixer_src(egu_w[bass.ds(e, 1)].rearrange("o p dc n -> (o p) dc n"),
                                           lambda j: edn_w[bass.ds(e, 1), j].rearrange("o p fc n -> (o p) fc n"), t)
                load_tile(at.raw(2 * t)[0], src, down_tile, True)

            AHEAD = PART_SLOTS // 2

            def load_expert(it, e, e_next):
                at = Pass(it)
                for t in range(AHEAD, MIX_TILES):
                    load_expert_tile(at, e, t)
                at_next = Pass(it + 1)
                for t in range(AHEAD):
                    load_expert_tile(at_next, e_next, t)

            for t in range(AHEAD):
                load_expert_tile(Pass(0), 0, t)
            sp.wait_ge(pT_sb, H)
            sp.dma_start(router[:, :, :], moe_router[0].rearrange("(dc p) e -> p dc e", p=P)).then_inc(router_in, 16)
            with sp.Fori(0, E - 1) as it:
                load_expert(it, it, it + 1)
            load_expert(E - 1, E - 1, 0)
            sp.wait_ge(routed, 1)
            n_pass = sp.value_load(passes_i[0:1, 0:1], min_val=1, max_val=2)
            with sp.If(n_pass > 1):
                with sp.Fori(E, 2 * E - 1) as it:
                    load_expert(it, it - E, it - (E - 1))
                load_expert(2 * E - 1, E - 1, 0)
            sp.dma_start(final_gain[:, :], final_norm_g.unsqueeze(0).to_broadcast([P, D])).then_inc(const_in, 16)
            for c in range(TC):
                sp.wait_ge(final_ready, c + 1)
                sp.dma_start(out[0, c * P:(c + 1) * P, :], xn[:, c, :]).then_inc(out_done, 16)
            sp.wait_ge(out_done, 16 * TC)

        @block.gpsimd
        def _(pool):
            n_step = [0]

            def step(ins):
                n_step[0] += 1
                ins.then_inc(pool_step, 1)
                pool.wait_ge(pool_step, n_step[0])

            step(pool.memset(ident[:, :], 0.0))
            pool.affine_select(out=ident[:, :], in_=ident[:, :], compare_op=ALU.not_equal, fill=1.0,
                               base=0, pattern=[[-1, P]], channel_multiplier=1).then_inc(pool_const, 1)
            step(pool.memset(ones[:, :], 1.0))
            pool.affine_select(out=upto[:, :], in_=ones[:, :], compare_op=ALU.is_ge, fill=0.0,
                               base=0, pattern=[[1, P]], channel_multiplier=-1).then_inc(pool_const, 1)
            pool.iota(slot_no[:, :], [[1, P]], base=0, channel_multiplier=0,
                      allow_small_or_imprecise_dtypes=True).then_inc(pool_const, 3)
            pool.memset(toep[:, :, :, :], 0.0).then_inc(toep_zero, 1)

            t = tmp_p[:, 0:QP * CH * C].rearrange("p (i s c) -> p i s c", i=QP, s=CH)
            pool.wait_ge(dve_prep, 2)
            pool.wait_ge(h_ready, 1)
            for q in range(ROUNDS):
                if q >= 1:
                    pool.wait_ge(bt_ps, 4 * q)
                i = slice(q * QP, (q + 1) * QP)
                b_of = lambda r: bb[:, r, i, :].unsqueeze(2).to_broadcast([P, QP, CH, C])
                p_of = lambda r: pr[:, r, :, i].rearrange("p s i -> p i s").unsqueeze(3).to_broadcast([P, QP, CH, C])
                step(pool.tensor_tensor(bp[:, 1, :, :, :], b_of(0), p_of(1), ALU.mult))
                step(pool.tensor_tensor(t, b_of(1), p_of(0), ALU.mult))
                pool.tensor_tensor(bp[:, 1, :, :, :], bp[:, 1, :, :, :], t, ALU.add).then_inc(bp_im, 1)

            def skip():
                pool.wait_ge(u_sb, 4)
                for s in range(CH):
                    ins = pool.tensor_tensor(h32[:, :, s, :], h32[:, :, s, :],
                                             bc32[:, 1, :].rearrange("n (g c) -> n g c", g=G), ALU.mult)
                ins.then_inc(hd_ready, 1)

            t9 = tmp_p[:, :].rearrange("p (i k c) -> p i k c", i=QP, k=KP)
            for q in range(ROUNDS):
                if q >= 2:
                    pool.wait_ge(y_ps, 4 * (q - 1))
                i = slice(q * QP, (q + 1) * QP)
                c_of = lambda r: c_q[:, r, i, :].unsqueeze(2).to_broadcast([P, QP, KP, C])
                p_of = lambda r: pw[:, r, :, i].rearrange("p k i -> p i k").unsqueeze(3).to_broadcast([P, QP, KP, C])
                g = gk[:, q % 2, 1, :, :, :]
                step(pool.tensor_tensor(g, c_of(0), p_of(1), ALU.mult))
                step(pool.tensor_tensor(t9, c_of(1), p_of(0), ALU.mult))
                step(pool.tensor_tensor(g, g, t9, ALU.add))
                pool.tensor_scalar(g, g, -1.0, None, ALU.mult).then_inc(gk_im, 1)
                if q == 1:
                    skip()

            pool.wait_ge(table_in, 16 * 6)
            edges = bucket_edges()
            step(pool.memset(relrow[:, :, :], NEG))
            for b in range(BUCKETS):
                lo, hi = SEQ - edges[b + 1], SEQ - edges[b]
                ins = pool.tensor_copy(relrow[:, :, lo:hi], table[:, b, :].unsqueeze(2).to_broadcast([P, H, hi - lo]))
            ins.then_inc(rel_filled, 1)

            for n in range(2 * FIRST_FFN, 2 * FIRST_QKV):
                if Before.is_down(n):
                    split_lo(pool, Before, n)

            def expert(it):
                at = Pass(it)
                for p in range(MIX_PARTS):
                    if at.is_down(p):
                        split_lo(pool, at, p)

            with pool.Fori(0, E) as it:
                expert(it)
            pool.wait_ge(routed, 1)
            n_pass = pool.value_load(passes_i[0:1, 0:1], min_val=1, max_val=2)
            with pool.If(n_pass > 1):
                with pool.Fori(E, 2 * E) as it:
                    expert(it)

        @block.scalar
        def _(act_e):
            n_step = [0]

            def step(ins):
                n_step[0] += 1
                ins.then_inc(act_step, 1)
                act_e.wait_ge(act_step, n_step[0])

            def activation(*a, **k):
                return nc.scalar.activation(*a, **k)

            n_root = [0]

            def root(ms):
                n_root[0] += 1
                act_e.wait_ge(ms_ready, n_root[0])
                activation(ms, ms, ACT.Sqrt).then_inc(rms_ready, 1)

            act_e.wait_ge(prep_in, 48)
            activation(dt_[:, :], log_dt[:, :], ACT.Exp).then_inc(act_prep, 1)
            act_e.wait_ge(dve_prep, 1)
            activation(prep[:, 1, :], prep[:, 0, :], ACT.Exp).then_inc(act_prep, 1)
            activation(prep[:, 3, :], prep[:, 2, :], ACT.Sin, scale=0.5).then_inc(act_prep, 1)
            activation(prep[:, 4, :], prep[:, 2, :], ACT.Sin).then_inc(act_prep, 1)
            act_e.wait_ge(x32_in, 16)
            for s in range(CH):
                ins = activation(uT[0:NCH, 0:NCH, :].rearrange("p a b -> p (a b)"), x32[:, s, :], ACT.Square,
                                 accum_out=small[0:NCH, s:s + 1])
                ins.then_inc(sq_done, 1)
                act_e.wait_ge(sq_done, s + 1)
            root(small[0:NCH, 0:CH])
            act_e.wait_ge(pe_prep, 1)
            for r in range(2):
                activation(c_q[:, r, :, :].rearrange("p i c -> p (i c)"), bank(4 + r), ACT.Copy).then_inc(act_prep, 1)
            for b in range(4):
                act_e.wait_ge(u_ps, b + 1)
                activation(uT[:, b * C:(b + 1) * C, :].rearrange("p g n -> p (g n)"), bank(b), ACT.Copy).then_inc(u_sb, 1)
            for q in range(ROUNDS):
                for b in range(4):
                    act_e.wait_ge(bt_ps, 4 * q + b + 1)
                    activation(bt[:, :, :, :].rearrange("p r i s -> p (r i s)")[:, b * BANK:(b + 1) * BANK],
                               bank(b), ACT.Copy).then_inc(bt_sb, 1)
                act_e.wait_ge(xin_ps, q + 1)
                src = bank(4, 2).rearrange("p (r i v n) -> p r i v n", r=2, i=QP, v=2)
                for h in range(2):
                    part = slice(h * ST, (h + 1) * ST)
                    for r in range(2):
                        activation(xin[part, r, q * QP:(q + 1) * QP, :], src[part, r, :, h, :],
                                   ACT.Copy).then_inc(xin_sb, 1)
            for q in range(ROUNDS):
                if q >= 1:
                    act_e.wait_ge(toep_in, 16 * CH * q)
                for b in range(4):
                    act_e.wait_ge(kern_ps, 4 * q + b + 1)
                    activation(kern[:, 4 * b:4 * b + 4, :].rearrange("p g k -> p (g k)"), bank(4 + b % 2)[0:C, :],
                               ACT.Copy).then_inc(kern_sb, 1)
            for p in range(2):
                split_hi(act_e, Before, p)
            for b in range(4):
                act_e.wait_ge(yT_ps, b + 1)
                act_e.wait_ge(hd_ready, 1)
                out_t = bank(6 + b % 2)
                activation(out_t, out_t, ACT.Gelu_apprx_tanh).then_inc(gelu_done, 1)
                act_e.wait_ge(gelu_done, b + 1)
                for k in range(2):
                    activation(hT_hi[:, b + 4 * k, :].rearrange("p (n t) -> p t n", t=CH),
                               out_t[:, k * SEQ:(k + 1) * SEQ].rearrange("p (t n) -> p t n", t=CH),
                               ACT.Copy).then_inc(hi_sides, 1)
            for p in range(2, PART_SLOTS):
                split_hi(act_e, Before, p)
            for n in range(GLU_BLOCKS):
                for p in range(4):
                    if p == 3:
                        act_e.wait_ge(part_used, 4 * n + 4)
                        for c in range(TC):
                            if n >= 1:
                                act_e.wait_ge(glu_add, TC * (n - 1) + c + 1)
                            activation(gate[:, c, :], bank(2 * (n % 2) + c)[:, FH:2 * FH], ACT.Sigmoid).then_inc(glu_sig, 1)
                    split_hi(act_e, Before, 4 * n + p + PART_SLOTS)

            def squares(ready, value):
                for c in range(TC):
                    act_e.wait_ge(ready, value(c))
                    activation(xn[:, c, :], x_res[:, c, :], ACT.Square,
                               accum_out=small[:, 8 + c:9 + c]).then_inc(sq_done, 1)
                root(small[:, 8:8 + TC])

            n_hT = [0]

            def round_side(side, ps_banks, ready):
                for k in range(2):
                    act_e.wait_ge(ready[0], ready[1](k))
                    activation(side(k), ps_banks(k), ACT.Copy).then_inc(hi_sides, 1)

            def round_hT():
                base = 2 * TC * n_hT[0]
                for c in range(TC):
                    round_side(lambda k: hT_hi[:, 4 * k:4 * k + 4, c * P:(c + 1) * P],
                               lambda k: bank(4 * c + k).rearrange("p (dc t) -> p dc t", dc=4),
                               (hT_gained, lambda k: base + 2 * c + k + 1))
                n_hT[0] += 1

            def mixer_pass(at, finish):
                for j in range(J + 1):
                    if j < J:
                        for p in range(w_part(j), w_part(j) + 4):
                            if p == w_part(j) + 3:
                                act_e.wait_ge(part_used, at.parts(p + 1))
                                for c in range(at.nb):
                                    activation(gate[:, c, :], bank(c)[:, 0:FH], ACT.Silu).then_inc(silu_done, 1)
                            split_hi(act_e, at, p + PART_SLOTS)
                    if j == J:
                        finish()
                    if j >= 1:
                        for p in range(d_part(j - 1), d_part(j - 1) + 2):
                            split_hi(act_e, at, p + PART_SLOTS)
                    if j < J:
                        for c in range(at.nb):
                            act_e.wait_ge(actT_ps, at.items(at.nb * j + c + 1))
                            activation(actT_hi[:, c, :], bank(2 + c)[:, 0:2 * P], ACT.Copy).then_inc(actT_hi_ready, 1)

            squares(glu_add, lambda c: GLU_BLOCKS * TC)
            round_hT()
            mixer_pass(Pass(), lambda: None)
            squares(ffn_add, lambda c: 2 * (c + 1))
            round_hT()
            act_e.wait_ge(lam_ready, 1)
            activation(lam[:, 2:4], lam[:, 0:2], ACT.Exp).then_inc(lam_ready, 1)
            for n in range(QKV_BLOCKS):
                p0 = 2 * FIRST_QKV + 4 * n
                for p in range(4):
                    split_hi(act_e, Before, p0 + p + PART_SLOTS)
                for m in range(4 if n < 4 else TC):
                    if n < 4:
                        o, src = (qT, kT)[n // 2][:, 4 * (n % 2) + m, :], bank(4 * (n % 2) + m)[:, 0:SEQ]
                    else:
                        o, src = v[:, m, (n - 4) * BANK:(n - 3) * BANK], bank(4 * (n % 2) + m)
                    activation(o, src, ACT.Copy, scale=HD ** -0.5 if n < 2 else 1.0).then_inc(qkv_sb, 1)

            def head_tail(h):
                act_e.wait_ge(pT_ps, h + 1)
                if h >= 2:
                    act_e.wait_ge(o_ps, h - 1)
                activation(pT[:, h % 2, :], bank(4 + h % 2)[:, 0:3 * P], ACT.Copy).then_inc(pT_sb, 1)
                act_e.wait_ge(o_ps, h + 1)
                for qb in range(2):
                    activation(sqscr[:, qb, :], bank(6 + h % 2)[:, qb * P:(qb + 1) * P], ACT.Square,
                               accum_out=osq[:, qb, h:h + 1]).then_inc(osq_done, 1)

            for h in range(H):
                act_e.wait_ge(max_done, h + 1)
                for m in range(2):
                    for qb in range(2):
                        cols = slice(0, P) if qb == 0 else slice(P, 3 * P)
                        k = 2 * qb + m
                        activation(sc[:, h % 2, m, cols], sc[:, h % 2, m, cols], ACT.Exp,
                                   bias=asm[:, h % 2, k:k + 1], accum_out=asm[:, h % 2, 4 + k:5 + k]
                                   ).then_inc(exp_done, 1)
                if h >= 1:
                    act_e.wait_ge(osq_done, 2 * (h - 1))
                    head_tail(h - 1)
            head_tail(H - 1)
            root(osq[:, :, :].rearrange("p c h -> p (c h)"))
            act_e.wait_ge(lam_ready, 3)
            for u in range(4):
                act_e.wait_ge(oT_ps, u + 1)
                c, k = divmod(u, 2)
                activation(bank(u), bank(u), ACT.Copy, scale=sub_gain[:, :]).then_inc(oT_gained, 1)
                act_e.wait_ge(oT_gained, u + 1)
                activation(hT_hi[:, 4 * k:4 * k + 4, c * P:(c + 1) * P],
                           bank(u).rearrange("p (dc t) -> p dc t", dc=4), ACT.Copy).then_inc(hi_sides, 1)
            for p in range(4 * WO_BLOCKS):
                split_hi(act_e, Before, 2 * FIRST_WO + p + PART_SLOTS)
            squares(wo_add, lambda c: 4)
            round_hT()
            act_e.wait_ge(top_diff, 1)
            activation(rt[:, :, 4, 0], rt[:, :, 3, 0], ACT.Exp).then_inc(top_exp, 1)

            def gathered(n):
                for k in range(2):
                    act_e.wait_ge(xe_gained, 2 * n + (k - 1))
                    activation(xeT_hi[:, 4 * k:4 * k + 4, :], bank(6 + k).rearrange("p (dc s) -> p dc s", dc=4),
                               ACT.Copy).then_inc(xeT_hi_ready, 1)

            def expert(it):
                at = Pass(it)

                def finish():
                    act_e.wait_ge(pgT_ps, it + 1)
                    activation(pick_gateT[:, :, :].rearrange("p c t -> p (c t)"), bank(3)[:, 0:TC * P],
                               ACT.Copy).then_inc(pgT_sb, 1)
                    act_e.wait_ge(part_used, at.parts(MIX_PARTS))
                    for k in range(2):
                        activation(ye[:, k * HALF:(k + 1) * HALF], bank(4 + k), ACT.Copy).then_inc(ye_sb, 1)

                mixer_pass(at, finish)
                gathered(it + 2)

            gathered(1)
            with act_e.Fori(0, E) as it:
                expert(it)
            act_e.wait_ge(routed, 1)
            n_pass = act_e.value_load(passes_i[0:1, 0:1], min_val=1, max_val=2)
            with act_e.If(n_pass > 1):
                with act_e.Fori(E, 2 * E) as it:
                    expert(it)
            for c in range(TC):
                act_e.wait_ge(scat_add, n_pass * (4 * E))
                activation(xn[:, c, :], x_res[:, c, :], ACT.Square,
                           accum_out=small[:, 8 + c:9 + c]).then_inc(sq_done, 1)
            root(small[:, 8:8 + TC])

        @block.vector
        def _(dve):
            n_step = [0]

            def step(ins):
                n_step[0] += 1
                ins.then_inc(dve_step, 1)
                dve.wait_ge(dve_step, n_step[0])

            tt, ts, stt = dve.tensor_tensor, dve.tensor_scalar, dve.scalar_tensor_tensor
            mul, add, sub = ALU.mult, ALU.add, ALU.subtract
            n_rms = [0]

            def inverse_mean(ms, width):
                step(ts(ms, ms, 1.0 / width, EPS, mul, add))
                dve.reciprocal(ms, ms).then_inc(ms_ready, 1)
                n_rms[0] += 1
                dve.wait_ge(rms_ready, n_rms[0])


            dve.wait_ge(prep_in, 48)
            dve.wait_ge(act_prep, 1)
            ar = a_raw[:, 0, :, :]
            ai = a_raw[:, 1, :, :]
            arf, aif = (z.rearrange("p h s -> p (h s)") for z in (ar, ai))
            dtb = dt_[:, :].unsqueeze(2).to_broadcast([PAIRS, 2, ST])
            w = lambda k: prep[:, k, :]
            w3 = lambda k: prep[:, k, :].rearrange("p (h s) -> p h s", h=2)
            step(tt(w3(0), ar, dtb, mul))
            step(tt(w3(2), ai, dtb, mul))
            step(ts(w(5), w(2), 1.0 / (2.0 * math.pi), 12582912.0, mul, add))
            step(ts(w(5), w(5), -12582912.0, None, add))
            c1, c2 = 6.28125, 0.0019340515136718750
            c3 = 2.0 * math.pi - c1 - c2
            for part in (c1, c2, c3):
                step(stt(w(2), w(5), -part, w(2), mul, add))
            step(ts(w(2), w(2), 3.1415925, -3.1415925, ALU.min, ALU.max))
            step(tt(w(6), arf, arf, mul))
            step(tt(w(7), aif, aif, mul))
            tt(w(6), w(6), w(7), add).then_inc(dve_prep, 1)
            dve.wait_ge(dve_prep, 1)
            step(dve.reciprocal(w(6), w(6)))
            dve.wait_ge(act_prep, 4)
            step(tt(w(3), w(3), w(3), mul))
            step(ts(w(3), w(3), -2.0, 1.0, mul, add))
            step(tt(w(8), w(1), w(3), mul))
            step(tt(w(9), w(1), w(4), mul))
            step(ts(w(7), w(8), -1.0, None, add))
            step(tt(w(10), w(7), arf, mul))
            step(tt(w(12), w(9), aif, mul))
            step(tt(w(10), w(10), w(12), add))
            step(tt(w(10), w(10), w(6), mul))
            step(tt(w(11), w(9), arf, mul))
            step(tt(w(12), w(7), aif, mul))
            step(tt(w(11), w(11), w(12), sub))
            tt(w(11), w(11), w(6), mul).then_inc(coef_ready, 1)
            dve.wait_ge(pe_prep, 3)
            step(dve.tensor_copy(gain[:, :, :].rearrange("p k c -> p (k c)"), bank(7)[:, 0:3 * DC]))
            step(dve.tensor_copy(coef4[:, :, :].rearrange("p k i -> p (k i)"), bank(6)[:, 0:4 * PAIRS]))
            dve.memset(pw[:, 0, 0, :], 1.0)
            dve.memset(pw[:, 1, 0, :], 0.0)
            step(dve.tensor_copy(pw[:, :, 1, :], coef4[:, 0:2, :]))
            for n in (1, 2, 4):
                lo, hi = slice(1, n + 1), slice(n + 1, 2 * n + 1)
                t = tmp_v[:, 0:n * PAIRS].rearrange("p (k i) -> p k i", k=n)
                by = lambda r: pw[:, r, n:n + 1, :].to_broadcast([P, n, PAIRS])
                step(tt(pw[:, 0, hi, :], pw[:, 0, lo, :], by(0), mul))
                step(tt(t, pw[:, 1, lo, :], by(1), mul))
                step(tt(pw[:, 0, hi, :], pw[:, 0, hi, :], t, sub))
                step(tt(pw[:, 1, hi, :], pw[:, 0, lo, :], by(1), mul))
                step(tt(t, pw[:, 1, lo, :], by(0), mul))
                step(tt(pw[:, 1, hi, :], pw[:, 1, hi, :], t, add))
            for s in range(CH):
                dve.tensor_copy(pr[:, :, s, :], pw[:, :, CH - 1 - s, :])
            for o in range(2):
                dve.tensor_copy(carry[:, o, o, :], pw[:, 0, CH, :])
            dve.tensor_copy(carry[:, 1, 0, :], pw[:, 1, CH, :])
            step(ts(carry[:, 0, 1, :], pw[:, 1, CH, :], -1.0, None, mul))
            dve.wait_ge(b_in, 64)
            cf = lambda r: coef4[:, 2 + r, :].unsqueeze(2).to_broadcast([P, PAIRS, C])
            t = tmp_v[:, 0:PAIRS * C].rearrange("p (i c) -> p i c", i=PAIRS)
            step(tt(bb[:, 0, :, :], b_raw[:, 0, :, :], cf(0), mul))
            step(tt(t, b_raw[:, 1, :, :], cf(1), mul))
            step(tt(bb[:, 0, :, :], bb[:, 0, :, :], t, sub))
            step(tt(bb[:, 1, :, :], b_raw[:, 1, :, :], cf(0), mul))
            step(tt(t, b_raw[:, 0, :, :], cf(1), mul))
            tt(bb[:, 1, :, :], bb[:, 1, :, :], t, add).then_inc(dve_prep, 1)
            dve.wait_ge(dve_prep, 2)

            dve.wait_ge(sq_done, CH)
            dve.wait_ge(bc_in, 32)
            inverse_mean(small[0:NCH, 0:CH], D)
            for s in range(CH):
                ins = stt(h32[:, :, s, :], x32[:, s, :].rearrange("n (g c) -> n g c", g=G), small[0:NCH, s:s + 1],
                          bc32[:, 0, :].rearrange("n (g c) -> n g c", g=G), mul, mul)
            ins.then_inc(h_ready, 1)
            dve.wait_ge(h_ready, 1)

            t = tmp_v[:, 0:QP * CH * C].rearrange("p (i s c) -> p i s c", i=QP, s=CH)
            for q in range(ROUNDS):
                if q >= 1:
                    dve.wait_ge(bt_ps, 4 * q)
                i = slice(q * QP, (q + 1) * QP)
                b_of = lambda r: bb[:, r, i, :].unsqueeze(2).to_broadcast([P, QP, CH, C])
                p_of = lambda r: pr[:, r, :, i].rearrange("p s i -> p i s").unsqueeze(3).to_broadcast([P, QP, CH, C])
                step(tt(bp[:, 0, :, :, :], b_of(0), p_of(0), mul))
                step(tt(t, b_of(1), p_of(1), mul))
                tt(bp[:, 0, :, :, :], bp[:, 0, :, :, :], t, sub).then_inc(bp_re, 1)
                dve.wait_ge(bp_re, q + 1)

            dve.wait_ge(act_prep, 6)

            def out_powers(q):
                t9 = tmp_v[:, :].rearrange("p (i k c) -> p i k c", i=QP, k=KP)
                i = slice(q * QP, (q + 1) * QP)
                c_of = lambda r: c_q[:, r, i, :].unsqueeze(2).to_broadcast([P, QP, KP, C])
                p_of = lambda r: pw[:, r, :, i].rearrange("p k i -> p i k").unsqueeze(3).to_broadcast([P, QP, KP, C])
                g = gk[:, q % 2, 0, :, :, :]
                step(tt(g, c_of(0), p_of(0), mul))
                step(tt(t9, c_of(1), p_of(1), mul))
                tt(g, g, t9, sub).then_inc(gk_re, 1)
                dve.wait_ge(gk_re, q + 1)

            out_powers(0)
            out_powers(1)
            dve.memset(state[:, :, :, 0], 0.0)
            dve.wait_ge(xin_sb, 4 * ROUNDS)
            step(dve.tensor_copy(state[:, :, :, 1], xin[:, :, :, 0]))
            prod = tmp_v[:, 0:4 * PAIRS].rearrange("p (o r i) -> p o r i", o=2, r=2)
            for n in range(1, NCH - 1):
                s_n = state[:, :, :, n].unsqueeze(1).to_broadcast([P, 2, 2, PAIRS])
                step(tt(prod, carry[:, :, :, :], s_n, mul))
                step(tt(prod[:, :, 0, :], prod[:, :, 0, :], prod[:, :, 1, :], add))
                ins = tt(state[:, :, :, n + 1], prod[:, :, 0, :], xin[:, :, :, n], add)
                if n < NCH - 2:
                    step(ins)
            ins.then_inc(state_ready, 1)
            def lo_of_output(q):
                dve.wait_ge(hi_sides, 2 * (q + 1))
                for k in range(2):
                    o = lambda z: z[:, q + 4 * k, :].rearrange("p (n t) -> p t n", t=CH)
                    tt(o(hT_lo), bank(6 + q % 2)[:, k * SEQ:(k + 1) * SEQ].rearrange("p (t n) -> p t n", t=CH),
                       o(hT_hi).bitcast(F32), sub).then_inc(lo_sides, 1)

            dve.wait_ge(hd_ready, 1)
            for q in range(ROUNDS):
                for b in range(4):
                    half, k = divmod(b, 2)
                    g = half * PAIRS + q * QP + 4 * k
                    dve.wait_ge(y_ps, 4 * q + b + 1)
                    if q >= 1:
                        dve.wait_ge(yT_ps, q)
                    tt(y32[:, :, half, 4 * k * C:4 * (k + 1) * C].rearrange("n t (g c) -> n g t c", g=4),
                       h32[:, g:g + 4, :, :], bank(b)[0:NCH, :].rearrange("n (g t c) -> n g t c", g=4, t=CH),
                       add).then_inc(y_sb, 1)
                if q + 2 < ROUNDS:
                    out_powers(q + 2)
                if q >= 1:
                    lo_of_output(q - 1)
            lo_of_output(ROUNDS - 1)
            for p in range(PART_SLOTS):
                split_lo(dve, Before, p)
            dve.wait_ge(xres_in, 16)
            for n in range(GLU_BLOCKS):
                for p in range(4):
                    if p == 3:
                        for c in range(TC):
                            u = TC * n + c
                            dve.wait_ge(glu_sig, u + 1)
                            step(tt(gate[:, c, :], gate[:, c, :], bank(2 * (n % 2) + c)[:, 0:FH], mul))
                            tt(x_res[:, c, n * FH:(n + 1) * FH], x_res[:, c, n * FH:(n + 1) * FH], gate[:, c, :],
                               add).then_inc(glu_add, 1)
                    split_lo(dve, Before, 4 * n + p + PART_SLOTS)

            n_norm = [0]
            n_side = [2 * ROUNDS]

            def lo_of_side(o, full, rounded):
                n_side[0] += 1
                dve.wait_ge(hi_sides, n_side[0])
                tt(o, full, rounded.bitcast(F32), sub).then_inc(lo_sides, 1)

            def mixer_pass(at, between):
                for j in range(J + 1):
                    if j < J:
                        for p in range(w_part(j), w_part(j) + 4):
                            if p == w_part(j) + 3:
                                for c in range(at.nb):
                                    dve.wait_ge(silu_done, at.items(at.nb * j + c + 1))
                                    tt(act[:, c, :], gate[:, c, :], bank(c)[:, FH:2 * FH], mul).then_inc(act_ready, 1)
                            if not at.is_down(p + PART_SLOTS):
                                split_lo(dve, at, p + PART_SLOTS)
                    if j >= 1:
                        for p in range(d_part(j - 1), d_part(j - 1) + 2):
                            if not at.is_down(p + PART_SLOTS):
                                split_lo(dve, at, p + PART_SLOTS)
                    if j < J:
                        for c in range(at.nb):
                            dve.wait_ge(actT_hi_ready, at.items(at.nb * j + c + 1))
                            tt(actT_lo[:, c, :], bank(2 + c)[:, 0:2 * P], actT_hi[:, c, :].bitcast(F32),
                               sub).then_inc(actT_lo_ready, 1)
                        between(j)

            def norm():
                k = n_norm[0]
                dve.wait_ge(sq_done, CH + TC * (k + 1))
                inverse_mean(small[:, 8:8 + TC], D)
                for c in range(TC):
                    ts(xn[:, c, :], x_res[:, c, :], small[:, 8 + c:9 + c], None, mul).then_inc(xn_ready, 1)
                for c in range(TC):
                    dve.wait_ge(hT_ps, TC * k + c + 1)
                    for half in range(2):
                        o = bank(4 * c + half).rearrange("p (dc t) -> p dc t", dc=4)
                        tt(o, o, gain[:, k, 4 * half:4 * half + 4].unsqueeze(2).to_broadcast([P, 4, P]),
                           mul).then_inc(hT_gained, 1)
                for c in range(TC):
                    for half in range(2):
                        lo_of_side(hT_lo[:, 4 * half:4 * half + 4, c * P:(c + 1) * P],
                                   bank(4 * c + half).rearrange("p (dc t) -> p dc t", dc=4),
                                   hT_hi[:, 4 * half:4 * half + 4, c * P:(c + 1) * P])
                n_norm[0] += 1

            norm()
            def lambda_products(j):
                if j == 4:
                    dve.wait_ge(table_in, 96)
                    for k in range(2):
                        step(tt(sqscr[:, k, 0:HD], lam_in[:, 2 * k, :], lam_in[:, 2 * k + 1, :], mul))
                    dve.tensor_reduce(lam[:, 0:2], sqscr[:, :, 0:HD], AX.X, add).then_inc(lam_ready, 1)

            mixer_pass(Pass(), lambda_products)
            for c in range(TC):
                dve.wait_ge(part_used, 2 * FIRST_QKV)
                for k in range(2):
                    o = x_res[:, c, k * HALF:(k + 1) * HALF]
                    tt(o, o, bank(4 + 2 * c + k), add).then_inc(ffn_add, 1)
            norm()
            dve.wait_ge(lam_ready, 2)
            step(tt(lam[:, 4:5], lam[:, 3:4], lam[:, 2:3], sub))
            step(ts(lam[:, 4:5], lam[:, 4:5], -LAMBDA_INIT, None, add))
            ts(sub_gain[:, :], sub_gain[:, :], 1.0 - LAMBDA_INIT, None, mul).then_inc(lam_ready, 1)
            for n in range(4 * QKV_BLOCKS):
                split_lo(dve, Before, 2 * FIRST_QKV + PART_SLOTS + n)
            dve.wait_ge(bias_in, 16)

            def scores(h):
                if h >= 2:
                    dve.wait_ge(probs_ready, h - 1)
                dve.wait_ge(sc_ps, h + 1)
                s = sc[:, h % 2, :, :]
                scores_ps = bank(2 * (h % 2), 2).rearrange("p (m k) -> p m k", m=2)[:, :, 0:3 * P]
                tt(s[:, :, 0:P], scores_ps[:, :, 0:P], bias[:, h, P:2 * P].unsqueeze(1).to_broadcast([P, 2, P]), add)
                tt(s[:, :, P:3 * P], scores_ps[:, :, P:3 * P], bias[:, h, :].unsqueeze(1).to_broadcast([P, 2, 2 * P]),
                   add).then_inc(sc_sb, 1)
                dve.wait_ge(sc_sb, h + 1)
                if h >= 2:
                    dve.wait_ge(o_sb, h - 1)
                st = asm[:, h % 2, :]
                dve.tensor_reduce(st[:, 0:2], s[:, :, 0:P], AX.X, ALU.max)
                step(dve.tensor_reduce(st[:, 2:4], s[:, :, P:3 * P], AX.X, ALU.max))
                ts(st[:, 0:4], st[:, 0:4], -1.0, None, mul).then_inc(max_done, 1)

            def combine(h):
                st = asm[:, h % 2, :]
                dve.wait_ge(exp_done, 4 * (h + 1))
                step(dve.reciprocal(st[:, 8:12], st[:, 4:8]))
                step(ts(st[:, 9:12:2], st[:, 9:12:2], lam[:, 4:5], None, mul))
                if h >= 2:
                    dve.wait_ge(pT_ps, h - 1)
                for qb in range(2):
                    cols = slice(0, P) if qb == 0 else slice(P, 3 * P)
                    step(ts(probs[:, h % 2, cols], sc[:, h % 2, 0, cols], st[:, 8 + 2 * qb:9 + 2 * qb], None, mul))
                    ins = stt(probs[:, h % 2, cols], sc[:, h % 2, 1, cols], st[:, 9 + 2 * qb:10 + 2 * qb],
                              probs[:, h % 2, cols], mul, add)
                ins.then_inc(probs_ready, 1)

            def head_out(h):
                dve.wait_ge(osq_done, 2 * (h + 1))
                dve.tensor_copy(qT[:, h, :], bank(6 + h % 2)[:, 0:2 * P]).then_inc(o_sb, 1)

            scores(0)
            for h in range(H):
                if h + 1 < H:
                    if h >= 1:
                        head_out(h - 1)
                    scores(h + 1)
                combine(h)
            head_out(H - 2)
            head_out(H - 1)
            inverse_mean(osq[:, :, :].rearrange("p c h -> p (c h)"), 2 * HD)
            dve.wait_ge(o_sb, H)
            for c in range(TC):
                o = qT[:, :, c * P:(c + 1) * P]
                tt(o, o, osq[:, c, :].unsqueeze(2).to_broadcast([P, H, P]), mul).then_inc(o_scaled, 1)
            for u in range(4):
                c, k = divmod(u, 2)
                lo_of_side(hT_lo[:, 4 * k:4 * k + 4, c * P:(c + 1) * P], bank(u).rearrange("p (dc t) -> p dc t", dc=4),
                           hT_hi[:, 4 * k:4 * k + 4, c * P:(c + 1) * P])
            for n in range(WO_BLOCKS):
                for p in range(4):
                    split_lo(dve, Before, 2 * FIRST_WO + 4 * n + p + PART_SLOTS)
                for c in range(TC):
                    o = x_res[:, c, n * BANK:(n + 1) * BANK]
                    tt(o, o, bank(4 + n * TC + c), add).then_inc(wo_add, 1)
            norm()

            dve.wait_ge(logit_ps, 1)
            logit, top, first, second, sel, comb = (rt[:, :, k, :] for k in (0, 1, 5, 6, 7, 8))
            step(dve.tensor_copy(logit, bank(6)[:, 0:TC * E].rearrange("p (c e) -> p c e", c=TC)))
            for c in range(TC):
                step(dve.max(rt[:, c, 1, :], rt[:, c, 0, :]))
                step(dve.max_index(top_i[:, c, :], rt[:, c, 1, :], rt[:, c, 0, :]))
                step(dve.tensor_copy(rt[:, c, 2, :], top_i[:, c, :]))
                for k, o in enumerate((5, 6)):
                    step(ts(rt[:, c, o, :], slot_no[:, 0:E], rt[:, c, 2, k:k + 1], None, ALU.is_equal))
            tt(rt[:, :, 3, 0], rt[:, :, 1, 1], rt[:, :, 1, 0], sub).then_inc(top_diff, 1)
            tt(sel, first, second, add).then_inc(sel_ready, 1)
            dve.wait_ge(top_exp, 1)
            step(ts(rt[:, :, 4, 1], rt[:, :, 4, 0], 1.0, None, add))
            step(dve.reciprocal(rt[:, :, 4, 2], rt[:, :, 4, 1]))
            step(tt(rt[:, :, 4, 3], rt[:, :, 4, 0], rt[:, :, 4, 2], mul))
            step(tt(comb, first, rt[:, :, 4, 2:3].to_broadcast([P, TC, E]), mul))
            step(tt(second, second, rt[:, :, 4, 3:4].to_broadcast([P, TC, E]), mul))
            step(tt(comb, comb, second, add))
            dve.memset(gates[:, :, 2 * E:2 * E + 1], 0.0)
            dve.tensor_copy(gates[:, :, 0:E], comb)
            dve.tensor_copy(gates[:, :, E:2 * E], comb)
            dve.wait_ge(cnt_ps, 1)
            dve.memset(key[:, :, 2 * E:2 * E + 1], -1.0)
            step(tt(key[:, :, 0:E], bank(7)[:, 0:TC * E].rearrange("p (c e) -> p c e", c=TC), sel, mul))
            step(ts(key[:, :, 0:E], key[:, :, 0:E], -1.0, None, add))
            dve.tensor_scalar(key[:, :, E:2 * E], key[:, :, 0:E], -float(P), None, add)
            step(dve.tensor_reduce(passes[:, 0:1], bank(7)[:, TC * E:(TC + 1) * E], AX.X, ALU.max))
            step(ts(passes[:, 1:2], passes[:, 0:1], float(P), 1.0, ALU.is_gt, add))
            dve.tensor_copy(passes_i[:, :], passes[:, 1:2]).then_inc(routed, 1)

            def pick_tokens(it):
                for c in range(TC):
                    ts(pick[:, c, :], slot_no[:, :], key[:, c, bass.ds(it, 1)], None, ALU.is_equal).then_inc(pick_ready, 1)

            def gathered(n):
                for k in range(2):
                    dve.wait_ge(gather_ps, 2 * n + (k - 1))
                    o = bank(6 + k).rearrange("p (dc s) -> p dc s", dc=4)
                    tt(o, o, gain[:, 2, 4 * k:4 * k + 4].unsqueeze(2).to_broadcast([P, 4, P]), mul).then_inc(xe_gained, 1)
                for k in range(2):
                    dve.wait_ge(xeT_hi_ready, 2 * n + (k - 1))
                    tt(xeT_lo[:, 4 * k:4 * k + 4, :], bank(6 + k).rearrange("p (dc s) -> p dc s", dc=4),
                       xeT_hi[:, 4 * k:4 * k + 4, :].bitcast(F32), sub).then_inc(xeT_lo_ready, 1)

            def expert(it):
                def picks(j):
                    if j == 4:
                        for c in range(TC):
                            ts(pick_gate[:, c, :], slot_no[:, :], key[:, c, bass.ds(it, 1)],
                               gates[:, c, bass.ds(it, 1)], ALU.is_equal, mul).then_inc(gate_pick_ready, 1)
                        pick_tokens(it + 1)

                mixer_pass(Pass(it), picks)
                gathered(it + 2)
                for u, b in enumerate(SCATTER_BANKS):
                    c, k = divmod(u, 2)
                    o = x_res[:, c, k * HALF:(k + 1) * HALF]
                    dve.wait_ge(scat_ps, it * 4 + (u + 1))
                    tt(o, o, bank(b), add).then_inc(scat_add, 1)
                dve.wait_ge(scat_add, it * 4 + 4)

            pick_tokens(0)
            gathered(1)
            with dve.Fori(0, E) as it:
                expert(it)
            n_pass = dve.value_load(passes_i[0:1, 0:1], min_val=1, max_val=2)
            with dve.If(n_pass > 1):
                with dve.Fori(E, 2 * E) as it:
                    expert(it)
            dve.wait_ge(const_in, 16)
            dve.wait_ge(sq_done, CH + TC * 4)
            inverse_mean(small[:, 8:8 + TC], D)
            for c in range(TC):
                stt(xn[:, c, :], x_res[:, c, :], small[:, 8 + c:9 + c], final_gain[:, :], mul, mul).then_inc(final_ready, 1)

        @block.tensor
        def _(pe):
            mm = pe.matmul

            def transpose(o, i, n=P):
                return pe.transpose(o, i, ident[0:n, 0:n])

            pe.wait_ge(pool_const, CONSTS)
            pe.wait_ge(c_in, 64)
            for r in range(2):
                for k in range(4):
                    ins = transpose(bank(4 + r)[:, k * P:(k + 1) * P], c_raw[:, r, k, :, :].rearrange("p h s -> p (h s)"))
            ins.then_inc(pe_prep, 1)
            pe.wait_ge(coef_ready, 1)
            for k in range(4):
                ins = transpose(bank(6)[:, k * PAIRS:(k + 1) * PAIRS], prep[:, 8 + k, :], PAIRS)
            ins.then_inc(pe_prep, 1)
            pe.wait_ge(gain_in, 48)
            transpose(bank(7)[:, 0:3 * DC], gain_rows[:, :], 3 * DC).then_inc(pe_prep, 1)
            pe.wait_ge(h_ready, 1)
            for g in range(G):
                b, k = divmod(g, C)
                ins = transpose(bank(b)[:, k * NCH:(k + 1) * NCH], h32[:, g, :, :].rearrange("n s c -> n (s c)"), NCH)
                if k == C - 1:
                    ins.then_inc(u_ps, 1)
            for q in range(ROUNDS):
                pe.wait_ge(bp_re, q + 1)
                pe.wait_ge(bp_im, q + 1)
                for b in range(4):
                    if q == 0:
                        pe.wait_ge(u_sb, b + 1)
                    else:
                        pe.wait_ge(bt_sb, 4 * (q - 1) + b + 1)
                    for k in range(4):
                        r, i = divmod(4 * b + k, QP)
                        ins = transpose(bank(b)[:, k * P:(k + 1) * P], bp[:, r, i, :, :].rearrange("p s c -> p (s c)"))
                    ins.then_inc(bt_ps, 1)
                pe.wait_ge(bt_sb, 4 * (q + 1))
                if q == 0:
                    pe.wait_ge(act_prep, 6)
                else:
                    pe.wait_ge(xin_sb, 4 * q)
                for r in range(2):
                    for i in range(QP):
                        g = q * QP + i
                        at = (r * QP + i) * 2 * NCH
                        ins = mm(bank(4, 2)[:, at:at + 2 * NCH], bt[:, r, i, :], uT[:, g::PAIRS, :],
                                 start=True, stop=True)
                ins.then_inc(xin_ps, 1)

            def groups(q):
                for b in range(4):
                    half, k = divmod(b, 2)
                    yield b, [(half, 4 * k + n) for n in range(4)]

            def impulse(q):
                pe.wait_ge(gk_re, q + 1)
                pe.wait_ge(gk_im, q + 1)
                if q == 0:
                    pe.wait_ge(xin_sb, 4 * ROUNDS)
                for b, members in groups(q):
                    if 4 * q + b >= 2:
                        pe.wait_ge(kern_sb, 4 * q + b - 1)
                    for n, (half, i) in enumerate(members):
                        part = slice(half * ST, (half + 1) * ST)
                        for r in range(2):
                            ins = mm(bank(4 + b % 2)[0:C, n * P:(n + 1) * P], bb[part, r, q * QP + i, :],
                                     gk[part, q % 2, r, i, 0:CH, :], start=(r == 0), stop=(r == 1))
                    ins.then_inc(kern_ps, 1)

            def mixer_out(q):
                pe.wait_ge(toep_in, 16 * CH * (q + 1))
                for b, members in groups(q):
                    if q >= 1:
                        pe.wait_ge(y_sb, 4 * (q - 1) + b + 1)
                    for n, (half, i) in enumerate(members):
                        part = slice(half * ST, (half + 1) * ST)
                        o = bank(b)[0:NCH, n * P:(n + 1) * P]
                        mm(o, uT[:, half * PAIRS + q * QP + i, :], toep[:, q % 2, 4 * b + n, :],
                           start=True, stop=False)
                        for r in range(2):
                            ins = mm(o, state[part, r, q * QP + i, :], gk[part, q % 2, r, i, 1:KP, :],
                                     start=False, stop=(r == 1))
                    ins.then_inc(y_ps, 1)

            def mixer_out_T(q):
                pe.wait_ge(y_sb, 4 * (q + 1))
                if q >= 2:
                    pe.wait_ge(lo_sides, 2 * (q - 1))
                for half in range(2):
                    for s in range(CH):
                        ins = transpose(bank(6 + q % 2)[:, half * SEQ + s * NCH:half * SEQ + (s + 1) * NCH],
                                        y32[:, s, half, :], NCH)
                ins.then_inc(yT_ps, 1)

            impulse(0)
            impulse(1)
            pe.wait_ge(state_ready, 1)
            mixer_out(0)
            for q in range(1, ROUNDS):
                if q + 1 < ROUNDS:
                    impulse(q + 1)
                mixer_out_T(q - 1)
                mixer_out(q)
            mixer_out_T(ROUNDS - 1)
            def part_ready(at, p):
                if at.is_down(p):
                    pe.wait_ge(lo_down, at.down(p + 1))
                else:
                    pe.wait_ge(lo_wide, at.wide(p + 1))
                return hi[at.slot(p)], lo[at.slot(p)]

            def split_mm(o, left, right, first, last):
                mm(o, left[0], right[0], start=first, stop=False)
                mm(o, left[0], right[1], start=False, stop=False)
                return mm(o, left[1], right[0], start=False, stop=last)

            def both(z, *index):
                return tuple(k[index] for k in z)

            hT = (hT_hi, hT_lo)
            every = slice(None)

            def token_blocks(at, p0, outs, side):
                for p in range(4):
                    w = part_ready(at, p0 + p)
                    for d in range(2):
                        dc = 2 * p + d
                        for c, o in enumerate(outs):
                            ins = split_mm(o, side(dc, c), both(w, every, slice(d * BANK, (d + 1) * BANK)),
                                           dc == 0, dc == DC - 1)
                    ins.then_inc(part_used, 1)

            def hT_block(dc, c):
                return both(hT, every, dc, slice(c * P, (c + 1) * P))

            pe.wait_ge(lo_sides, 2 * ROUNDS)
            for n in range(GLU_BLOCKS):
                if n >= 2:
                    pe.wait_ge(glu_add, TC * (n - 1))
                token_blocks(Before, 4 * n, [bank(2 * (n % 2) + c) for c in range(TC)], hT_block)

            n_norm = [0]

            def norm_transposes():
                k = n_norm[0]
                for c in range(TC):
                    pe.wait_ge(xn_ready, TC * k + c + 1)
                    for dc in range(DC):
                        ins = transpose(bank(4 * c, 2)[:, dc * P:(dc + 1) * P], xn[:, c, dc * P:(dc + 1) * P])
                    ins.then_inc(hT_ps, 1)
                n_norm[0] += 1

            def mixer_pass(at, side, finish):
                for j in range(J + 1):
                    if j < J:
                        token_blocks(at, w_part(j), [bank(c) for c in range(at.nb)], side)
                    if j == J:
                        finish()
                    if j >= 1:
                        pe.wait_ge(actT_hi_ready, at.items(at.nb * j))
                        pe.wait_ge(actT_lo_ready, at.items(at.nb * j))
                        for f in range(2):
                            w = part_ready(at, d_part(j - 1) + f)
                            for c in range(at.nb):
                                a = both((actT_hi, actT_lo), every, c, slice(f * P, (f + 1) * P))
                                for k in range(2):
                                    ins = split_mm(bank(4 + 2 * c + k), a,
                                                   both(w, every, slice(k * HALF, (k + 1) * HALF)),
                                                   j == 1 and f == 0, j == J and f == 1)
                            ins.then_inc(part_used, 1)
                    if j < J:
                        for c in range(at.nb):
                            pe.wait_ge(act_ready, at.items(at.nb * j + c + 1))
                            for f in range(2):
                                ins = transpose(bank(2 + c)[:, f * P:(f + 1) * P], act[:, c, f * P:(f + 1) * P])
                            ins.then_inc(actT_ps, 1)

            norm_transposes()
            pe.wait_ge(lo_sides, 2 * ROUNDS + 4)
            mixer_pass(Pass(), hT_block, lambda: None)
            pe.wait_ge(ffn_add, 4)
            norm_transposes()
            pe.wait_ge(lo_sides, 2 * ROUNDS + 8)
            for n in range(QKV_BLOCKS):
                if n >= 2:
                    pe.wait_ge(qkv_sb, 4 * (n - 1))
                p0 = 2 * FIRST_QKV + 4 * n
                b0 = 4 * (n % 2)
                if n >= 4:
                    token_blocks(Before, p0, [bank(b0 + c) for c in range(TC)], hT_block)
                    continue
                for p in range(4):
                    w = part_ready(Before, p0 + p)
                    for d in range(2):
                        dc = 2 * p + d
                        for m in range(4):
                            at_m = d * BANK + m * P
                            ins = split_mm(bank(b0 + m)[:, 0:SEQ], both(w, every, slice(at_m, at_m + P)),
                                           both(hT, every, dc), dc == 0, dc == DC - 1)
                    ins.then_inc(part_used, 1)

            def score_products(h):
                if h == 0:
                    pe.wait_ge(qkv_sb, 4 * 4 + 2 * TC)
                if h >= 2:
                    pe.wait_ge(sc_sb, h - 1)
                for m in range(2):
                    part = slice(m * HD, (m + 1) * HD)
                    o = bank(2 * (h % 2) + m)
                    mm(o[:, 0:P], qT[part, h, 0:P], kT[part, h, 0:P], start=True, stop=True)
                    ins = mm(o[:, P:3 * P], qT[part, h, P:2 * P], kT[part, h, :], start=True, stop=True)
                ins.then_inc(sc_ps, 1)

            score_products(0)
            for h in range(H):
                if h + 1 < H:
                    score_products(h + 1)
                pe.wait_ge(probs_ready, h + 1)
                if h >= 2:
                    pe.wait_ge(pT_sb, h - 1)
                for k in range(3):
                    ins = transpose(bank(4 + h % 2)[:, k * P:(k + 1) * P], probs[:, h % 2, k * P:(k + 1) * P])
                ins.then_inc(pT_ps, 1)
                pe.wait_ge(pT_sb, h + 1)
                if h >= 2:
                    pe.wait_ge(o_sb, h - 1)
                o = bank(6 + h % 2)
                head = slice(h * P, (h + 1) * P)
                mm(o[:, 0:P], pT[:, h % 2, 0:P], v[:, 0, head], start=True, stop=True)
                mm(o[:, P:2 * P], pT[:, h % 2, P:2 * P], v[:, 0, head], start=True, stop=False)
                mm(o[:, P:2 * P], pT[:, h % 2, 2 * P:3 * P], v[:, 1, head], start=False, stop=True).then_inc(o_ps, 1)
            pe.wait_ge(o_scaled, TC)
            for u in range(4):
                c, k = divmod(u, 2)
                for n in range(4):
                    ins = transpose(bank(u)[:, n * P:(n + 1) * P], qT[:, 4 * k + n, c * P:(c + 1) * P])
                ins.then_inc(oT_ps, 1)
            pe.wait_ge(lo_sides, 2 * ROUNDS + 12)
            for n in range(WO_BLOCKS):
                token_blocks(Before, 2 * FIRST_WO + 4 * n, [bank(4 + n * TC + c) for c in range(TC)], hT_block)
            pe.wait_ge(wo_add, 4)
            norm_transposes()
            pe.wait_ge(lo_sides, 2 * ROUNDS + 16)
            pe.wait_ge(router_in, 16)
            for c in range(TC):
                for dc in range(DC):
                    for k in range(2):
                        ins = mm(bank(6)[:, c * E:(c + 1) * E], hT_block(dc, c)[k].bitcast(F32), router[:, dc, :],
                                 start=(dc == 0 and k == 0), stop=(dc == DC - 1 and k == 1))
            ins.then_inc(logit_ps, 1)
            pe.wait_ge(sel_ready, 1)
            counts = bank(7)
            mm(counts[:, 0:E], upto[:, :], rt[:, 0, 7, :], start=True, stop=True)
            mm(counts[:, E:2 * E], ones[:, :], rt[:, 0, 7, :], start=True, stop=False)
            mm(counts[:, E:2 * E], upto[:, :], rt[:, 1, 7, :], start=False, stop=True)
            mm(counts[:, 2 * E:3 * E], ones[:, :], rt[:, 0, 7, :], start=True, stop=False)
            mm(counts[:, 2 * E:3 * E], ones[:, :], rt[:, 1, 7, :], start=False, stop=True).then_inc(cnt_ps, 1)

            def gather(n_pick):
                pe.wait_ge(pick_ready, n_pick)
                for dc in range(DC):
                    for c in range(TC):
                        ins = mm(bank(6, 2)[:, dc * P:(dc + 1) * P], xn[:, c, dc * P:(dc + 1) * P], pick[:, c, :],
                                 start=(c == 0), stop=(c == TC - 1))
                    if dc % 4 == 3:
                        ins.then_inc(gather_ps, 1)

            def expert(it):
                def finish():
                    pe.wait_ge(gate_pick_ready, it * TC + TC)
                    for c in range(TC):
                        ins = transpose(bank(3)[:, c * P:(c + 1) * P], pick_gate[:, c, :])
                    ins.then_inc(pgT_ps, 1)

                pe.wait_ge(xeT_hi_ready, it * 2 + 2)
                pe.wait_ge(xeT_lo_ready, it * 2 + 2)
                mixer_pass(Pass(it), lambda dc, c: both((xeT_hi, xeT_lo), every, dc), finish)
                gather(it * TC + 2 * TC)
                pe.wait_ge(pgT_sb, it + 1)
                pe.wait_ge(ye_sb, it * 2 + 2)
                for u, b in enumerate(SCATTER_BANKS):
                    c, k = divmod(u, 2)
                    mm(bank(b), pick_gateT[:, c, :], ye[:, k * HALF:(k + 1) * HALF],
                       start=True, stop=True).then_inc(scat_ps, 1)
                pe.wait_ge(scat_add, it * 4 + 4)

            gather(TC)
            with pe.Fori(0, E) as it:
                expert(it)
            pe.wait_ge(routed, 1)
            n_pass = pe.value_load(passes_i[0:1, 0:1], min_val=1, max_val=2)
            with pe.If(n_pass > 1):
                with pe.Fori(E, 2 * E) as it:
                    expert(it)


_INS = ["x", "norm_mix_g", "norm_ffn_g", "final_norm_g", "ssm_a_re", "ssm_a_im", "ssm_log_dt", "ssm_b_re",
        "ssm_b_im", "ssm_c_re", "ssm_c_im", "ssm_d", "ssm_w_glu", "attn_w_qkv", "attn_lambda_q1",
        "attn_lambda_k1", "attn_lambda_q2", "attn_lambda_k2", "attn_subln_g", "attn_w_o", "rel_bias",
        "ffn_w_gate_up", "ffn_w_down", "moe_router", "moe_w_gate_up", "moe_w_down"]


def kernel(**inputs):
    import numpy as _np
    import concourse.bacc as _bacc
    from concourse import mybir as _mybir
    from concourse.bass_utils import run_bass_kernel_spmd as _run

    nc = _bacc.Bacc("TRN2", target_bir_lowering=False, num_devices=1)
    arrays, args = {}, []
    for name in _INS:
        a = _np.ascontiguousarray(inputs[name])
        arrays[f"in_{name}_dram"] = a
        args.append(nc.dram_tensor(f"in_{name}_dram", a.shape, _mybir.dt.from_np(a.dtype), kind="ExternalInput").ap())
    args.append(nc.dram_tensor("out_0_dram", (1, SEQ, D), F32, kind="ExternalOutput").ap())
    trunk(nc, *args)
    r = _run(nc, [arrays], core_ids=[0])
    return r.results[0]["out_0_dram"]
```

```python
import math
from contextlib import ExitStack

import concourse.bass as bass
from concourse import mybir

F32 = mybir.dt.float32
F32R = mybir.dt.float32r
I32 = mybir.dt.int32
U32 = mybir.dt.uint32
ALU = mybir.AluOpType
ACT = mybir.ActivationFunctionType
AX = mybir.AxisListType

P = 128
D = 1024
DC = D // P
SEQ = 256
TC = SEQ // P
EPS = 1e-6
BANK = 512

G = 64
C = 16
ST = 64
CH = P // C
NCH = SEQ // CH
PAIRS = G // 2
QP = 8
ROUNDS = PAIRS // QP
ACT_STEPS = 5
POOL_PAIRS = 5
KP = CH + 1

H = 8
HD = 64
BUCKETS = 32
MAX_EXACT = BUCKETS // 2
MAX_DIST = 128
RELW = 2 * P + P
NEG = -1.0e30
LAMBDA_INIT = 0.8 - 0.6 * math.exp(-0.3)

F = 2816
E = 8
FH = 256
J = F // FH
HALF = D // 2

TILE = 4 * BANK
PART = TILE // 2
RAW_SLOTS = 11
PART_SLOTS = 6
GLU_BLOCKS = 2 * D // BANK
QKV_BLOCKS = 3 * D // BANK
WO_BLOCKS = D // BANK
MIX_TILES = 3 * J
MIX_PARTS = 2 * MIX_TILES
FIRST_FFN = 2 * GLU_BLOCKS
FIRST_QKV = FIRST_FFN + MIX_TILES
FIRST_WO = FIRST_QKV + 2 * QKV_BLOCKS
FIRST_MOE = FIRST_WO + 2 * WO_BLOCKS
assert MIX_TILES % RAW_SLOTS == 0 and MIX_PARTS % PART_SLOTS == 0


def w_part(j):
    return 6 * j - 2 if j else 0


def d_part(j):
    return 6 * j + 8 if j < J - 1 else MIX_PARTS - 2


def is_down(p):
    p %= MIX_PARTS
    return any(d_part(j) <= p < d_part(j) + 2 for j in range(J))


def downs_before(p):
    turns, p = divmod(p, MIX_PARTS)
    return 2 * J * turns + sum(is_down(k) for k in range(p))


def bucket_edges():
    import numpy as np
    n = np.arange(SEQ)
    f = np.maximum(n, 1).astype(np.float32)
    large = MAX_EXACT + (np.log(f / np.float32(MAX_EXACT)) / np.float32(math.log(MAX_DIST / MAX_EXACT))
                         * np.float32(BUCKETS - MAX_EXACT)).astype(np.int32)
    b = np.where(n < MAX_EXACT, n, np.minimum(large, BUCKETS - 1))
    return [int(np.searchsorted(b, k)) for k in range(BUCKETS)] + [SEQ]


def trunk(nc, x, norm_mix_g, norm_ffn_g, final_norm_g, ssm_a_re, ssm_a_im, ssm_log_dt, ssm_b_re,
          ssm_b_im, ssm_c_re, ssm_c_im, ssm_d, ssm_w_glu, attn_w_qkv, attn_lambda_q1,
          attn_lambda_k1, attn_lambda_q2, attn_lambda_k2, attn_subln_g, attn_w_o, rel_bias,
          ffn_w_gate_up, ffn_w_down, moe_router, moe_w_gate_up, moe_w_down, out):
    ctx = ExitStack()
    with ctx:
        def sem(name):
            return ctx.enter_context(nc.semaphore(name))

        def sbuf_in(stack):
            return lambda name, shape, dt=F32: stack.enter_context(nc.sbuf_tensor(name, shape, dt))

        sb = sbuf_in(ctx)
        x_res = sb("x_res", [P, TC, D])
        ident = sb("ident", [P, P])
        ones = sb("ones", [P, P])
        upto = sb("upto", [P, P])
        slot_no = sb("slot_no", [P, P])
        eps = sb("eps", [P, 1])
        small = sb("small", [P, 64])
        beside = ExitStack()
        bp = sbuf_in(beside)("bp", [P, 2, 2, QP, CH, C])
        beside.close()
        sc = sbuf_in(beside)("sc", [P, 2, 2, 3 * P])
        probs = sbuf_in(beside)("probs", [P, 2, 3 * P])
        pT = sbuf_in(beside)("pT", [P, 2, 3 * P])
        beside.close()
        final_gain = sbuf_in(beside)("final_gain", [P, D])
        beside.close()
        hT_hi = sb("hT_hi", [P, DC, SEQ], F32R)
        hT_lo = sb("hT_lo", [P, DC, SEQ], F32R)
        raw = [None] * RAW_SLOTS
        EARLY = 2
        for r in range(EARLY):
            raw[r] = sb(f"raw{r}", [P, TILE])

        ssm_stack = ExitStack()
        ss = sbuf_in(ssm_stack)
        toep = ss("toep", [P, 2, 2 * QP, P])
        state_diag = ss("state_diag", [P, 2, PAIRS, 2, NCH])
        uT = ss("uT", [P, G, NCH])
        bt_stack = ExitStack()
        bt = (sbuf_in(bt_stack)("bt", [P, 2, QP, P]),
              x_res[:, :, :].rearrange("p c d -> p (c d)").rearrange("p (r i s) -> p r i s", r=2, i=QP))
        bt_stack.close()
        y64 = ss("y64", [2 * NCH, 2, CH, P])
        a_raw = ss("a_raw", [PAIRS, 2, 2, ST])
        log_dt = ss("log_dt", [PAIRS, 2])
        dt_ = ss("dt_", [PAIRS, 2])
        gain_raw = ss("gain_raw", [G, CH, C])
        gain_u = ss("gain_u", [P, G])
        skip_raw = ss("skip_raw", [PAIRS, 2, C])
        skip = ss("skip", [2 * C, PAIRS, C])
        eye2 = ss("eye2", [2 * C, C])
        zero = ss("zero", [2 * C, BANK], mybir.dt.bfloat16)
        prep = ss("prep", [PAIRS, 14, P])
        coef4 = ss("coef4", [P, 4, PAIRS])
        b_raw = ss("b_raw", [P, 2, PAIRS, C])
        c_stack = ExitStack()
        c_raw = sbuf_in(c_stack)("c_raw", [P, 2, 4, 2, ST])
        c_stack.close()
        c_neg = ss("c_neg", [P, 2, PAIRS, C])
        c_q = ss("c_q", [P, 2, PAIRS, C])
        bb = ss("bb", [P, 2, PAIRS, C])
        bb_diag = ss("bb_diag", [P, 2, PAIRS, 2, C])
        pw = ss("pw", [P, 2, KP, PAIRS])
        pr = ss("pr", [P, 2, CH, PAIRS])
        carry = ss("carry", [P, 2, 2, PAIRS])
        tmp_v = ss("tmp_v", [P, QP * KP * C])
        tmp_p = ss("tmp_p", [P, QP * KP * C])
        x_stack = ExitStack()
        x32 = sbuf_in(x_stack)("x32", [NCH, CH, D])
        h32 = sbuf_in(x_stack)("h32", [NCH, G, CH, C])
        x_stack.close()
        gk = ss("gk", [P, ROUNDS, 2, QP, KP, C])
        xin = ss("xin", [P, 2, PAIRS, NCH])
        state = ss("state", [P, 2, PAIRS, NCH])
        kern = (ss("kern", [2 * C, 2 * QP, P]),
                bp[0:2 * C, 1, :, :, :, :].rearrange("p r i s c -> p (r i) (s c)"))
        ssm_stack.close()

        xn = sb("xn", [P, TC, D])
        gain = sb("gain", [P, D])
        for r in range(EARLY, RAW_SLOTS):
            raw[r] = sb(f"raw{r}", [P, TILE])
        hi = [sb(f"hi{k}", [P, PART], F32R) for k in range(PART_SLOTS)]
        lo = [sb(f"lo{k}", [P, PART], F32R) for k in range(PART_SLOTS)]
        mixer_stack = ExitStack()
        sx = sbuf_in(mixer_stack)
        gate = sx("gate", [P, 2, FH])
        act = sx("act", [P, 2, FH])
        actT_hi = sx("actT_hi", [P, 2, 2 * P], F32R)
        actT_lo = sx("actT_lo", [P, 2, 2 * P], F32R)
        mixer_stack.close()
        v = sb("v", [P, TC, D])

        attn_stack = ExitStack()
        sa = sbuf_in(attn_stack)
        table = sa("table", [P, BUCKETS, H])
        asm = sa("asm", [P, 2, 16])
        lam_in = sa("lam_in", [P, 4, HD])
        lam = sa("lam", [P, 8])
        sub_gain = sa("sub_gain", [P, 1])
        osq = sa("osq", [P, TC, H])
        sqscr = sa("sqscr", [P, 2, P])
        rel_stack = ExitStack()
        relrow = sbuf_in(rel_stack)("relrow", [P, H, RELW])
        rel_stack.close()
        qT = sa("qT", [P, H, SEQ])
        kT = sa("kT", [P, H, SEQ])
        bias = xn[:, :, :].rearrange("p c d -> p (c d)").rearrange("p (h k) -> p h k", h=H)
        attn_stack.close()

        moe_stack = ExitStack()
        sm = sbuf_in(moe_stack)
        xeT_hi = sm("xeT_hi", [P, DC, P], F32R)
        xeT_lo = sm("xeT_lo", [P, DC, P], F32R)
        pick = sm("pick", [P, TC, P])
        pick_gate = sm("pick_gate", [P, TC, P])
        pick_gateT = sm("pick_gateT", [P, TC, P])
        ye = sm("ye", [P, D])
        router = sm("router", [P, DC, E])
        router_hi = sm("router_hi", [P, DC, E], F32R)
        router_lo = sm("router_lo", [P, DC, E], F32R)
        logitsT = sm("logitsT", [E, SEQ])
        rt = sm("rt", [P, TC, 12, E])
        top_i = sm("top_i", [P, TC, 8], U32)
        key = sm("key", [P, TC, 2 * E + 1])
        gates = sm("gates", [P, TC, 2 * E + 1])
        passes = sm("passes", [P, 8])
        passes_i = sm("passes_i", [P, 1], I32)
        moe_stack.close()

        ps = ctx.enter_context(nc.psum_tensor("ps", [P, 8 * BANK], F32))

        def bank(b, n=1):
            return ps[:, b * BANK:(b + n) * BANK]

        SCATTER_BANKS = (4, 5, 1, 3)

        rel_scratch = nc.dram_tensor("rel_scratch", [P, H * RELW], F32, kind="Internal")

        x32_in, xres_in = sem("x32_in"), sem("xres_in")
        prep_in, bc_in, b_in, c_in = sem("prep_in"), sem("bc_in"), sem("b_in"), sem("c_in")
        gain_in, const_in = sem("gain_in"), sem("const_in")
        raw_in = [sem(f"raw_in{r}") for r in range(RAW_SLOTS)]
        hi_ready, lo_wide, lo_down, part_used = (
            sem("hi_ready"), sem("lo_wide"), sem("lo_down"), sem("part_used"))
        pool_const, pool_step = sem("pool_const"), sem("pool_step")
        dve_step, act_step = sem("dve_step"), sem("act_step")
        pe_prep, act_prep = sem("pe_prep"), sem("act_prep")
        dve_prep, coef_ready, coef_sb = sem("dve_prep"), sem("coef_ready"), sem("coef_sb")
        u_ps, u_sb = sem("u_ps"), sem("u_sb")
        h_ready, h_pool, zeroed = sem("h_ready"), sem("h_pool"), sem("zeroed")
        bp_re, bp_im, bt_ps, bt_sb = sem("bp_re"), sem("bp_im"), sem("bt_ps"), sem("bt_sb")
        xin_ps, xin_sb = sem("xin_ps"), sem("xin_sb")
        gk_re, gk_im, kern_ps, kern_sb = sem("gk_re"), sem("gk_im"), sem("kern_ps"), sem("kern_sb")
        toep_in, inside_done = sem("toep_in"), sem("inside_done")
        bb_diag_ready, state_top, state_bottom = sem("bb_diag_ready"), sem("state_top"), sem("state_bottom")
        state_ready, y_ps, y_sb = sem("state_ready"), sem("y_ps"), sem("y_sb")
        yT_ps, gelu_done = sem("yT_ps"), sem("gelu_done")
        glu_sig, glu_add = sem("glu_sig"), sem("glu_add")
        rms_ready, rms_inv, o_scaled = sem("rms_ready"), sem("rms_inv"), sem("o_scaled")
        sq_done, xn_ready, hT_ps = sem("sq_done"), sem("xn_ready"), sem("hT_ps")
        hi_sides, lo_sides = sem("hi_sides"), sem("lo_sides")
        silu_done, act_ready = sem("silu_done"), sem("act_ready")
        actT_ps, actT_hi_ready, actT_lo_ready = sem("actT_ps"), sem("actT_hi_ready"), sem("actT_lo_ready")
        ffn_add, block_done = sem("ffn_add"), sem("block_done")
        qkv_sb = sem("qkv_sb")
        table_in, rel_filled, rel_out, bias_in, lam_ready = (
            sem("table_in"), sem("rel_filled"), sem("rel_out"), sem("bias_in"), sem("lam_ready"))
        sc_ps, sc_sb, max_done, exp_done, probs_ready = (
            sem("sc_ps"), sem("sc_sb"), sem("max_done"), sem("exp_done"), sem("probs_ready"))
        pT_ps, pT_sb, o_ps, osq_done, o_sb = sem("pT_ps"), sem("pT_sb"), sem("o_ps"), sem("osq_done"), sem("o_sb")
        oT_ps, wo_add = sem("oT_ps"), sem("wo_add")
        (router_in, router_hi_ready, router_split, logitsT_ps, logitsT_sb, logit_ps, top_diff, top_exp,
         sel_ready, cnt_ps, routed) = (
            sem("router_in"), sem("router_hi_ready"), sem("router_split"), sem("logitsT_ps"), sem("logitsT_sb"),
            sem("logit_ps"), sem("top_diff"), sem("top_exp"), sem("sel_ready"),
            sem("cnt_ps"), sem("routed"))
        pick_ready, gate_pick_ready, gather_ps, xeT_hi_ready, xeT_lo_ready = (
            sem("pick_ready"), sem("gate_pick_ready"), sem("gather_ps"),
            sem("xeT_hi_ready"), sem("xeT_lo_ready"))
        pgT_ps, pgT_sb, ye_sb, scat_ps, scat_add = (
            sem("pgT_ps"), sem("pgT_sb"), sem("ye_sb"), sem("scat_ps"), sem("scat_add"))
        final_ready, out_done = sem("final_ready"), sem("out_done")

        CONSTS = 6

        glu_w = ssm_w_glu[0].rearrange("(dc p) n -> p dc n", p=P)
        qkv_w = attn_w_qkv[0].rearrange("(dc p) n -> p dc n", p=P)
        wo_w = attn_w_o[0].rearrange("(dc p) n -> p dc n", p=P)
        gu_w = ffn_w_gate_up[0].rearrange("(dc p) n -> p dc n", p=P)
        dn_w = ffn_w_down[0].rearrange("(j fc p) n -> j p fc n", p=P, fc=2)
        egu_w = moe_w_gate_up[0].rearrange("e (dc p) n -> e p dc n", p=P)
        edn_w = moe_w_down[0].rearrange("e (j fc p) n -> e j p fc n", p=P, fc=2)

        WIDE_BEFORE = 2 * (FIRST_MOE - J)
        DOWN_BEFORE = 2 * J

        def static_counts(n):
            p = min(max(n - 2 * FIRST_FFN, 0), MIX_PARTS)
            return n - downs_before(p), downs_before(p)

        class Pass:

            def __init__(self, it=None):
                self.it, self.dense = it, it is None
                self.nb = TC if self.dense else 1

            def add(self, per_pass, n):
                return n if self.dense else self.it * per_pass + n

            def parts(self, p):
                return self.add(MIX_PARTS, 2 * (FIRST_FFN if self.dense else FIRST_MOE) + p)

            def wide(self, p):
                if self.dense:
                    return static_counts(2 * FIRST_FFN + p)[0]
                return self.add(4 * J, WIDE_BEFORE + p - downs_before(p))

            def down(self, p):
                if self.dense:
                    return static_counts(2 * FIRST_FFN + p)[1]
                return self.add(2 * J, DOWN_BEFORE + downs_before(p))

            def items(self, k):
                return self.add(J, (0 if self.dense else TC * J) + k)

            def slot(self, p):
                return (2 * (FIRST_FFN if self.dense else FIRST_MOE) + p) % PART_SLOTS

            def raw(self, p):
                n = (FIRST_FFN if self.dense else FIRST_MOE) + p // 2
                fills = self.add(MIX_TILES // RAW_SLOTS, n // RAW_SLOTS + 1)
                return n % RAW_SLOTS, fills, slice(p % 2 * PART, (p % 2 + 1) * PART)

            def is_down(self, p):
                return is_down(p) and (not self.dense or p < MIX_PARTS)

        class Before:
            parts = staticmethod(lambda n: n)
            wide = staticmethod(lambda n: static_counts(n)[0] if n < 2 * FIRST_MOE else
                                WIDE_BEFORE + (n - 2 * FIRST_MOE) - downs_before(n - 2 * FIRST_MOE))
            slot = staticmethod(lambda n: n % PART_SLOTS)
            raw = staticmethod(lambda n: (n // 2 % RAW_SLOTS, n // 2 // RAW_SLOTS + 1,
                                          slice(n % 2 * PART, (n % 2 + 1) * PART)))
            is_down = staticmethod(lambda n: 2 * FIRST_FFN <= n < 2 * FIRST_QKV and is_down(n - 2 * FIRST_FFN))

        def split_hi(act_e, at, p):
            r, fills, cols = at.raw(p)
            act_e.wait_ge(raw_in[r], fills * 32)
            if at is not Before or p >= PART_SLOTS:
                act_e.wait_ge(part_used, at.parts(p - PART_SLOTS + 1))
            nc.scalar.activation(hi[at.slot(p)][:, :], raw[r][:, cols], ACT.Copy).then_inc(hi_ready, 1)

        def split_lo(eng, at, p):
            r, _, cols = at.raw(p)
            eng.wait_ge(hi_ready, at.parts(p + 1))
            eng.tensor_tensor(lo[at.slot(p)][:, :], raw[r][:, cols], hi[at.slot(p)][:, :].bitcast(F32),
                              ALU.subtract).then_inc(lo_down if at.is_down(p) else lo_wide, 1)

        block = ctx.enter_context(nc.Block())

        @block.sync
        def _(sp):
            sp.dma_start(a_raw[:, 0, :, :], ssm_a_re[0].rearrange("(h i) p -> i h p", h=2)).then_inc(prep_in, 16)
            sp.dma_start(a_raw[:, 1, :, :], ssm_a_im[0].rearrange("(h i) p -> i h p", h=2)).then_inc(prep_in, 16)
            sp.dma_start(log_dt[:, :], ssm_log_dt[0].rearrange("(h i) -> i h", h=2),
                         allow_slow_non_contiguous=True).then_inc(prep_in, 16)
            sp.dma_start(x32[:, :, :], x[0].rearrange("(n t) d -> n t d", t=CH)).then_inc(x32_in, 16)
            sp.dma_start(gain_raw[:, :, :], norm_mix_g[0:1, :].rearrange("o (g c) -> g o c", c=C).to_broadcast(
                [G, CH, C])).then_inc(bc_in, 16)
            sp.dma_start(skip_raw[:, :, :], ssm_d[0].rearrange("(h i c) -> i h c", h=2, c=C)).then_inc(bc_in, 16)
            for r, src in enumerate((ssm_c_re, ssm_c_im)):
                for h in range(2):
                    sp.dma_start(c_raw[:, r, :, h, :], src[0][h * PAIRS:(h + 1) * PAIRS].rearrange(
                        "g c p -> (g c) p").rearrange("(k r) p -> r k p", r=P)).then_inc(c_in, 16)
            for r, src in enumerate((ssm_b_re, ssm_b_im)):
                for h in range(2):
                    sp.dma_start(b_raw[h * ST:(h + 1) * ST, r, :, :],
                                 src[0][h * PAIRS:(h + 1) * PAIRS].rearrange("i p c -> p i c")).then_inc(b_in, 16)

            def tile_dst(r, down_tile, halves):
                if down_tile:
                    return raw[r][:, :].rearrange("p (fc n) -> p fc n", fc=2)
                if halves:
                    return raw[r][:, :].rearrange("p (dc two w) -> p dc two w", dc=4, two=2)
                return raw[r][:, :].rearrange("p (dc w) -> p dc w", dc=4)

            def load_tile(r, src, down_tile, halves):
                dst = tile_dst(r, down_tile, halves)
                for k in range(2):
                    if down_tile or not halves:
                        part = slice(k * dst.shape[1] // 2, (k + 1) * dst.shape[1] // 2)
                        sp.dma_start(dst[:, part, :], src[:, part, :]).then_inc(raw_in[r], 16)
                    else:
                        sp.dma_start(dst[:, :, k, :], src[:, :, k, :]).then_inc(raw_in[r], 16)

            def halves_src(src, width, block, half):
                return src.rearrange("p dc (two w) -> p dc two w", two=2)[
                    :, 4 * half:4 * half + 4, :, block * FH:(block + 1) * FH]

            def mixer_src(gate_up, down_w, t):
                for j in range(J):
                    if t == d_part(j) // 2:
                        return down_w(j), True
                    if t - w_part(j) // 2 in (0, 1):
                        return halves_src(gate_up, F, j, t - w_part(j) // 2), False

            def load_static(n):
                if n >= RAW_SLOTS:
                    wides, downs = static_counts(2 * (n - RAW_SLOTS + 1))
                    if Before.is_down(2 * (n - RAW_SLOTS)):
                        sp.wait_ge(lo_down, downs)
                    else:
                        sp.wait_ge(lo_wide, wides)
                down_tile, halves = False, n < FIRST_QKV
                if n < FIRST_FFN:
                    src = halves_src(glu_w, D, n // 2, n % 2)
                elif n < FIRST_QKV:
                    src, down_tile = mixer_src(gu_w, lambda j: dn_w[j], n - FIRST_FFN)
                else:
                    w, m = (qkv_w, (n - FIRST_QKV + 8) % (2 * QKV_BLOCKS)) if n < FIRST_WO else (wo_w, n - FIRST_WO)
                    src = w[:, 4 * (m % 2):4 * (m % 2) + 4, m // 2 * BANK:(m // 2 + 1) * BANK]
                load_tile(n % RAW_SLOTS, src, down_tile, halves)

            def load_gain(src):
                sp.dma_start(gain[:, :], src.to_broadcast([P, D])).then_inc(gain_in, 16)

            for n in range(EARLY):
                load_static(n)
            sp.wait_ge(xin_ps, ROUNDS)
            sp.dma_start(x_res[:, :, :], x[0].rearrange("(c p) d -> p c d", p=P)).then_inc(xres_in, 16)
            sp.wait_ge(zeroed, 1)
            for q in range(0, ROUNDS, 2):
                sp.wait_ge(kern_sb, 2 * (q + 2))
                if q:
                    sp.wait_ge(inside_done, q)
                for s in range(CH):
                    for h in range(2):
                        sp.dma_start(toep[s * C:(s + 1) * C, h, :, s * C:P],
                                     kern[q // 2][h * C:(h + 1) * C, :, 0:P - s * C]).then_inc(toep_in, 16)
            sp.wait_ge(yT_ps, ROUNDS)
            for n in range(EARLY, FIRST_FFN):
                load_static(n)
                if n == FIRST_FFN - 1:
                    load_gain(norm_ffn_g[0:1, :])
            sp.dma_start(table[:, :, :], rel_bias.rearrange("b h -> (b h)").unsqueeze(0).to_broadcast(
                [P, BUCKETS * H])).then_inc(table_in, 16)
            for k, src in enumerate((attn_lambda_q1, attn_lambda_k1, attn_lambda_q2, attn_lambda_k2)):
                sp.dma_start(lam_in[:, k, :], src.to_broadcast([P, HD])).then_inc(table_in, 16)
            sp.dma_start(sub_gain[:, :], attn_subln_g.rearrange("o d -> d o"),
                         allow_slow_non_contiguous=True).then_inc(table_in, 16)
            for n in range(FIRST_FFN, FIRST_QKV):
                load_static(n)
                if n == FIRST_FFN + RAW_SLOTS:
                    sp.wait_ge(rel_filled, 1)
                    sp.dma_start(rel_scratch.ap(), relrow[:, :, :]).then_inc(rel_out, 16)
                    sp.wait_ge(xn_ready, TC)
                    load_gain(norm_mix_g[1:2, :])
            for n in range(FIRST_QKV, FIRST_WO):
                load_static(n)
                if n == FIRST_QKV + RAW_SLOTS - 3:
                    sp.wait_ge(rel_out, 16)
                    sp.wait_ge(hT_ps, 2 * 2 * TC)
                    load_gain(norm_ffn_g[1:2, :])
                    sp.dma_start(bias[:, :, :], bass.AP(rel_scratch, P - 1, [[H * RELW - 1, P], [RELW, H], [1, 2 * P]])
                                 ).then_inc(bias_in, 16)
            for n in range(FIRST_WO, FIRST_MOE):
                load_static(n)

            def load_expert_tile(at, e, t):
                last = 2 * (t - RAW_SLOTS)
                if last < 0:
                    sp.wait_ge(part_used, at.parts(last + 2))
                elif is_down(last):
                    sp.wait_ge(lo_down, at.down(last + 2))
                else:
                    sp.wait_ge(lo_wide, at.wide(last + 2))
                src, down_tile = mixer_src(egu_w[bass.ds(e, 1)].rearrange("o p dc n -> (o p) dc n"),
                                           lambda j: edn_w[bass.ds(e, 1), j].rearrange("o p fc n -> (o p) fc n"), t)
                load_tile(at.raw(2 * t)[0], src, down_tile, True)

            AHEAD = (4 + PART_SLOTS) // 2

            def load_expert(it, e, e_next):
                at = Pass(it)
                for t in range(AHEAD, MIX_TILES):
                    load_expert_tile(at, e, t)
                at_next = Pass(it + 1)
                for t in range(AHEAD):
                    load_expert_tile(at_next, e_next, t)

            for t in range(AHEAD):
                load_expert_tile(Pass(0), 0, t)
            sp.wait_ge(pT_sb, H)
            sp.dma_start(router[:, :, :], moe_router[0].rearrange("(dc p) e -> p dc e", p=P)).then_inc(router_in, 16)
            with sp.Fori(0, E - 1) as it:
                load_expert(it, it, it + 1)
            load_expert(E - 1, E - 1, 0)
            sp.wait_ge(routed, 1)
            n_pass = sp.value_load(passes_i[0:1, 0:1], min_val=1, max_val=2)
            with sp.If(n_pass > 1):
                with sp.Fori(E, 2 * E - 1) as it:
                    load_expert(it, it - E, it - (E - 1))
                load_expert(2 * E - 1, E - 1, 0)
            sp.dma_start(final_gain[:, :], final_norm_g.unsqueeze(0).to_broadcast([P, D])).then_inc(const_in, 16)
            for c in range(TC):
                sp.wait_ge(final_ready, c + 1)
                sp.dma_start(out[0, c * P:(c + 1) * P, :], xn[:, c, :]).then_inc(out_done, 16)
            sp.wait_ge(out_done, 16 * TC)

        @block.gpsimd
        def _(pool):
            n_step = [0]

            def step(ins):
                n_step[0] += 1
                ins.then_inc(pool_step, 1)
                pool.wait_ge(pool_step, n_step[0])

            pool.memset(eps[:, :], EPS).then_inc(pool_const, 1)
            step(pool.memset(ident[:, :], 0.0))
            pool.affine_select(out=ident[:, :], in_=ident[:, :], compare_op=ALU.not_equal, fill=1.0,
                               base=0, pattern=[[-1, P]], channel_multiplier=1).then_inc(pool_const, 1)
            step(pool.memset(ones[:, :], 1.0))
            pool.affine_select(out=upto[:, :], in_=ones[:, :], compare_op=ALU.is_ge, fill=0.0,
                               base=0, pattern=[[1, P]], channel_multiplier=-1).then_inc(pool_const, 1)
            pool.iota(slot_no[:, :], [[1, P]], base=0, channel_multiplier=0,
                      allow_small_or_imprecise_dtypes=True).then_inc(pool_const, 3)
            pool.memset(bb_diag[:, :, :, :, :], 0.0)
            pool.memset(zero[:, :], 0.0)
            pool.memset(state_diag[:, :, :, :, :], 0.0)
            pool.memset(toep[:, :, :, :], 0.0).then_inc(zeroed, 1)

            pool.wait_ge(x32_in, 16)
            pool.wait_ge(rms_inv, 1)
            for s in range(ACT_STEPS, CH):
                ins = pool.tensor_tensor(h32[:, :, s, :], x32[:, s, :].rearrange("n (g c) -> n g c", g=G),
                                         small[0:NCH, s:s + 1].unsqueeze(2).to_broadcast([NCH, G, C]), ALU.mult)
            ins.then_inc(h_pool, 1)

            pool.wait_ge(dve_prep, 2)
            t = tmp_p[:, 0:POOL_PAIRS * CH * C].rearrange("p (i s c) -> p i s c", i=POOL_PAIRS, s=CH)
            for q in range(ROUNDS):
                if q >= 2:
                    pool.wait_ge(bt_ps, 4 * (q - 1))
                i = slice(q * QP, q * QP + POOL_PAIRS)
                b_of = lambda r: bb[:, r, i, :].unsqueeze(2).to_broadcast([P, POOL_PAIRS, CH, C])
                p_of = lambda r: pr[:, r, :, i].rearrange("p s i -> p i s").unsqueeze(3).to_broadcast(
                    [P, POOL_PAIRS, CH, C])
                o = bp[:, q % 2, 1, 0:POOL_PAIRS, :, :]
                step(pool.tensor_tensor(o, b_of(0), p_of(1), ALU.mult))
                step(pool.tensor_tensor(t, b_of(1), p_of(0), ALU.mult))
                pool.tensor_tensor(o, o, t, ALU.add).then_inc(bp_im, 1)

            t9 = tmp_p[:, :].rearrange("p (i k c) -> p i k c", i=QP, k=KP)
            pool.wait_ge(act_prep, 6)
            pool.wait_ge(u_ps, 4)
            for q in range(ROUNDS):
                i = slice(q * QP, (q + 1) * QP)
                c_of = lambda r: c_neg[:, r, i, :].unsqueeze(2).to_broadcast([P, QP, KP, C])
                p_of = lambda r: pw[:, r, :, i].rearrange("p k i -> p i k").unsqueeze(3).to_broadcast([P, QP, KP, C])
                g = gk[:, q, 1, :, :, :]
                step(pool.tensor_tensor(g, c_of(0), p_of(1), ALU.mult))
                step(pool.tensor_tensor(t9, c_of(1), p_of(0), ALU.mult))
                ins = pool.tensor_tensor(g, g, t9, ALU.add)
                if q == ROUNDS - 1:
                    step(ins)
                    g = gk[:, q, 0, :, :, :]
                    step(pool.tensor_tensor(g, c_of(0), p_of(0), ALU.mult))
                    step(pool.tensor_tensor(t9, c_of(1), p_of(1), ALU.mult))
                    ins = pool.tensor_tensor(g, t9, g, ALU.subtract)
                ins.then_inc(gk_im, 1)

            pool.wait_ge(table_in, 16 * 6)
            edges = bucket_edges()
            step(pool.memset(relrow[:, :, :], NEG))
            for b in range(BUCKETS):
                lo, hi = SEQ - edges[b + 1], SEQ - edges[b]
                ins = pool.tensor_copy(relrow[:, :, lo:hi], table[:, b, :].unsqueeze(2).to_broadcast([P, H, hi - lo]))
            ins.then_inc(rel_filled, 1)

            for n in range(2 * FIRST_FFN, 2 * FIRST_QKV):
                if Before.is_down(n):
                    split_lo(pool, Before, n)

            def expert(it):
                at = Pass(it)
                for p in range(MIX_PARTS):
                    if at.is_down(p):
                        split_lo(pool, at, p)

            with pool.Fori(0, E) as it:
                expert(it)
            pool.wait_ge(routed, 1)
            n_pass = pool.value_load(passes_i[0:1, 0:1], min_val=1, max_val=2)
            with pool.If(n_pass > 1):
                with pool.Fori(E, 2 * E) as it:
                    expert(it)

        @block.scalar
        def _(act_e):
            n_step = [0]

            def step(ins):
                n_step[0] += 1
                ins.then_inc(act_step, 1)
                act_e.wait_ge(act_step, n_step[0])

            def activation(*a, **k):
                return nc.scalar.activation(*a, **k)

            def root(ms, width):
                activation(ms, ms, ACT.Sqrt, scale=1.0 / width, bias=eps[0:ms.shape[0], :]).then_inc(rms_ready, 1)

            act_e.wait_ge(prep_in, 48)
            activation(dt_[:, :], log_dt[:, :], ACT.Exp).then_inc(act_prep, 1)
            act_e.wait_ge(dve_prep, 1)
            activation(prep[:, 1, :], prep[:, 0, :], ACT.Exp).then_inc(act_prep, 1)
            activation(prep[:, 3, :], prep[:, 2, :], ACT.Sin, scale=0.5).then_inc(act_prep, 1)
            activation(prep[:, 4, :], prep[:, 2, :], ACT.Sin).then_inc(act_prep, 1)
            act_e.wait_ge(x32_in, 16)
            for s in range(CH):
                ins = activation(uT[0:NCH, 0:NCH, :].rearrange("p a b -> p (a b)"), x32[:, s, :], ACT.Square,
                                 accum_out=small[0:NCH, s:s + 1])
                ins.then_inc(sq_done, 1)
                act_e.wait_ge(sq_done, s + 1)
            act_e.wait_ge(pool_const, CONSTS)
            root(small[0:NCH, 0:CH], D)
            act_e.wait_ge(pe_prep, 1)
            for r in range(2):
                o = lambda z: z[:, r, :, :].rearrange("p i c -> p (i c)")
                activation(o(c_neg), bank(4 + r), ACT.Copy, scale=-1.0)
                activation(o(c_q), bank(4 + r), ACT.Copy).then_inc(act_prep, 1)
            act_e.wait_ge(rms_inv, 1)
            for s in range(ACT_STEPS):
                ins = activation(h32[:, :, s, :], x32[:, s, :].rearrange("n (g c) -> n g c", g=G), ACT.Copy,
                                 scale=small[0:NCH, s:s + 1])
            ins.then_inc(h_ready, 1)
            act_e.wait_ge(dve_prep, 2)
            act_e.wait_ge(zeroed, 1)
            for h in range(2):
                part = slice(h * ST, (h + 1) * ST)
                activation(bb_diag[part, :, :, h, :].rearrange("p r i c -> p (r i) c"),
                           bb[part, :, :, :].rearrange("p r i c -> p (r i) c"), ACT.Copy).then_inc(bb_diag_ready, 1)
            def chunk_inputs(q):
                act_e.wait_ge(xin_ps, q + 1)
                src = bank(4 + 2 * (q % 2), 2).rearrange("p (r i v n) -> p r i v n", r=2, i=QP, v=2)
                for h in range(2):
                    part = slice(h * ST, (h + 1) * ST)
                    for r in range(2):
                        activation(xin[part, r, q * QP:(q + 1) * QP, :], src[part, r, :, h, :],
                                   ACT.Copy).then_inc(xin_sb, 1)

            for q in range(ROUNDS):
                if q >= 2:
                    act_e.wait_ge(xin_ps, q - 1)
                for b in range(4):
                    act_e.wait_ge(bt_ps, 4 * q + b + 1)
                    activation(bt[q % 2].rearrange("p r i s -> p (r i s)")[:, b * BANK:(b + 1) * BANK],
                               bank(b), ACT.Copy).then_inc(bt_sb, 1)
                if q >= 1:
                    chunk_inputs(q - 1)
            chunk_inputs(ROUNDS - 1)

            def responses(q):
                for b in range(2):
                    act_e.wait_ge(kern_ps, 2 * q + b + 1)
                    activation(kern[q // 2][:, q % 2 * QP + 4 * b:q % 2 * QP + 4 * b + 4, :].rearrange("p i k -> p (i k)"),
                               bank(4 + b)[0:2 * C, :], ACT.Copy).then_inc(kern_sb, 1)

            for q in range(ROUNDS):
                responses(q)
            act_e.wait_ge(state_ready, 1)
            for q in range(ROUNDS):
                activation(state_diag[0:ST, :, q * QP:(q + 1) * QP, 0, :], state[0:ST, :, q * QP:(q + 1) * QP, :],
                           ACT.Copy).then_inc(state_top, 1)
            for b in range(4):
                if b >= 2:
                    act_e.wait_ge(y_ps, 2)
                    for p in (2 * b - 4, 2 * b - 3):
                        split_hi(act_e, Before, p)
                act_e.wait_ge(yT_ps, b + 1)
                out_t = bank(6 + b % 2)
                activation(out_t, out_t, ACT.Gelu_apprx_tanh).then_inc(gelu_done, 1)
                act_e.wait_ge(gelu_done, b + 1)
                for k in range(2):
                    activation(hT_hi[:, b + 4 * k, :].rearrange("p (n t) -> p t n", t=CH),
                               out_t.rearrange("p (t h n) -> p h t n", t=CH, h=2)[:, k],
                               ACT.Copy).then_inc(hi_sides, 1)
            for p in range(4, PART_SLOTS):
                split_hi(act_e, Before, p)
            n_squares = [0]

            def square(c, ready, value):
                if c == 0:
                    activation(small[:, 16 + n_squares[0]:17 + n_squares[0]], eps[:, :], ACT.Sqrt)
                act_e.wait_ge(ready, value)
                activation(xn[:, c, :], x_res[:, c, :], ACT.Square, accum_out=small[:, 8 + c:9 + c]).then_inc(sq_done, 1)
                n_squares[0] += 1
                act_e.wait_ge(sq_done, CH + n_squares[0])
                root(small[:, 8 + c:9 + c], D)

            for n in range(GLU_BLOCKS):
                last = n == GLU_BLOCKS - 1

                def gate_of(c):
                    if n >= 1:
                        act_e.wait_ge(glu_add, TC * (n - 1) + c + 1)
                    activation(gate[:, c, :], bank(2 * (n % 2) + c)[:, FH:2 * FH], ACT.Sigmoid).then_inc(glu_sig, 1)

                if last:
                    act_e.wait_ge(block_done, 1)
                    gate_of(0)
                for p in range(2 if last else 4):
                    if p == 3:
                        act_e.wait_ge(part_used, 4 * n + 4)
                        for c in range(TC):
                            gate_of(c)
                    split_hi(act_e, Before, 4 * n + p + PART_SLOTS)
            act_e.wait_ge(part_used, 4 * GLU_BLOCKS)
            gate_of(1)

            def split_block_end(first_part):
                for p in (2, 3):
                    split_hi(act_e, Before, first_part - 4 + p + PART_SLOTS)

            n_hT = [0]

            def round_hT():
                base = 2 * TC * n_hT[0]
                for c in range(TC):
                    for k in range(2):
                        act_e.wait_ge(hT_ps, base + 2 * c + k + 1)
                        activation(hT_hi[:, 4 * k:4 * k + 4, c * P:(c + 1) * P],
                                   bank(4 * c + k).rearrange("p (dc t) -> p dc t", dc=4), ACT.Copy).then_inc(hi_sides, 1)
                n_hT[0] += 1

            def gates_of(at, j):
                for p in range(w_part(j), w_part(j) + 4):
                    if p == w_part(j) + 3:
                        act_e.wait_ge(part_used, at.parts(p + 1))
                        for c in range(at.nb):
                            activation(gate[:, c, :], bank(c)[:, 0:FH], ACT.Silu).then_inc(silu_done, 1)
                    split_hi(act_e, at, p + PART_SLOTS)

            def turned(at, j):
                for c in range(at.nb):
                    act_e.wait_ge(actT_ps, at.items(at.nb * j + c + 1))
                    activation(actT_hi[:, c, :], bank(2 + c)[:, 0:2 * P], ACT.Copy).then_inc(actT_hi_ready, 1)

            def mixer_pass(at, finish):
                for j in range(1, J + 1):
                    if j < J:
                        gates_of(at, j)
                    else:
                        finish()
                    for p in range(d_part(j - 1), d_part(j - 1) + 2):
                        if j < J or not at.dense:
                            split_hi(act_e, at, p + PART_SLOTS)
                    if j < J:
                        turned(at, j)

            for c in range(TC):
                square(c, glu_add, TC * GLU_BLOCKS - 1 + c)
            round_hT()
            split_block_end(2 * FIRST_FFN)
            gates_of(Pass(), 0)
            turned(Pass(), 0)
            mixer_pass(Pass(), lambda: square(0, ffn_add, 2))
            square(1, ffn_add, 4)
            round_hT()
            split_block_end(2 * FIRST_QKV)
            act_e.wait_ge(lam_ready, 1)
            activation(lam[:, 2:4], lam[:, 0:2], ACT.Exp).then_inc(lam_ready, 1)
            for n in range(QKV_BLOCKS):
                p0 = 2 * FIRST_QKV + 4 * n
                for p in range(4):
                    split_hi(act_e, Before, p0 + p + PART_SLOTS)
                for m in range(TC if n < 2 else 4):
                    if n < 2:
                        o, src = v[:, m, n * BANK:(n + 1) * BANK], bank(4 * (n % 2) + m)
                    else:
                        o, src = (qT, kT)[n // 2 - 1][:, 4 * (n % 2) + m, :], bank(4 * (n % 2) + m)[:, 0:SEQ]
                    activation(o, src, ACT.Copy, scale=HD ** -0.5 if n in (2, 3) else 1.0).then_inc(qkv_sb, 1)

            def head_tail(h):
                act_e.wait_ge(pT_ps, h + 1)
                if h >= 2:
                    act_e.wait_ge(o_ps, h - 1)
                activation(pT[:, h % 2, :], bank(4 + h % 2)[:, 0:3 * P], ACT.Copy).then_inc(pT_sb, 1)
                act_e.wait_ge(o_ps, h + 1)
                for qb in range(2):
                    activation(sqscr[:, qb, :], bank(6 + h % 2)[:, qb * P:(qb + 1) * P], ACT.Square,
                               accum_out=osq[:, qb, h:h + 1]).then_inc(osq_done, 1)

            for h in range(H):
                act_e.wait_ge(max_done, h + 1)
                for m in range(2):
                    for qb in range(2):
                        cols = slice(0, P) if qb == 0 else slice(P, 3 * P)
                        k = 2 * qb + m
                        activation(sc[:, h % 2, m, cols], sc[:, h % 2, m, cols], ACT.Exp,
                                   bias=asm[:, h % 2, k:k + 1], accum_out=asm[:, h % 2, 4 + k:5 + k]
                                   ).then_inc(exp_done, 1)
                if h >= 1:
                    act_e.wait_ge(osq_done, 2 * (h - 1))
                    head_tail(h - 1)
            head_tail(H - 1)
            act_e.wait_ge(osq_done, 2 * H)
            root(osq[:, :, :].rearrange("p c h -> p (c h)"), 2 * HD)
            act_e.wait_ge(lam_ready, 3)
            for u in range(4):
                act_e.wait_ge(oT_ps, u + 1)
                c, k = divmod(u, 2)
                activation(hT_hi[:, 4 * k:4 * k + 4, c * P:(c + 1) * P], bank(u).rearrange("p (dc t) -> p dc t", dc=4),
                           ACT.Copy, scale=sub_gain[:, :]).then_inc(hi_sides, 1)
            for p in range(4 * WO_BLOCKS):
                if p == 4 * (WO_BLOCKS - 1):
                    act_e.wait_ge(router_in, 16)
                    activation(router_hi[:, :, :], router[:, :, :], ACT.Copy).then_inc(router_hi_ready, 1)
                    square(0, wo_add, TC * WO_BLOCKS - 1)
                if p < 4 * WO_BLOCKS - 2:
                    split_hi(act_e, Before, 2 * FIRST_WO + p + PART_SLOTS)
            square(1, wo_add, TC * WO_BLOCKS)
            round_hT()
            split_block_end(2 * FIRST_MOE)
            act_e.wait_ge(top_diff, 1)
            activation(rt[:, :, 4, 0], rt[:, :, 3, 0], ACT.Exp).then_inc(top_exp, 1)

            def gathered(n):
                for k in range(2):
                    act_e.wait_ge(gather_ps, 2 * n + (k - 1))
                    activation(xeT_hi[:, 4 * k:4 * k + 4, :], bank(6 + k).rearrange("p (dc s) -> p dc s", dc=4),
                               ACT.Copy).then_inc(xeT_hi_ready, 1)

            def expert(it):
                at = Pass(it)

                def finish():
                    act_e.wait_ge(pgT_ps, it + 1)
                    activation(pick_gateT[:, :, :].rearrange("p c t -> p (c t)"), bank(3)[:, 0:TC * P],
                               ACT.Copy).then_inc(pgT_sb, 1)
                    gathered(it + 2)

                mixer_pass(at, finish)
                act_e.wait_ge(part_used, at.parts(MIX_PARTS))
                for k in range(2):
                    activation(ye[:, k * HALF:(k + 1) * HALF], bank(4 + k), ACT.Copy).then_inc(ye_sb, 1)
                gates_of(Pass(it + 1), 0)
                turned(Pass(it + 1), 0)

            gathered(1)
            gates_of(Pass(0), 0)
            turned(Pass(0), 0)
            with act_e.Fori(0, E) as it:
                expert(it)
            act_e.wait_ge(routed, 1)
            n_pass = act_e.value_load(passes_i[0:1, 0:1], min_val=1, max_val=2)
            with act_e.If(n_pass > 1):
                with act_e.Fori(E, 2 * E) as it:
                    expert(it)
            for c in range(TC):
                square(c, scat_add, n_pass * (4 * E))

        @block.vector
        def _(dve):
            n_step = [0]

            def step(ins):
                n_step[0] += 1
                ins.then_inc(dve_step, 1)
                dve.wait_ge(dve_step, n_step[0])

            tt, ts, stt = dve.tensor_tensor, dve.tensor_scalar, dve.scalar_tensor_tensor
            mul, add, sub = ALU.mult, ALU.add, ALU.subtract
            n_rms = [0]

            def invert(rms):
                n_rms[0] += 1
                dve.wait_ge(rms_ready, n_rms[0])
                dve.reciprocal(rms, rms).then_inc(rms_inv, 1)
                dve.wait_ge(rms_inv, n_rms[0])

            dve.wait_ge(prep_in, 48)
            dve.wait_ge(act_prep, 1)
            ar = a_raw[:, 0, :, :]
            ai = a_raw[:, 1, :, :]
            arf, aif = (z.rearrange("p h s -> p (h s)") for z in (ar, ai))
            dtb = dt_[:, :].unsqueeze(2).to_broadcast([PAIRS, 2, ST])
            w = lambda k: prep[:, k, :]
            w3 = lambda k: prep[:, k, :].rearrange("p (h s) -> p h s", h=2)
            step(tt(w3(0), ar, dtb, mul))
            step(tt(w3(2), ai, dtb, mul))
            step(ts(w(5), w(2), 1.0 / (2.0 * math.pi), 12582912.0, mul, add))
            step(ts(w(5), w(5), -12582912.0, None, add))
            c1, c2 = 6.28125, 0.0019340515136718750
            c3 = 2.0 * math.pi - c1 - c2
            for part in (c1, c2, c3):
                step(stt(w(2), w(5), -part, w(2), mul, add))
            step(ts(w(2), w(2), 3.1415925, -3.1415925, ALU.min, ALU.max))
            step(tt(w(6), arf, arf, mul))
            step(tt(w(7), aif, aif, mul))
            tt(w(6), w(6), w(7), add).then_inc(dve_prep, 1)
            dve.wait_ge(dve_prep, 1)
            step(dve.reciprocal(w(6), w(6)))
            dve.wait_ge(act_prep, 4)
            step(tt(w(3), w(3), w(3), mul))
            step(ts(w(3), w(3), -2.0, 1.0, mul, add))
            step(tt(w(8), w(1), w(3), mul))
            step(tt(w(9), w(1), w(4), mul))
            step(ts(w(7), w(8), -1.0, None, add))
            step(tt(w(10), w(7), arf, mul))
            step(tt(w(12), w(9), aif, mul))
            step(tt(w(10), w(10), w(12), add))
            step(tt(w(10), w(10), w(6), mul))
            step(tt(w(11), w(9), arf, mul))
            step(tt(w(12), w(7), aif, mul))
            step(tt(w(11), w(11), w(12), sub))
            tt(w(11), w(11), w(6), mul).then_inc(coef_ready, 1)
            dve.wait_ge(pe_prep, 2)
            step(dve.tensor_copy(coef4[:, :, :].rearrange("p k i -> p (k i)"), bank(6)[:, 0:4 * PAIRS]))
            dve.tensor_copy(gain_u[:, :], bank(6)[:, P:P + G])
            dve.wait_ge(pool_const, CONSTS)
            step(tt(eye2[:, :], ident[0:2 * C, 0:C], ident[0:2 * C, C:2 * C], add))
            tt(skip[:, :, :], eye2[:, :].unsqueeze(1).to_broadcast([2 * C, PAIRS, C]),
               bank(6)[0:2 * C, P + G:P + G + PAIRS].unsqueeze(2).to_broadcast([2 * C, PAIRS, C]),
               mul).then_inc(coef_sb, 1)
            dve.memset(pw[:, 0, 0, :], 1.0)
            dve.memset(pw[:, 1, 0, :], 0.0)
            step(dve.tensor_copy(pw[:, :, 1, :], coef4[:, 0:2, :]))
            for n in (1, 2, 4):
                lo, hi = slice(1, n + 1), slice(n + 1, 2 * n + 1)
                t = tmp_v[:, 0:n * PAIRS].rearrange("p (k i) -> p k i", k=n)
                by = lambda r: pw[:, r, n:n + 1, :].to_broadcast([P, n, PAIRS])
                step(tt(pw[:, 0, hi, :], pw[:, 0, lo, :], by(0), mul))
                step(tt(t, pw[:, 1, lo, :], by(1), mul))
                step(tt(pw[:, 0, hi, :], pw[:, 0, hi, :], t, sub))
                step(tt(pw[:, 1, hi, :], pw[:, 0, lo, :], by(1), mul))
                step(tt(t, pw[:, 1, lo, :], by(0), mul))
                step(tt(pw[:, 1, hi, :], pw[:, 1, hi, :], t, add))
            invert(small[0:NCH, 0:CH])
            for s in range(CH):
                dve.tensor_copy(pr[:, :, s, :], pw[:, :, CH - 1 - s, :])
            for o in range(2):
                dve.tensor_copy(carry[:, o, o, :], pw[:, 0, CH, :])
            dve.tensor_copy(carry[:, 1, 0, :], pw[:, 1, CH, :])
            step(ts(carry[:, 0, 1, :], pw[:, 1, CH, :], -1.0, None, mul))
            dve.wait_ge(b_in, 64)
            cf = lambda r: coef4[:, 2 + r, :].unsqueeze(2).to_broadcast([P, PAIRS, C])
            t = tmp_v[:, 0:PAIRS * C].rearrange("p (i c) -> p i c", i=PAIRS)
            step(tt(bb[:, 0, :, :], b_raw[:, 0, :, :], cf(0), mul))
            step(tt(t, b_raw[:, 1, :, :], cf(1), mul))
            step(tt(bb[:, 0, :, :], bb[:, 0, :, :], t, sub))
            step(tt(bb[:, 1, :, :], b_raw[:, 1, :, :], cf(0), mul))
            step(tt(t, b_raw[:, 0, :, :], cf(1), mul))
            tt(bb[:, 1, :, :], bb[:, 1, :, :], t, add).then_inc(dve_prep, 1)
            dve.wait_ge(dve_prep, 2)

            def in_powers(q):
                if q >= 2:
                    dve.wait_ge(bt_ps, 4 * (q - 1))
                for r, first, op in ((1, POOL_PAIRS, add), (0, 0, sub)):
                    n = QP - first
                    t = tmp_v[:, 0:n * CH * C].rearrange("p (i s c) -> p i s c", i=n, s=CH)
                    i = slice(q * QP + first, (q + 1) * QP)
                    b_of = lambda z: bb[:, z, i, :].unsqueeze(2).to_broadcast([P, n, CH, C])
                    p_of = lambda z: pr[:, z, :, i].rearrange("p s i -> p i s").unsqueeze(3).to_broadcast([P, n, CH, C])
                    o = bp[:, q % 2, r, first:QP, :, :]
                    step(tt(o, b_of(0), p_of(r), mul))
                    step(tt(t, b_of(1), p_of(1 - r), mul))
                    ins = tt(o, o, t, op)
                    if r == 1:
                        step(ins)
                ins.then_inc(bp_re, 1)
                dve.wait_ge(bp_re, q + 1)

            in_powers(0)
            in_powers(1)
            for b in range(4):
                dve.wait_ge(u_ps, b + 1)
                tt(uT[:, b * C:(b + 1) * C, :], bank(4 + b).rearrange("p (g n) -> p g n", g=C),
                   gain_u[:, b * C:(b + 1) * C].unsqueeze(2).to_broadcast([P, C, NCH]), mul).then_inc(u_sb, 1)
            for q in range(2, ROUNDS):
                in_powers(q)

            dve.wait_ge(act_prep, 6)

            def out_powers(q):
                t9 = tmp_v[:, :].rearrange("p (i k c) -> p i k c", i=QP, k=KP)
                i = slice(q * QP, (q + 1) * QP)
                c_of = lambda r: c_q[:, r, i, :].unsqueeze(2).to_broadcast([P, QP, KP, C])
                p_of = lambda r: pw[:, r, :, i].rearrange("p k i -> p i k").unsqueeze(3).to_broadcast([P, QP, KP, C])
                g = gk[:, q, 0, :, :, :]
                step(tt(g, c_of(0), p_of(0), mul))
                step(tt(t9, c_of(1), p_of(1), mul))
                tt(g, g, t9, sub).then_inc(gk_re, 1)
                dve.wait_ge(gk_re, q + 1)

            for q in range(ROUNDS - 1):
                out_powers(q)
            dve.memset(state[:, :, :, 0], 0.0)
            dve.wait_ge(xin_sb, 4 * ROUNDS)
            step(dve.tensor_copy(state[:, :, :, 1], xin[:, :, :, 0]))
            prod = tmp_v[:, 0:4 * PAIRS].rearrange("p (o r i) -> p o r i", o=2, r=2)
            for n in range(1, NCH - 1):
                s_n = state[:, :, :, n].unsqueeze(1).to_broadcast([P, 2, 2, PAIRS])
                step(tt(prod, carry[:, :, :, :], s_n, mul))
                step(tt(prod[:, :, 0, :], prod[:, :, 0, :], prod[:, :, 1, :], add))
                ins = tt(state[:, :, :, n + 1], prod[:, :, 0, :], xin[:, :, :, n], add)
                if n < NCH - 2:
                    step(ins)
            ins.then_inc(state_ready, 1)
            dve.wait_ge(state_ready, 1)
            dve.wait_ge(zeroed, 1)
            def lo_of_output(q):
                dve.wait_ge(hi_sides, 2 * (q + 1))
                if q == 0:
                    dve.wait_ge(toep_in, 2 * 16 * 2 * CH)
                for k in range(2):
                    o = lambda z: z[:, q + 4 * k, :].rearrange("p (n t) -> p t n", t=CH)
                    tt(o(hT_lo), bank(6 + q % 2).rearrange("p (t h n) -> p h t n", t=CH, h=2)[:, k],
                       o(hT_hi).bitcast(F32), sub).then_inc(lo_sides, 1)

            for q in range(ROUNDS):
                dve.tensor_copy(state_diag[ST:P, :, q * QP:(q + 1) * QP, 1, :],
                                state[ST:P, :, q * QP:(q + 1) * QP, :]).then_inc(state_bottom, 1)
            for q in range(ROUNDS):
                if q >= 2:
                    dve.wait_ge(yT_ps, q - 1)
                for b in range(2):
                    dve.wait_ge(y_ps, 2 * q + b + 1)
                    dve.tensor_copy(y64[:, q % 2, :, 4 * b * C:4 * (b + 1) * C].rearrange("n t (i c) -> n i t c", i=4),
                                    bank(2 * (q % 2) + b)[0:2 * NCH, :].rearrange("n (i t c) -> n i t c", i=4, t=CH)
                                    ).then_inc(y_sb, 1)
                if q >= 1:
                    lo_of_output(q - 1)
            for p in range(2):
                split_lo(dve, Before, p)
            lo_of_output(ROUNDS - 1)
            for p in range(2, PART_SLOTS):
                split_lo(dve, Before, p)
            dve.wait_ge(xres_in, 16)
            n_norm = [0]

            def normalise(c):
                dve.wait_ge(gain_in, 16 * (n_norm[0] // TC + 1))
                n_norm[0] += 1
                invert(small[:, 8 + c:9 + c])
                stt(xn[:, c, :], x_res[:, c, :], small[:, 8 + c:9 + c], gain[:, :], mul, mul).then_inc(xn_ready, 1)

            for n in range(GLU_BLOCKS):
                last = n == GLU_BLOCKS - 1

                def gated(c):
                    dve.wait_ge(glu_sig, TC * n + c + 1)
                    step(tt(gate[:, c, :], gate[:, c, :], bank(2 * (n % 2) + c)[:, 0:FH], mul))
                    tt(x_res[:, c, n * FH:(n + 1) * FH], x_res[:, c, n * FH:(n + 1) * FH], gate[:, c, :],
                       add).then_inc(glu_add, 1)

                if last:
                    gated(0)
                for p in range(2 if last else 4):
                    if p == 3:
                        for c in range(TC):
                            gated(c)
                    split_lo(dve, Before, 4 * n + p + PART_SLOTS)
            gated(1)
            for c in range(TC):
                normalise(c)

            def split_block_end(first_part):
                for p in (2, 3):
                    split_lo(dve, Before, first_part - 4 + p + PART_SLOTS)

            n_side = [2 * ROUNDS]

            def lo_of_side(o, full, rounded):
                n_side[0] += 1
                dve.wait_ge(hi_sides, n_side[0])
                tt(o, full, rounded.bitcast(F32), sub).then_inc(lo_sides, 1)

            def hidden(at, j):
                for p in range(w_part(j), w_part(j) + 4):
                    if p == w_part(j) + 3:
                        for c in range(at.nb):
                            dve.wait_ge(silu_done, at.items(at.nb * j + c + 1))
                            tt(act[:, c, :], gate[:, c, :], bank(c)[:, FH:2 * FH], mul).then_inc(act_ready, 1)
                    if not at.is_down(p + PART_SLOTS):
                        split_lo(dve, at, p + PART_SLOTS)

            def turned(at, j):
                for c in range(at.nb):
                    dve.wait_ge(actT_hi_ready, at.items(at.nb * j + c + 1))
                    tt(actT_lo[:, c, :], bank(2 + c)[:, 0:2 * P], actT_hi[:, c, :].bitcast(F32),
                       sub).then_inc(actT_lo_ready, 1)

            def mixer_pass(at, between, finish):
                for j in range(1, J + 1):
                    if j < J:
                        hidden(at, j)
                    else:
                        finish()
                    for p in range(d_part(j - 1), d_part(j - 1) + 2):
                        if not at.is_down(p + PART_SLOTS) and (j < J or not at.dense):
                            split_lo(dve, at, p + PART_SLOTS)
                    if j < J:
                        turned(at, j)
                        between(j)

            def lo_hT():
                for c in range(TC):
                    for half in range(2):
                        lo_of_side(hT_lo[:, 4 * half:4 * half + 4, c * P:(c + 1) * P],
                                   bank(4 * c + half).rearrange("p (dc t) -> p dc t", dc=4),
                                   hT_hi[:, 4 * half:4 * half + 4, c * P:(c + 1) * P])

            lo_hT()
            split_block_end(2 * FIRST_FFN)
            def lambda_products(j):
                if j == 4:
                    dve.wait_ge(table_in, 96)
                    for k in range(2):
                        step(tt(sqscr[:, k, 0:HD], lam_in[:, 2 * k, :], lam_in[:, 2 * k + 1, :], mul))
                    dve.tensor_reduce(lam[:, 0:2], sqscr[:, :, 0:HD], AX.X, add).then_inc(lam_ready, 1)

            hidden(Pass(), 0)
            turned(Pass(), 0)
            def add_ffn(c):
                for k in range(2):
                    o = x_res[:, c, k * HALF:(k + 1) * HALF]
                    tt(o, o, bank(4 + 2 * c + k), add).then_inc(ffn_add, 1)
                normalise(c)

            def first_tokens():
                dve.wait_ge(block_done, 2)
                add_ffn(0)

            mixer_pass(Pass(), lambda_products, first_tokens)
            dve.wait_ge(part_used, 2 * FIRST_QKV)
            add_ffn(1)
            lo_hT()
            split_block_end(2 * FIRST_QKV)
            dve.wait_ge(lam_ready, 2)
            step(tt(lam[:, 4:5], lam[:, 3:4], lam[:, 2:3], sub))
            step(ts(lam[:, 4:5], lam[:, 4:5], -LAMBDA_INIT, None, add))
            ts(sub_gain[:, :], sub_gain[:, :], 1.0 - LAMBDA_INIT, None, mul).then_inc(lam_ready, 1)
            for n in range(4 * QKV_BLOCKS):
                split_lo(dve, Before, 2 * FIRST_QKV + PART_SLOTS + n)
            dve.wait_ge(bias_in, 16)

            def scores(h):
                if h >= 2:
                    dve.wait_ge(probs_ready, h - 1)
                dve.wait_ge(sc_ps, h + 1)
                s = sc[:, h % 2, :, :]
                scores_ps = bank(2 * (h % 2), 2).rearrange("p (m k) -> p m k", m=2)[:, :, 0:3 * P]
                tt(s[:, :, 0:P], scores_ps[:, :, 0:P], bias[:, h, P:2 * P].unsqueeze(1).to_broadcast([P, 2, P]), add)
                tt(s[:, :, P:3 * P], scores_ps[:, :, P:3 * P], bias[:, h, :].unsqueeze(1).to_broadcast([P, 2, 2 * P]),
                   add).then_inc(sc_sb, 1)
                dve.wait_ge(sc_sb, h + 1)
                if h >= 2:
                    dve.wait_ge(exp_done, 4 * (h - 1))
                st = asm[:, h % 2, :]
                dve.tensor_reduce(st[:, 0:2], s[:, :, 0:P], AX.X, ALU.max)
                step(dve.tensor_reduce(st[:, 2:4], s[:, :, P:3 * P], AX.X, ALU.max))
                ts(st[:, 0:4], st[:, 0:4], -1.0, None, mul).then_inc(max_done, 1)

            def combine(h):
                st = asm[:, h % 2, :]
                dve.wait_ge(exp_done, 4 * (h + 1))
                step(dve.reciprocal(st[:, 8:12], st[:, 4:8]))
                step(ts(st[:, 9:12:2], st[:, 9:12:2], lam[:, 4:5], None, mul))
                if h >= 2:
                    dve.wait_ge(pT_ps, h - 1)
                for qb in range(2):
                    cols = slice(0, P) if qb == 0 else slice(P, 3 * P)
                    step(ts(probs[:, h % 2, cols], sc[:, h % 2, 0, cols], st[:, 8 + 2 * qb:9 + 2 * qb], None, mul))
                    ins = stt(probs[:, h % 2, cols], sc[:, h % 2, 1, cols], st[:, 9 + 2 * qb:10 + 2 * qb],
                              probs[:, h % 2, cols], mul, add)
                ins.then_inc(probs_ready, 1)

            def head_out(h):
                dve.wait_ge(osq_done, 2 * (h + 1))
                dve.tensor_copy(qT[:, h, :], bank(6 + h % 2)[:, 0:2 * P]).then_inc(o_sb, 1)

            scores(0)
            for h in range(H):
                if h + 1 < H:
                    scores(h + 1)
                if h >= 2:
                    head_out(h - 2)
                combine(h)
            head_out(H - 2)
            head_out(H - 1)
            invert(osq[:, :, :].rearrange("p c h -> p (c h)"))
            dve.wait_ge(o_sb, H)
            for c in range(TC):
                o = qT[:, :, c * P:(c + 1) * P]
                tt(o, o, osq[:, c, :].unsqueeze(2).to_broadcast([P, H, P]), mul).then_inc(o_scaled, 1)
            for u in range(4):
                c, k = divmod(u, 2)
                n_side[0] += 1
                dve.wait_ge(hi_sides, n_side[0])
                stt(hT_lo[:, 4 * k:4 * k + 4, c * P:(c + 1) * P], bank(u).rearrange("p (dc t) -> p dc t", dc=4),
                    sub_gain[:, :], hT_hi[:, 4 * k:4 * k + 4, c * P:(c + 1) * P].bitcast(F32),
                    mul, sub).then_inc(lo_sides, 1)
            for n in range(WO_BLOCKS):
                last = n == WO_BLOCKS - 1

                def add_wo(c):
                    o = x_res[:, c, n * BANK:(n + 1) * BANK]
                    tt(o, o, bank(4 + n * TC + c), add).then_inc(wo_add, 1)

                if last:
                    dve.wait_ge(router_hi_ready, 1)
                    tt(router_lo[:, :, :], router[:, :, :], router_hi[:, :, :].bitcast(F32), sub).then_inc(router_split, 1)
                    dve.wait_ge(block_done, 3)
                    add_wo(0)
                    normalise(0)
                for p in range(2 if last else 4):
                    split_lo(dve, Before, 2 * FIRST_WO + 4 * n + p + PART_SLOTS)
                if not last:
                    for c in range(TC):
                        add_wo(c)
            dve.wait_ge(part_used, 2 * FIRST_MOE)
            add_wo(1)
            normalise(1)
            lo_hT()
            split_block_end(2 * FIRST_MOE)

            dve.wait_ge(logitsT_ps, 1)
            dve.tensor_copy(logitsT[:, :], bank(7)[0:E, 0:SEQ]).then_inc(logitsT_sb, 1)
            dve.wait_ge(logit_ps, 1)
            logit, top, first, second, sel, comb = (rt[:, :, k, :] for k in (0, 1, 5, 6, 7, 8))
            step(dve.tensor_copy(logit, bank(6)[:, 0:TC * E].rearrange("p (c e) -> p c e", c=TC)))
            for c in range(TC):
                step(dve.max(rt[:, c, 1, :], rt[:, c, 0, :]))
                step(dve.max_index(top_i[:, c, :], rt[:, c, 1, :], rt[:, c, 0, :]))
                step(dve.tensor_copy(rt[:, c, 2, :], top_i[:, c, :]))
                for k, o in enumerate((5, 6)):
                    step(ts(rt[:, c, o, :], slot_no[:, 0:E], rt[:, c, 2, k:k + 1], None, ALU.is_equal))
            tt(rt[:, :, 3, 0], rt[:, :, 1, 1], rt[:, :, 1, 0], sub).then_inc(top_diff, 1)
            tt(sel, first, second, add).then_inc(sel_ready, 1)
            dve.wait_ge(top_exp, 1)
            step(ts(rt[:, :, 4, 1], rt[:, :, 4, 0], 1.0, None, add))
            step(dve.reciprocal(rt[:, :, 4, 2], rt[:, :, 4, 1]))
            step(tt(rt[:, :, 4, 3], rt[:, :, 4, 0], rt[:, :, 4, 2], mul))
            step(tt(comb, first, rt[:, :, 4, 2:3].to_broadcast([P, TC, E]), mul))
            step(tt(second, second, rt[:, :, 4, 3:4].to_broadcast([P, TC, E]), mul))
            step(tt(comb, comb, second, add))
            dve.memset(gates[:, :, 2 * E:2 * E + 1], 0.0)
            dve.tensor_copy(gates[:, :, 0:E], comb)
            dve.tensor_copy(gates[:, :, E:2 * E], comb)
            dve.wait_ge(cnt_ps, 1)
            dve.memset(key[:, :, 2 * E:2 * E + 1], -1.0)
            step(tt(key[:, :, 0:E], bank(7)[:, 0:TC * E].rearrange("p (c e) -> p c e", c=TC), sel, mul))
            step(ts(key[:, :, 0:E], key[:, :, 0:E], -1.0, None, add))
            dve.tensor_scalar(key[:, :, E:2 * E], key[:, :, 0:E], -float(P), None, add)
            step(dve.tensor_reduce(passes[:, 0:1], bank(7)[:, TC * E:(TC + 1) * E], AX.X, ALU.max))
            step(ts(passes[:, 1:2], passes[:, 0:1], float(P), 1.0, ALU.is_gt, add))
            dve.tensor_copy(passes_i[:, :], passes[:, 1:2]).then_inc(routed, 1)

            def pick_tokens(it):
                for c in range(TC):
                    ts(pick[:, c, :], slot_no[:, :], key[:, c, bass.ds(it, 1)], None, ALU.is_equal).then_inc(pick_ready, 1)

            def gathered(n):
                for k in range(2):
                    dve.wait_ge(xeT_hi_ready, 2 * n + (k - 1))
                    tt(xeT_lo[:, 4 * k:4 * k + 4, :], bank(6 + k).rearrange("p (dc s) -> p dc s", dc=4),
                       xeT_hi[:, 4 * k:4 * k + 4, :].bitcast(F32), sub).then_inc(xeT_lo_ready, 1)

            def expert(it):
                def picks(j):
                    if j == 4:
                        for c in range(TC):
                            ts(pick_gate[:, c, :], slot_no[:, :], key[:, c, bass.ds(it, 1)],
                               gates[:, c, bass.ds(it, 1)], ALU.is_equal, mul).then_inc(gate_pick_ready, 1)
                        pick_tokens(it + 1)

                mixer_pass(Pass(it), picks, lambda: gathered(it + 2))
                hidden(Pass(it + 1), 0)
                for u, b in enumerate(SCATTER_BANKS):
                    c, k = divmod(u, 2)
                    o = x_res[:, c, k * HALF:(k + 1) * HALF]
                    dve.wait_ge(scat_ps, it * 4 + (u + 1))
                    tt(o, o, bank(b), add).then_inc(scat_add, 1)
                turned(Pass(it + 1), 0)
                dve.wait_ge(scat_add, it * 4 + 4)

            pick_tokens(0)
            gathered(1)
            hidden(Pass(0), 0)
            turned(Pass(0), 0)
            with dve.Fori(0, E) as it:
                expert(it)
            n_pass = dve.value_load(passes_i[0:1, 0:1], min_val=1, max_val=2)
            with dve.If(n_pass > 1):
                with dve.Fori(E, 2 * E) as it:
                    expert(it)
            dve.wait_ge(const_in, 16)
            for c in range(TC):
                invert(small[:, 8 + c:9 + c])
                stt(xn[:, c, :], x_res[:, c, :], small[:, 8 + c:9 + c], final_gain[:, :], mul, mul).then_inc(final_ready, 1)

        @block.tensor
        def _(pe):
            mm = pe.matmul

            def transpose(o, i, n=P):
                return pe.transpose(o, i, ident[0:n, 0:n])

            pe.wait_ge(pool_const, CONSTS)
            pe.wait_ge(c_in, 64)
            for r in range(2):
                for k in range(4):
                    ins = transpose(bank(4 + r)[:, k * P:(k + 1) * P], c_raw[:, r, k, :, :].rearrange("p h s -> p (h s)"))
            ins.then_inc(pe_prep, 1)
            pe.wait_ge(coef_ready, 1)
            for k in range(4):
                transpose(bank(6)[:, k * PAIRS:(k + 1) * PAIRS], prep[:, 8 + k, :], PAIRS)
            pe.wait_ge(bc_in, 32)
            transpose(bank(6)[:, P:P + G], gain_raw[:, :, :].rearrange("g s c -> g (s c)"), G)
            transpose(bank(6)[0:2 * C, P + G:P + G + PAIRS], skip_raw[:, :, :].rearrange("i h c -> i (h c)"),
                      PAIRS).then_inc(pe_prep, 1)
            pe.wait_ge(h_ready, 1)
            pe.wait_ge(h_pool, 1)
            pe.wait_ge(act_prep, 6)
            pe.wait_ge(coef_sb, 1)
            for g in range(G):
                b, k = divmod(g, C)
                ins = transpose(bank(4 + b)[:, k * NCH:(k + 1) * NCH], h32[:, g, :, :].rearrange("n s c -> n (s c)"), NCH)
                if k == C - 1:
                    ins.then_inc(u_ps, 1)
            def in_powers_T(q):
                pe.wait_ge(bp_re, q + 1)
                pe.wait_ge(bp_im, q + 1)
                for b in range(4):
                    if q >= 1:
                        pe.wait_ge(bt_sb, 4 * (q - 1) + b + 1)
                    for k in range(4):
                        r, i = divmod(4 * b + k, QP)
                        ins = transpose(bank(b)[:, k * P:(k + 1) * P], bp[:, q % 2, r, i, :, :].rearrange("p s c -> p (s c)"))
                    ins.then_inc(bt_ps, 1)

            def chunk_inputs(q):
                pe.wait_ge(bt_sb, 4 * (q + 1))
                if q == 0:
                    pe.wait_ge(u_sb, 4)
                if q >= 2:
                    pe.wait_ge(xin_sb, 4 * (q - 1))
                for r in range(2):
                    for i in range(QP):
                        at = (r * QP + i) * 2 * NCH
                        ins = mm(bank(4 + 2 * (q % 2), 2)[:, at:at + 2 * NCH], bt[q % 2][:, r, i, :],
                                 uT[:, q * QP + i::PAIRS, :], start=True, stop=True)
                ins.then_inc(xin_ps, 1)

            for q in range(ROUNDS):
                in_powers_T(q)
                if q >= 1:
                    chunk_inputs(q - 1)
            chunk_inputs(ROUNDS - 1)

            def impulse(q):
                pe.wait_ge(gk_re, min(q + 1, ROUNDS - 1))
                pe.wait_ge(gk_im, q + 1)
                if q == 0:
                    pe.wait_ge(bb_diag_ready, 2)
                    pe.wait_ge(xin_sb, 4 * ROUNDS)
                for b in range(2):
                    if q >= 1:
                        pe.wait_ge(kern_sb, 2 * (q - 1) + b + 1)
                    o = bank(4 + b)[0:2 * C, :]
                    for n in range(4):
                        i = 4 * b + n
                        for r in range(2):
                            mm(o[:, n * P:(n + 1) * P], bb_diag[:, r, q * QP + i, :, :].rearrange("p h c -> p (h c)"),
                               gk[:, q, r, i, 0:CH, :], start=(n == 0 and r == 0), stop=False)
                    at = q * QP + 4 * b
                    mm(o.rearrange("m (n k) -> m n k", n=4)[:, :, 0:C], ident[0:2 * C, 0:2 * C],
                       skip[:, at:at + 4, :], start=False, stop=True).then_inc(kern_ps, 1)

            def inside(q):
                pe.wait_ge(toep_in, 16 * 2 * CH * (q // 2 + 1))
                if q >= 2:
                    pe.wait_ge(y_sb, 2 * (q - 1))
                for b in range(2):
                    mm(bank(2 * (q % 2) + b)[0:2 * NCH, :], zero[:, 0:2 * NCH], zero[:, :], start=True, stop=False)
                    for n in range(4):
                        for h in range(2):
                            i = 4 * b + n
                            ins = mm(bank(2 * (q % 2) + b)[h * NCH:(h + 1) * NCH, n * P:(n + 1) * P],
                                     uT[:, h * PAIRS + q * QP + i, :], toep[:, h, q % 2 * QP + i, :],
                                     start=False, stop=False)
                ins.then_inc(inside_done, 1)

            def carried(q):
                pe.wait_ge(state_top, q + 1)
                pe.wait_ge(state_bottom, q + 1)
                for b in range(2):
                    for n in range(4):
                        i = 4 * b + n
                        for r in range(2):
                            ins = mm(bank(2 * (q % 2) + b)[0:2 * NCH, n * P:(n + 1) * P],
                                     state_diag[:, r, q * QP + i, :, :].rearrange("p h n -> p (h n)"),
                                     gk[:, q, r, i, 1:KP, :], start=False, stop=(n == 3 and r == 1))
                    ins.then_inc(y_ps, 1)

            def mixer_out_T(q):
                pe.wait_ge(y_sb, 2 * (q + 1))
                if q >= 2:
                    pe.wait_ge(lo_sides, 2 * (q - 1))
                for s in range(CH):
                    ins = transpose(bank(6 + q % 2)[:, s * 2 * NCH:(s + 1) * 2 * NCH], y64[:, q % 2, s, :], 2 * NCH)
                ins.then_inc(yT_ps, 1)

            impulse(0)
            impulse(1)
            impulse(2)
            impulse(3)
            inside(0)
            inside(1)
            carried(0)
            carried(1)
            mixer_out_T(0)
            mixer_out_T(1)
            inside(2)
            carried(2)
            inside(3)
            mixer_out_T(2)
            carried(3)
            mixer_out_T(3)

            def part_ready(at, p):
                if at.is_down(p):
                    pe.wait_ge(lo_down, at.down(p + 1))
                else:
                    pe.wait_ge(lo_wide, at.wide(p + 1))
                return hi[at.slot(p)], lo[at.slot(p)]

            def split_mm(o, left, right, first, last):
                mm(o, left[0], right[0], start=first, stop=False)
                mm(o, left[0], right[1], start=False, stop=False)
                return mm(o, left[1], right[0], start=False, stop=last)

            def both(z, *index):
                return tuple(k[index] for k in z)

            hT = (hT_hi, hT_lo)
            every = slice(None)

            def token_blocks(at, p0, outs, side):
                for p in range(4):
                    w = part_ready(at, p0 + p)
                    for d in range(2):
                        dc = 2 * p + d
                        for c, o in enumerate(outs):
                            ins = split_mm(o, side(dc, c), both(w, every, slice(d * BANK, (d + 1) * BANK)),
                                           dc == 0, dc == DC - 1)
                    ins.then_inc(part_used, 1)

            def by_tokens(at, p0, outs, side, sides=None, early=False):
                parts = [None] * 4
                for c, o in enumerate(outs):
                    if sides is not None:
                        pe.wait_ge(lo_sides, sides + 2 * (c + 1))
                    for p in range(4):
                        if c == 0:
                            parts[p] = part_ready(at, p0 + p)
                        for d in range(2):
                            dc = 2 * p + d
                            ins = split_mm(o, side(dc, c), both(parts[p], every, slice(d * BANK, (d + 1) * BANK)),
                                           dc == 0, dc == DC - 1)
                        if c == len(outs) - 1:
                            ins.then_inc(part_used, 1)
                        elif early and p == 3:
                            ins.then_inc(block_done, 1)

            def hT_block(dc, c):
                return both(hT, every, dc, slice(c * P, (c + 1) * P))

            pe.wait_ge(lo_sides, 2 * ROUNDS)
            for n in range(GLU_BLOCKS):
                if n >= 2:
                    pe.wait_ge(glu_add, TC * (n - 1))
                outs = [bank(2 * (n % 2) + c) for c in range(TC)]
                if n < GLU_BLOCKS - 1:
                    token_blocks(Before, 4 * n, outs, hT_block)
                else:
                    by_tokens(Before, 4 * n, outs, hT_block, early=True)

            n_norm = [0]

            def norm_transposes():
                k = n_norm[0]
                for c in range(TC):
                    pe.wait_ge(xn_ready, TC * k + c + 1)
                    for dc in range(DC):
                        ins = transpose(bank(4 * c, 2)[:, dc * P:(dc + 1) * P], xn[:, c, dc * P:(dc + 1) * P])
                        if dc % 4 == 3:
                            ins.then_inc(hT_ps, 1)
                n_norm[0] += 1

            def gate_up(at, j, side):
                token_blocks(at, w_part(j), [bank(c) for c in range(at.nb)], side)

            def turn(at, j):
                for c in range(at.nb):
                    pe.wait_ge(act_ready, at.items(at.nb * j + c + 1))
                    for f in range(2):
                        ins = transpose(bank(2 + c)[:, f * P:(f + 1) * P], act[:, c, f * P:(f + 1) * P])
                    ins.then_inc(actT_ps, 1)

            def mixer_pass(at, side, finish):
                for j in range(1, J + 1):
                    if j < J:
                        gate_up(at, j, side)
                    else:
                        finish()
                    pe.wait_ge(actT_hi_ready, at.items(at.nb * j))
                    pe.wait_ge(actT_lo_ready, at.items(at.nb * j))
                    if j == J and at.dense:
                        parts = [part_ready(at, d_part(j - 1) + f) for f in range(2)]
                        for c in range(at.nb):
                            for f in range(2):
                                a = both((actT_hi, actT_lo), every, c, slice(f * P, (f + 1) * P))
                                for k in range(2):
                                    ins = split_mm(bank(4 + 2 * c + k), a,
                                                   both(parts[f], every, slice(k * HALF, (k + 1) * HALF)),
                                                   False, f == 1)
                                if c == at.nb - 1:
                                    ins.then_inc(part_used, 1)
                                elif f == 1:
                                    ins.then_inc(block_done, 1)
                        continue
                    for f in range(2):
                        w = part_ready(at, d_part(j - 1) + f)
                        for c in range(at.nb):
                            a = both((actT_hi, actT_lo), every, c, slice(f * P, (f + 1) * P))
                            for k in range(2):
                                ins = split_mm(bank(4 + 2 * c + k), a,
                                               both(w, every, slice(k * HALF, (k + 1) * HALF)),
                                               j == 1 and f == 0, j == J and f == 1)
                        ins.then_inc(part_used, 1)
                    if j < J:
                        turn(at, j)

            norm_transposes()
            by_tokens(Pass(), w_part(0), [bank(c) for c in range(TC)], hT_block, sides=2 * ROUNDS)
            turn(Pass(), 0)
            mixer_pass(Pass(), hT_block, lambda: None)
            norm_transposes()
            for n in range(QKV_BLOCKS):
                if n >= 2:
                    pe.wait_ge(qkv_sb, TC * min(n - 1, 2) + 4 * max(n - 3, 0))
                p0 = 2 * FIRST_QKV + 4 * n
                b0 = 4 * (n % 2)
                if n < 2:
                    outs = [bank(b0 + c) for c in range(TC)]
                    if n == 0:
                        by_tokens(Before, p0, outs, hT_block, sides=2 * ROUNDS + 4)
                    else:
                        token_blocks(Before, p0, outs, hT_block)
                    continue
                for p in range(4):
                    w = part_ready(Before, p0 + p)
                    for d in range(2):
                        dc = 2 * p + d
                        for m in range(4):
                            at_m = d * BANK + m * P
                            ins = split_mm(bank(b0 + m)[:, 0:SEQ], both(w, every, slice(at_m, at_m + P)),
                                           both(hT, every, dc), dc == 0, dc == DC - 1)
                    ins.then_inc(part_used, 1)

            def score_products(h):
                if h == 0:
                    pe.wait_ge(qkv_sb, 4 * 4 + 2 * TC)
                if h >= 2:
                    pe.wait_ge(sc_sb, h - 1)
                for m in range(2):
                    part = slice(m * HD, (m + 1) * HD)
                    o = bank(2 * (h % 2) + m)
                    mm(o[:, 0:P], qT[part, h, 0:P], kT[part, h, 0:P], start=True, stop=True)
                    ins = mm(o[:, P:3 * P], qT[part, h, P:2 * P], kT[part, h, :], start=True, stop=True)
                ins.then_inc(sc_ps, 1)

            score_products(0)
            score_products(1)
            for h in range(H):
                if h + 2 < H:
                    score_products(h + 2)
                pe.wait_ge(probs_ready, h + 1)
                if h >= 2:
                    pe.wait_ge(pT_sb, h - 1)
                for k in range(3):
                    ins = transpose(bank(4 + h % 2)[:, k * P:(k + 1) * P], probs[:, h % 2, k * P:(k + 1) * P])
                ins.then_inc(pT_ps, 1)
                pe.wait_ge(pT_sb, h + 1)
                if h >= 2:
                    pe.wait_ge(o_sb, h - 1)
                o = bank(6 + h % 2)
                head = slice(h * P, (h + 1) * P)
                mm(o[:, 0:P], pT[:, h % 2, 0:P], v[:, 0, head], start=True, stop=True)
                mm(o[:, P:2 * P], pT[:, h % 2, P:2 * P], v[:, 0, head], start=True, stop=False)
                mm(o[:, P:2 * P], pT[:, h % 2, 2 * P:3 * P], v[:, 1, head], start=False, stop=True).then_inc(o_ps, 1)
            pe.wait_ge(o_scaled, TC)
            for u in range(4):
                c, k = divmod(u, 2)
                for n in range(4):
                    ins = transpose(bank(u)[:, n * P:(n + 1) * P], qT[:, 4 * k + n, c * P:(c + 1) * P])
                ins.then_inc(oT_ps, 1)
            pe.wait_ge(lo_sides, 2 * ROUNDS + 12)
            for n in range(WO_BLOCKS):
                outs = [bank(4 + n * TC + c) for c in range(TC)]
                if n < WO_BLOCKS - 1:
                    token_blocks(Before, 2 * FIRST_WO + 4 * n, outs, hT_block)
                else:
                    by_tokens(Before, 2 * FIRST_WO + 4 * n, outs, hT_block, early=True)
            norm_transposes()
            pe.wait_ge(lo_sides, 2 * ROUNDS + 16)
            pe.wait_ge(router_split, 1)
            for dc in range(DC):
                ins = split_mm(bank(7)[0:E, 0:SEQ], both((router_hi, router_lo), every, dc), both(hT, every, dc),
                               dc == 0, dc == DC - 1)
            ins.then_inc(logitsT_ps, 1)
            pe.wait_ge(logitsT_sb, 1)
            for c in range(TC):
                ins = transpose(bank(6)[:, c * E:(c + 1) * E], logitsT[:, c * P:(c + 1) * P], E)
            ins.then_inc(logit_ps, 1)
            pe.wait_ge(sel_ready, 1)
            counts = bank(7)
            mm(counts[:, 0:E], upto[:, :], rt[:, 0, 7, :], start=True, stop=True)
            mm(counts[:, E:2 * E], ones[:, :], rt[:, 0, 7, :], start=True, stop=False)
            mm(counts[:, E:2 * E], upto[:, :], rt[:, 1, 7, :], start=False, stop=True)
            mm(counts[:, 2 * E:3 * E], ones[:, :], rt[:, 0, 7, :], start=True, stop=False)
            mm(counts[:, 2 * E:3 * E], ones[:, :], rt[:, 1, 7, :], start=False, stop=True).then_inc(cnt_ps, 1)

            def gather(n_pick):
                pe.wait_ge(pick_ready, n_pick)
                for dc in range(DC):
                    for c in range(TC):
                        ins = mm(bank(6, 2)[:, dc * P:(dc + 1) * P], xn[:, c, dc * P:(dc + 1) * P], pick[:, c, :],
                                 start=(c == 0), stop=(c == TC - 1))
                    if dc % 4 == 3:
                        ins.then_inc(gather_ps, 1)

            def xeT_block(dc, c):
                return both((xeT_hi, xeT_lo), every, dc)

            def expert(it):
                def finish():
                    pe.wait_ge(gate_pick_ready, it * TC + TC)
                    for c in range(TC):
                        ins = transpose(bank(3)[:, c * P:(c + 1) * P], pick_gate[:, c, :])
                    ins.then_inc(pgT_ps, 1)
                    gather(it * TC + 2 * TC)

                mixer_pass(Pass(it), xeT_block, finish)
                pe.wait_ge(xeT_hi_ready, it * 2 + 4)
                pe.wait_ge(xeT_lo_ready, it * 2 + 4)
                gate_up(Pass(it + 1), 0, xeT_block)
                pe.wait_ge(pgT_sb, it + 1)
                pe.wait_ge(ye_sb, it * 2 + 2)
                for u, b in enumerate(SCATTER_BANKS):
                    c, k = divmod(u, 2)
                    mm(bank(b), pick_gateT[:, c, :], ye[:, k * HALF:(k + 1) * HALF],
                       start=True, stop=True).then_inc(scat_ps, 1)
                turn(Pass(it + 1), 0)
                pe.wait_ge(scat_add, it * 4 + 4)

            gather(TC)
            pe.wait_ge(xeT_hi_ready, 2)
            pe.wait_ge(xeT_lo_ready, 2)
            gate_up(Pass(0), 0, xeT_block)
            turn(Pass(0), 0)
            with pe.Fori(0, E) as it:
                expert(it)
            pe.wait_ge(routed, 1)
            n_pass = pe.value_load(passes_i[0:1, 0:1], min_val=1, max_val=2)
            with pe.If(n_pass > 1):
                with pe.Fori(E, 2 * E) as it:
                    expert(it)


_INS = ["x", "norm_mix_g", "norm_ffn_g", "final_norm_g", "ssm_a_re", "ssm_a_im", "ssm_log_dt", "ssm_b_re",
        "ssm_b_im", "ssm_c_re", "ssm_c_im", "ssm_d", "ssm_w_glu", "attn_w_qkv", "attn_lambda_q1",
        "attn_lambda_k1", "attn_lambda_q2", "attn_lambda_k2", "attn_subln_g", "attn_w_o", "rel_bias",
        "ffn_w_gate_up", "ffn_w_down", "moe_router", "moe_w_gate_up", "moe_w_down"]


def kernel(**inputs):
    import numpy as _np
    import concourse.bacc as _bacc
    from concourse import mybir as _mybir
    from concourse.bass_utils import run_bass_kernel_spmd as _run

    nc = _bacc.Bacc("TRN2", target_bir_lowering=False, num_devices=1)
    arrays, args = {}, []
    for name in _INS:
        a = _np.ascontiguousarray(inputs[name])
        arrays[f"in_{name}_dram"] = a
        args.append(nc.dram_tensor(f"in_{name}_dram", a.shape, _mybir.dt.from_np(a.dtype), kind="ExternalInput").ap())
    args.append(nc.dram_tensor("out_0_dram", (1, SEQ, D), F32, kind="ExternalOutput").ap())
    trunk(nc, *args)
    r = _run(nc, [arrays], core_ids=[0])
    return r.results[0]["out_0_dram"]
```
